# Optimizing a Trainium2 kernel written in Bass

```python
import math
import jax, jax.numpy as jnp
from jax import lax
import numpy as np

D_MODEL = 1024
BATCH = 1
SEQ = 256
DEPTH = 1

HEAD_DIM = 64
BLOCK_Q = 128
RMS_EPS = 1e-6
NEG_INF = -1e30
TINY = 1e-30

FOX_HEADS = 4
FORGET_BIAS_INIT = 3.0
DIL_WINDOWS = (128, 512, 2048)
DIL_RATES = (1, 4, 16)
DIL_HEADS_PER_GROUP = 2
DIL_HEADS = DIL_HEADS_PER_GROUP * len(DIL_WINDOWS)
NSA_HEADS = 6
NSA_KV_GROUPS = 2
NSA_CMP_BLOCK = 32
NSA_CMP_STRIDE = 16
NSA_CMP_HIDDEN = 256
NSA_SEL_BLOCK = 64
NSA_SEL_TOPK = 8
NSA_WINDOW = 512
FORCE_SCORE = 1e6
ALIBI_HEADS = DIL_HEADS + NSA_HEADS
D_FF = 2816
CONV_WIDTH = 3

FOX_W = FOX_HEADS * HEAD_DIM
DIL_W = DIL_HEADS * HEAD_DIM
NSA_W = NSA_HEADS * HEAD_DIM
NSA_KV_W = NSA_KV_GROUPS * HEAD_DIM
IN_SPLITS = (FOX_W, FOX_W, FOX_W, FOX_HEADS,
             DIL_W, DIL_W, DIL_W,
             NSA_W, NSA_KV_W, NSA_KV_W, NSA_KV_W, NSA_KV_W, NSA_KV_W, NSA_KV_W, NSA_HEADS * 3,
             3 * D_MODEL)
D_IN = sum(IN_SPLITS)


def rms_norm(x, g):
    xf = x.astype(jnp.float32)
    y = xf * lax.rsqrt(jnp.mean(xf * xf, axis=-1, keepdims=True) + RMS_EPS)
    return (y * g.astype(jnp.float32)).astype(x.dtype)

def alibi_slopes(n):
    return jnp.exp2(-8.0 * jnp.arange(1, n + 1, dtype=jnp.float32) / n)

def masked_softmax(s, mask):
    s = jnp.where(mask, s, NEG_INF)
    m = jnp.max(s, axis=-1, keepdims=True)
    e = jnp.where(mask, jnp.exp(s - m), 0.0)
    l = jnp.maximum(jnp.sum(e, axis=-1, keepdims=True), TINY)
    return e / l, (m + jnp.log(l))[..., 0]

def fox_attention(q, k, v, f_logit):
    B_, S, H, dh = q.shape
    nb = S // BLOCK_Q
    scale = dh ** -0.5
    c = jnp.cumsum(jax.nn.log_sigmoid(f_logit.astype(jnp.float32)), axis=1)
    c = jnp.transpose(c, (0, 2, 1))
    q_blocks = q.reshape(B_, nb, BLOCK_Q, H, dh).transpose(1, 0, 2, 3, 4)
    c_blocks = c.reshape(B_, H, nb, BLOCK_Q).transpose(2, 0, 1, 3)
    kpos = jnp.arange(S)

    def body(args):
        qb, cb, i = args
        qpos = i * BLOCK_Q + jnp.arange(BLOCK_Q)
        s = jnp.einsum('bqhd,bkhd->bhqk', qb, k).astype(jnp.float32) * scale
        s = s + cb[..., :, None] - c[:, :, None, :]
        p, _ = masked_softmax(s, kpos[None, :] <= qpos[:, None])
        return jnp.einsum('bhqk,bkhd->bqhd', p.astype(v.dtype), v)

    out = lax.map(body, (q_blocks, c_blocks, jnp.arange(nb)))
    return out.transpose(1, 0, 2, 3, 4).reshape(B_, S, H * dh)

def dilated_attention(q, k, v, slopes):
    B_, S, H, dh = q.shape
    P = DIL_HEADS_PER_GROUP
    nb = S // BLOCK_Q
    scale = dh ** -0.5
    q_blocks = q.reshape(B_, nb, BLOCK_Q, H, dh).transpose(1, 0, 2, 3, 4)

    def body(args):
        qb, i = args
        qpos = i * BLOCK_Q + jnp.arange(BLOCK_Q)
        outs, lses = [], []
        for g, (w, r) in enumerate(zip(DIL_WINDOWS, DIL_RATES)):
            hs = slice(g * P, (g + 1) * P)
            offs = r * jnp.arange(w // r + 1)
            kidx = qpos[:, None] - offs[None, :]
            valid = kidx >= 0
            kidx = jnp.maximum(kidx, 0)
            kg = k[:, :, hs][:, kidx]
            vg = v[:, :, hs][:, kidx]
            s = jnp.einsum('bqhd,bqkhd->bhqk', qb[:, :, hs], kg).astype(jnp.float32) * scale
            s = s - slopes[hs][None, :, None, None] * offs.astype(jnp.float32)[None, None, None, :]
            p, lse = masked_softmax(s, valid[None, None])
            outs.append(jnp.einsum('bhqk,bqkhd->bqhd', p.astype(vg.dtype), vg))
            lses.append(lse)
        alpha = jax.nn.softmax(jnp.stack(lses, 0), axis=0)
        o = jnp.stack(outs, 0) * alpha.transpose(0, 1, 3, 2)[..., None].astype(qb.dtype)
        return o.transpose(1, 2, 0, 3, 4).reshape(B_, BLOCK_Q, H * dh)

    out = lax.map(body, (q_blocks, jnp.arange(nb)))
    return out.transpose(1, 0, 2, 3).reshape(B_, S, H * dh)

def compress_blocks(kv, pe, w1, w2):
    B_, S, G, dh = kv.shape
    n_cmp = (S - NSA_CMP_BLOCK) // NSA_CMP_STRIDE + 1
    idx = jnp.arange(n_cmp)[:, None] * NSA_CMP_STRIDE + jnp.arange(NSA_CMP_BLOCK)[None, :]
    blocks = kv[:, idx] + pe[None, None, :, None, :]
    flat = blocks.transpose(0, 1, 3, 2, 4).reshape(B_, n_cmp, G, NSA_CMP_BLOCK * dh)
    return jax.nn.gelu(flat @ w1) @ w2

def nsa_attention(q, k_cmp, v_cmp, k_sel, v_sel, k_win, v_win, gate_logits, slopes,
                  cmp_pe, k_w1, k_w2, v_w1, v_w2):
    B_, S, H, dh = q.shape
    G = NSA_KV_GROUPS
    R = H // G
    nb = S // BLOCK_Q
    scale = dh ** -0.5
    kc = compress_blocks(k_cmp, cmp_pe, k_w1, k_w2)
    vc = compress_blocks(v_cmp, cmp_pe, v_w1, v_w2)
    n_cmp = kc.shape[1]
    cmp_end = jnp.arange(n_cmp) * NSA_CMP_STRIDE + NSA_CMP_BLOCK - 1
    cmp_start = cmp_end - (NSA_CMP_BLOCK - 1)
    n_sel = S // NSA_SEL_BLOCK
    sel_idx = jnp.arange(n_sel)
    sel_start = sel_idx * NSA_SEL_BLOCK
    overlap = ((cmp_start[:, None] < sel_start[None, :] + NSA_SEL_BLOCK)
               & (cmp_end[:, None] >= sel_start[None, :])).astype(jnp.float32)
    top_k = min(NSA_SEL_TOPK, n_sel)
    n_tok = top_k * NSA_SEL_BLOCK
    slope = slopes.reshape(G, R)[None, :, :, None, None]
    ks_t = k_sel.transpose(0, 2, 1, 3)
    vs_t = v_sel.transpose(0, 2, 1, 3)
    pad = ((0, 0), (NSA_WINDOW, 0), (0, 0), (0, 0))
    kw_pad = jnp.pad(k_win, pad)
    vw_pad = jnp.pad(v_win, pad)
    gather = jax.vmap(jax.vmap(lambda t, ii: t[ii]))
    q_blocks = q.reshape(B_, nb, BLOCK_Q, G, R, dh).transpose(1, 0, 2, 3, 4, 5)
    g_blocks = jax.nn.sigmoid(gate_logits).reshape(B_, nb, BLOCK_Q, G, R, 3).transpose(1, 0, 2, 3, 4, 5)

    def body(args):
        qb, gb, i = args
        q0 = i * BLOCK_Q
        qpos = q0 + jnp.arange(BLOCK_Q)
        s = jnp.einsum('bqgrd,bcgd->bgrqc', qb, kc).astype(jnp.float32) * scale
        s = s - slope * (qpos[:, None] - cmp_end[None, :]).astype(jnp.float32)
        p_c, _ = masked_softmax(s, cmp_end[None, :] <= qpos[:, None])
        o_c = jnp.einsum('bgrqc,bcgd->bqgrd', p_c.astype(vc.dtype), vc)
        imp = jnp.einsum('bgrqc,cj->bgqj', p_c, overlap)
        qblk = qpos // NSA_SEL_BLOCK
        causal = sel_start[None, :] <= qpos[:, None]
        forced = ((sel_idx[None, :] == 0) | (sel_idx[None, :] == qblk[:, None])
                  | (sel_idx[None, :] == qblk[:, None] - 1))
        score = jnp.where(causal & forced, FORCE_SCORE, jnp.where(causal, imp, -1.0))
        _, blk = lax.top_k(score, top_k)
        blk_ok = blk * NSA_SEL_BLOCK <= qpos[None, None, :, None]
        tok = (blk[..., None] * NSA_SEL_BLOCK + jnp.arange(NSA_SEL_BLOCK)).reshape(B_, G, BLOCK_Q, n_tok)
        tok_ok = jnp.repeat(blk_ok, NSA_SEL_BLOCK, axis=-1) & (tok <= qpos[None, None, :, None])
        kg = gather(ks_t, tok)
        vg = gather(vs_t, tok)
        s = jnp.einsum('bqgrd,bgqtd->bgrqt', qb, kg).astype(jnp.float32) * scale
        s = s - slope * (qpos[None, None, :, None] - tok)[:, :, None].astype(jnp.float32)
        p_s, _ = masked_softmax(s, tok_ok[:, :, None])
        o_s = jnp.einsum('bgrqt,bgqtd->bqgrd', p_s.astype(vg.dtype), vg)
        kw = lax.dynamic_slice_in_dim(kw_pad, q0, NSA_WINDOW + BLOCK_Q, axis=1)
        vw = lax.dynamic_slice_in_dim(vw_pad, q0, NSA_WINDOW + BLOCK_Q, axis=1)
        kpos = q0 - NSA_WINDOW + jnp.arange(NSA_WINDOW + BLOCK_Q)
        diff = qpos[:, None] - kpos[None, :]
        mask_w = (kpos[None, :] >= 0) & (diff >= 0) & (diff < NSA_WINDOW)
        s = jnp.einsum('bqgrd,bkgd->bgrqk', qb, kw).astype(jnp.float32) * scale
        s = s - slope * diff.astype(jnp.float32)
        p_w, _ = masked_softmax(s, mask_w)
        o_w = jnp.einsum('bgrqk,bkgd->bqgrd', p_w.astype(vw.dtype), vw)
        gb = gb.astype(qb.dtype)
        o = gb[..., 0:1] * o_c + gb[..., 1:2] * o_s + gb[..., 2:3] * o_w
        return o.reshape(B_, BLOCK_Q, H * dh)

    out = lax.map(body, (q_blocks, g_blocks, jnp.arange(nb)))
    return out.transpose(1, 0, 2, 3).reshape(B_, S, H * dh)

def conv_ffn(h, w_up, conv_w, conv_b, w_down):
    a, b = jnp.split(h @ w_up, 2, axis=-1)
    a = lax.conv_general_dilated(a, conv_w.reshape(CONV_WIDTH, 1, D_FF), window_strides=(1,),
                                 padding=[(CONV_WIDTH - 1, 0)],
                                 dimension_numbers=('NWC', 'WIO', 'NWC'),
                                 feature_group_count=D_FF) + conv_b
    return (jax.nn.gelu(a) * b) @ w_down

def first_inputs(seed: int = 0) -> dict:
    key = jax.random.key(seed)
    ks = jax.random.split(key, 20)
    f32 = jnp.float32

    def nrm(k, shape, scale):
        return jax.random.normal(k, shape, f32) * scale

    L = DEPTH
    fo = 3 * FOX_W
    b_in = nrm(ks[3], (L, D_IN), 0.02).at[:, fo:fo + FOX_HEADS].add(FORGET_BIAS_INIT)
    return {
        "x": nrm(ks[0], (BATCH, SEQ, D_MODEL), 1.0),
        "norm1_g": 1.0 + nrm(ks[1], (L, D_MODEL), 0.02),
        "w_in": nrm(ks[2], (L, D_MODEL, D_IN), D_MODEL ** -0.5),
        "b_in": b_in,
        "cmp_pe": nrm(ks[4], (L, NSA_CMP_BLOCK, HEAD_DIM), 0.02),
        "cmp_k_w1": nrm(ks[5], (L, NSA_CMP_BLOCK * HEAD_DIM, NSA_CMP_HIDDEN), (NSA_CMP_BLOCK * HEAD_DIM) ** -0.5),
        "cmp_k_w2": nrm(ks[6], (L, NSA_CMP_HIDDEN, HEAD_DIM), NSA_CMP_HIDDEN ** -0.5),
        "cmp_v_w1": nrm(ks[7], (L, NSA_CMP_BLOCK * HEAD_DIM, NSA_CMP_HIDDEN), (NSA_CMP_BLOCK * HEAD_DIM) ** -0.5),
        "cmp_v_w2": nrm(ks[8], (L, NSA_CMP_HIDDEN, HEAD_DIM), NSA_CMP_HIDDEN ** -0.5),
        "w_pa": nrm(ks[9], (L, FOX_W, D_MODEL), FOX_W ** -0.5),
        "w_pb": nrm(ks[10], (L, DIL_W, D_MODEL), DIL_W ** -0.5),
        "w_pc": nrm(ks[11], (L, NSA_W, D_MODEL), NSA_W ** -0.5),
        "w_o": nrm(ks[12], (L, D_MODEL, D_MODEL), D_MODEL ** -0.5),
        "norm2_g": 1.0 + nrm(ks[13], (L, D_MODEL), 0.02),
        "w_up": nrm(ks[14], (L, D_MODEL, 2 * D_FF), D_MODEL ** -0.5),
        "conv_w": nrm(ks[15], (L, CONV_WIDTH, D_FF), CONV_WIDTH ** -0.5),
        "conv_b": nrm(ks[16], (L, D_FF), 0.02),
        "w_down": nrm(ks[17], (L, D_FF, D_MODEL), D_FF ** -0.5),
        "final_g": 1.0 + nrm(ks[18], (D_MODEL,), 0.02),
    }

def first_block(x, norm1_g, w_in, b_in, cmp_pe, cmp_k_w1, cmp_k_w2, cmp_v_w1, cmp_v_w2,
              w_pa, w_pb, w_pc, w_o, norm2_g, w_up, conv_w, conv_b, w_down, final_g):
    B_, S, D = x.shape
    dh = HEAD_DIM
    G = NSA_KV_GROUPS
    slopes = alibi_slopes(ALIBI_HEADS)
    dil_slopes = slopes[0::2]
    nsa_slopes = slopes[1::2]
    split_at = np.cumsum(IN_SPLITS)[:-1].tolist()
    for l in range(DEPTH):
        h = rms_norm(x, norm1_g[l])
        proj = h @ w_in[l] + b_in[l]
        (qa, ka, va, fa, qb, kb, vb, qc, kc_, vc_, ksl, vsl, kwn, vwn, gc, gates) = jnp.split(proj, split_at, axis=-1)
        y_a = fox_attention(qa.reshape(B_, S, FOX_HEADS, dh), ka.reshape(B_, S, FOX_HEADS, dh),
                            va.reshape(B_, S, FOX_HEADS, dh), fa)
        y_b = dilated_attention(qb.reshape(B_, S, DIL_HEADS, dh), kb.reshape(B_, S, DIL_HEADS, dh),
                                vb.reshape(B_, S, DIL_HEADS, dh), dil_slopes)
        y_c = nsa_attention(qc.reshape(B_, S, NSA_HEADS, dh),
                            kc_.reshape(B_, S, G, dh), vc_.reshape(B_, S, G, dh),
                            ksl.reshape(B_, S, G, dh), vsl.reshape(B_, S, G, dh),
                            kwn.reshape(B_, S, G, dh), vwn.reshape(B_, S, G, dh),
                            gc.reshape(B_, S, NSA_HEADS, 3), nsa_slopes,
                            cmp_pe[l], cmp_k_w1[l], cmp_k_w2[l], cmp_v_w1[l], cmp_v_w2[l])
        g = jax.nn.sigmoid(gates).reshape(B_, S, 3, D)
        merged = (g[:, :, 0] * (y_a @ w_pa[l]) + g[:, :, 1] * (y_b @ w_pb[l])
                  + g[:, :, 2] * (y_c @ w_pc[l]))
        x = x + merged @ w_o[l]
        x = x + conv_ffn(rms_norm(x, norm2_g[l]), w_up[l], conv_w[l], conv_b[l], w_down[l])
    return rms_norm(x, final_g)


DEPTH_2 = 2

N_EVEN = (DEPTH_2 + 1) // 2
N_ODD = DEPTH_2 // 2
LN_EPS = 1e-5

W_A = D_MODEL
CONV_K = 31
A_GROUPS = 8
H_B = 4
DQK_B = D_MODEL // (2 * H_B)
DV_B = D_MODEL // H_B
W_B = H_B * DV_B
CHUNK = 64
H_C = 8
QK_NOPE = 128
QK_ROPE = 64
V_HEAD = 128
Q_LORA = 3 * D_MODEL // 8
KV_LORA = D_MODEL // 4
W_C = H_C * V_HEAD
Q_BLOCK = 128
ROPE_THETA = 10000.0
D_GROUPS = 4
D_GROUP_CH = D_MODEL // 8
W_D = D_GROUPS * D_GROUP_CH

EVEN_SIZES = (W_A, W_A, W_A, H_B * DQK_B, H_B * DQK_B, W_B, W_B, W_B, 4 * H_B)
ODD_SIZES = (Q_LORA, KV_LORA, QK_ROPE, W_D, W_C, W_D)
P_EVEN = sum(EVEN_SIZES)
P_ODD = sum(ODD_SIZES)


def split_cols(p, sizes):
    idx = [int(i) for i in np.cumsum(sizes)[:-1]]
    return jnp.split(p, idx, axis=-1)

def rms_norm_2(x, g):
    xf = x.astype(jnp.float32)
    y = xf * lax.rsqrt(jnp.mean(xf * xf, axis=-1, keepdims=True) + RMS_EPS)
    return (y * g.astype(jnp.float32)).astype(x.dtype)

def group_layer_norm(x, g, b, groups):
    B, S, C = x.shape
    xf = x.astype(jnp.float32).reshape(B, S, groups, C // groups)
    mu = jnp.mean(xf, axis=-1, keepdims=True)
    xc = xf - mu
    var = jnp.mean(xc * xc, axis=-1, keepdims=True)
    y = (xc * lax.rsqrt(var + LN_EPS)).reshape(B, S, C)
    return (y * g.astype(jnp.float32) + b.astype(jnp.float32)).astype(x.dtype)

def depthwise_conv_centred(x, w, b):
    K = w.shape[0]
    y = lax.conv_general_dilated(
        x, w[:, None, :].astype(x.dtype), window_strides=(1,),
        padding=[(K // 2, K // 2)], dimension_numbers=("NWC", "WIO", "NWC"),
        feature_group_count=x.shape[-1])
    return y + b.astype(x.dtype)

def rope_tables(positions):
    inv = ROPE_THETA ** (-jnp.arange(0, QK_ROPE, 2, dtype=jnp.float32) / QK_ROPE)
    ang = positions.astype(jnp.float32)[..., None] * inv
    return jnp.cos(ang), jnp.sin(ang)

def apply_rope(x, cos, sin):
    half = x.shape[-1] // 2
    xf = x.astype(jnp.float32)
    x1, x2 = xf[..., :half], xf[..., half:]
    return jnp.concatenate([x1 * cos - x2 * sin, x1 * sin + x2 * cos], axis=-1).astype(x.dtype)

def mlstm_chunkwise(q, k, v, i_pre, f_pre):
    B, H, S, dk = q.shape
    dv = v.shape[-1]
    nc = S // CHUNK
    f32 = jnp.float32

    def chunks(a):
        return jnp.moveaxis(a.reshape(B, H, nc, CHUNK, *a.shape[3:]), 2, 0)

    qc = chunks(q.astype(f32))
    kc = chunks(k.astype(f32) * (dk ** -0.5))
    vc = chunks(v.astype(f32))
    ic = chunks(i_pre.astype(f32))
    bc = jnp.cumsum(chunks(jax.nn.log_sigmoid(f_pre.astype(f32))), axis=-1)
    tril = jnp.tril(jnp.ones((CHUNK, CHUNK), dtype=bool))

    def step(carry, inp):
        C, n, m = carry
        qb, kb, vb, ib, bb = inp
        D = jnp.where(tril, bb[..., :, None] - bb[..., None, :] + ib[..., None, :], -jnp.inf)
        a = bb + m[..., None]
        m_t = jnp.maximum(a, jnp.max(D, axis=-1))
        Dw = jnp.exp(D - m_t[..., None])
        aw = jnp.exp(a - m_t)
        s = jnp.einsum('bhtd,bhsd->bhts', qb, kb) * Dw
        num = jnp.einsum('bhts,bhsv->bhtv', s, vb) + aw[..., None] * jnp.einsum('bhtd,bhdv->bhtv', qb, C)
        den = jnp.sum(s, axis=-1) + aw * jnp.einsum('bhtd,bhd->bht', qb, n)
        h = num / jnp.maximum(jnp.abs(den), jnp.exp(-m_t))[..., None]
        bL = bb[..., -1]
        g = bL[..., None] - bb + ib
        m_new = jnp.maximum(bL + m, jnp.max(g, axis=-1))
        wk = jnp.exp(g - m_new[..., None])
        decay = jnp.exp(bL + m - m_new)
        C_new = decay[..., None, None] * C + jnp.einsum('bhs,bhsd,bhsv->bhdv', wk, kb, vb)
        n_new = decay[..., None] * n + jnp.einsum('bhs,bhsd->bhd', wk, kb)
        return (C_new, n_new, m_new), h

    init = (jnp.zeros((B, H, dk, dv), f32), jnp.zeros((B, H, dk), f32), jnp.zeros((B, H), f32))
    _, hs = lax.scan(step, init, (qc, kc, vc, ic, bc))
    return jnp.moveaxis(hs, 0, 2).reshape(B, H, S, dv)

def even_layer(x, g_pre, g_post, w_in, b_gate, conv_w, conv_b, gn_g, gn_b, hn_g, w_out):
    B, S, _ = x.shape
    h = rms_norm_2(x, g_pre)
    p = h @ w_in
    a_val, a_gate, z_a, q, k, v, o, z_b, gates = split_cols(p, EVEN_SIZES)
    u = a_val * jax.nn.sigmoid(a_gate)
    u = depthwise_conv_centred(u, conv_w, conv_b)
    u = jax.nn.silu(group_layer_norm(u, gn_g, gn_b, A_GROUPS))
    y_a = u * jax.nn.silu(z_a)
    to_heads = lambda t, d: t.reshape(B, S, H_B, d).transpose(0, 2, 1, 3)
    qh, kh, vh = to_heads(q, DQK_B), to_heads(k, DQK_B), to_heads(v, DV_B)
    gt = (gates.astype(jnp.float32) + b_gate.astype(jnp.float32)).reshape(B, S, 4, H_B).transpose(2, 0, 3, 1)
    i_f, f_f, i_b, f_b = gt[0], gt[1], gt[2], gt[3]
    h_fwd = mlstm_chunkwise(qh, kh, vh, i_f, f_f)
    fl = lambda t: jnp.flip(t, axis=2)
    h_bwd = fl(mlstm_chunkwise(fl(qh), fl(kh), fl(vh), fl(i_b), fl(f_b)))
    hm = (h_fwd + h_bwd).transpose(0, 2, 1, 3)
    hm = rms_norm_2(hm, hn_g.reshape(H_B, DV_B)).astype(x.dtype)
    hm = jax.nn.sigmoid(o.reshape(B, S, H_B, DV_B)) * hm
    y_b = hm.reshape(B, S, W_B) * jax.nn.silu(z_b)
    y = jnp.concatenate([y_a, y_b], axis=-1) @ w_out
    return x + rms_norm_2(y, g_post)

def odd_layer(x, cos, sin, g_pre, g_post, w_in, g_q, w_uq, g_kv, w_ukv, w_fd, w_out):
    B, S, _ = x.shape
    h = rms_norm_2(x, g_pre)
    p = h @ w_in
    c_q, c_kv, k_r, f_in, z_c, z_d = split_cols(p, ODD_SIZES)
    qh = (rms_norm_2(c_q, g_q) @ w_uq).reshape(B, S, H_C, QK_NOPE + QK_ROPE)
    q_nope = qh[..., :QK_NOPE]
    q_rope = apply_rope(qh[..., QK_NOPE:], cos[:, :, None, :], sin[:, :, None, :])
    kv = (rms_norm_2(c_kv, g_kv) @ w_ukv).reshape(B, S, H_C, QK_NOPE + V_HEAD)
    k_nope, v = kv[..., :QK_NOPE], kv[..., QK_NOPE:]
    k_rope = apply_rope(k_r, cos, sin)
    scale = (QK_NOPE + QK_ROPE) ** -0.5
    nb = S // Q_BLOCK
    blk = lambda t: jnp.moveaxis(t.reshape(B, nb, Q_BLOCK, *t.shape[2:]), 1, 0)

    def attend(qs):
        qn, qr = qs
        s = jnp.einsum('bqhd,bkhd->bhqk', qn, k_nope) + jnp.einsum('bqhr,bkr->bhqk', qr, k_rope)
        pr = jax.nn.softmax(s.astype(jnp.float32) * scale, axis=-1).astype(v.dtype)
        return jnp.einsum('bhqk,bkhd->bqhd', pr, v)

    att = lax.map(attend, (blk(q_nope), blk(q_rope)))
    att = jnp.moveaxis(att, 0, 1).reshape(B, S, W_C)
    y_c = att * jax.nn.silu(z_c)
    fg = f_in.astype(jnp.float32).reshape(B, S, D_GROUPS, D_GROUP_CH)
    fr = jnp.real(jnp.fft.fft2(fg, axes=(1, 3), norm="ortho")).astype(x.dtype).reshape(B, S, W_D)
    y_d = (fr @ w_fd) * jax.nn.silu(z_d)
    y = jnp.concatenate([y_c, y_d], axis=-1) @ w_out
    return x + rms_norm_2(y, g_post)

def second_inputs(seed: int = 0) -> dict:
    key = jax.random.key(seed)
    ks = jax.random.split(key, 24)
    f32 = jnp.float32
    nrm = lambda k, shape, fan_in: jax.random.normal(k, shape, f32) * (fan_in ** -0.5)
    gain = lambda k, shape: 1.0 + 0.05 * jax.random.normal(k, shape, f32)
    small = lambda k, shape: 0.02 * jax.random.normal(k, shape, f32)
    x = jax.random.normal(ks[0], (BATCH, SEQ, D_MODEL), f32)
    positions = (jnp.arange(SEQ, dtype=jnp.int32)[None, :]
                 + jax.random.randint(ks[1], (BATCH, 1), 0, 1024, dtype=jnp.int32))
    fbias = jnp.linspace(3.0, 6.0, H_B, dtype=f32)
    gate_base = jnp.concatenate([jnp.zeros((H_B,), f32), fbias, jnp.zeros((H_B,), f32), fbias])
    even_b_gate = gate_base[None, :] + 0.1 * jax.random.normal(ks[2], (N_EVEN, 4 * H_B), f32)
    return {
        "x": x,
        "positions": positions,
        "even_g_pre": gain(ks[3], (N_EVEN, D_MODEL)),
        "even_g_post": gain(ks[4], (N_EVEN, D_MODEL)),
        "even_w_in": nrm(ks[5], (N_EVEN, D_MODEL, P_EVEN), D_MODEL),
        "even_b_gate": even_b_gate,
        "even_conv_w": nrm(ks[6], (N_EVEN, CONV_K, W_A), CONV_K),
        "even_conv_b": small(ks[7], (N_EVEN, W_A)),
        "even_gn_g": gain(ks[8], (N_EVEN, W_A)),
        "even_gn_b": small(ks[9], (N_EVEN, W_A)),
        "even_hn_g": gain(ks[10], (N_EVEN, W_B)),
        "even_w_out": nrm(ks[11], (N_EVEN, W_A + W_B, D_MODEL), W_A + W_B),
        "odd_g_pre": gain(ks[12], (N_ODD, D_MODEL)),
        "odd_g_post": gain(ks[13], (N_ODD, D_MODEL)),
        "odd_w_in": nrm(ks[14], (N_ODD, D_MODEL, P_ODD), D_MODEL),
        "odd_g_q": gain(ks[15], (N_ODD, Q_LORA)),
        "odd_w_uq": nrm(ks[16], (N_ODD, Q_LORA, H_C * (QK_NOPE + QK_ROPE)), Q_LORA),
        "odd_g_kv": gain(ks[17], (N_ODD, KV_LORA)),
        "odd_w_ukv": nrm(ks[18], (N_ODD, KV_LORA, H_C * (QK_NOPE + V_HEAD)), KV_LORA),
        "odd_w_fd": nrm(ks[19], (N_ODD, W_D, W_D), W_D),
        "odd_w_out": nrm(ks[20], (N_ODD, W_C + W_D, D_MODEL), W_C + W_D),
    }

def second_block(x, positions, even_g_pre, even_g_post, even_w_in, even_b_gate, even_conv_w,
              even_conv_b, even_gn_g, even_gn_b, even_hn_g, even_w_out, odd_g_pre, odd_g_post,
              odd_w_in, odd_g_q, odd_w_uq, odd_g_kv, odd_w_ukv, odd_w_fd, odd_w_out):
    cos, sin = rope_tables(positions)
    h = x
    for layer in range(DEPTH_2):
        j = layer // 2
        if layer % 2 == 0:
            h = even_layer(h, even_g_pre[j], even_g_post[j], even_w_in[j], even_b_gate[j],
                           even_conv_w[j], even_conv_b[j], even_gn_g[j], even_gn_b[j],
                           even_hn_g[j], even_w_out[j])
        else:
            h = odd_layer(h, cos, sin, odd_g_pre[j], odd_g_post[j], odd_w_in[j], odd_g_q[j],
                          odd_w_uq[j], odd_g_kv[j], odd_w_ukv[j], odd_w_fd[j], odd_w_out[j])
    return h


def setup_inputs(seed=0):
    out = dict(first_inputs(seed))
    for name, value in second_inputs(seed + 1).items():
        if name != "x":
            out[name + "_2"] = value
    return out


def reference(
    x, norm1_g, w_in, b_in, cmp_pe, cmp_k_w1, cmp_k_w2, cmp_v_w1, cmp_v_w2, w_pa, w_pb, w_pc,
    w_o, norm2_g, w_up, conv_w, conv_b, w_down, final_g, positions_2, even_g_pre_2,
    even_g_post_2, even_w_in_2, even_b_gate_2, even_conv_w_2, even_conv_b_2, even_gn_g_2,
    even_gn_b_2, even_hn_g_2, even_w_out_2, odd_g_pre_2, odd_g_post_2, odd_w_in_2, odd_g_q_2,
    odd_w_uq_2, odd_g_kv_2, odd_w_ukv_2, odd_w_fd_2, odd_w_out_2,
):
    x = first_block(
        x, norm1_g, w_in, b_in, cmp_pe, cmp_k_w1, cmp_k_w2, cmp_v_w1, cmp_v_w2, w_pa, w_pb,
        w_pc, w_o, norm2_g, w_up, conv_w, conv_b, w_down, final_g,
    )
    return second_block(
        x, positions_2, even_g_pre_2, even_g_post_2, even_w_in_2, even_b_gate_2, even_conv_w_2,
        even_conv_b_2, even_gn_g_2, even_gn_b_2, even_hn_g_2, even_w_out_2, odd_g_pre_2,
        odd_g_post_2, odd_w_in_2, odd_g_q_2, odd_w_uq_2, odd_g_kv_2, odd_w_ukv_2, odd_w_fd_2,
        odd_w_out_2,
    )


_drawn_inputs = setup_inputs


def setup_inputs(seed=0):
    import zlib

    import numpy as np

    out = dict(_drawn_inputs(seed))
    spreads = {}
    factors = {'norm1_g': 2.741,
     'cmp_pe': 5.577,
     'even_gn_b_2': 4.118,
     'odd_g_q_2': 8.0,
     'odd_g_kv_2': 5.321}
    for name, (base, spread) in spreads.items():
        noise = np.random.default_rng([zlib.crc32(name.encode()), seed]).standard_normal(out[name].shape)
        drawn = base * np.exp(spread * noise) if base else spread * noise
        out[name] = __import__('jax').numpy.asarray(drawn.astype(out[name].dtype))
    for name, factor in factors.items():
        out[name] = (out[name] * factor).astype(out[name].dtype)
    return out
```

```python
from contextlib import ExitStack

import numpy as np

import concourse.bass as bass
from concourse import mybir

P = 128
S = 256
TT = S // P
D = 1024
KD = D // P
DFF = 2816
NF = DFF // P
DH = 64
EPS, LN_EPS = 1e-6, 1e-5
MASKED = -1e30
RING = 4
UNIT = 2048
MLA_SCALE = 192 ** -0.5
TURN = (6.28125, 0.0019350051879882812, 3.0199159795074593e-07)
MAGIC = 1.5 * 2.0 ** 23
PI_IN = 3.1415925
LSTM_COLS = ((0, P), (0, S), (0, S), (P, S))

F32 = mybir.dt.float32
I32 = mybir.dt.int32
ALU = mybir.AluOpType
ACT = mybir.ActivationFunctionType
AX = mybir.AxisListType

CONST = dict(ident=128, mean=3 * 128, neg_upper=2 * 256, neg_lower=2 * 256, causal=256, anti=256,
             dil_bias=6 * 256, nsa_bias=6 * 256, cmp_bias=12 * 32, cmp_mask=12 * 32, rows=4 * 128,
             inv_freq=1)
LATE = dict(dft_ch=256, dft_cos=2 * 256, dft_nsin=2 * 256, rope_swap=128)
VECS = dict(g1=8, b_feat=18, b_gates=24, pe=16, g2=8, conv_w=66, conv_b=22, g3=8, taps=8 * 31,
            tap_b=8, gn_g=8, gn_b=8, hn_g=8, g4=8, g_q=3, g_kv=2)
ROWS = dict(b_v=896, b_small=22, b_gate=16)


def offsets(table):
    at, out = 0, {}
    for name, n in table.items():
        out[name] = (at, n)
        at += n
    return out, at


C_AT, NC_ = offsets(CONST)
V_AT, NV_ = offsets(VECS)
R_AT, NR_ = offsets(ROWS)
L_AT, NL_ = offsets(LATE)
assert NL_ <= CONST["dil_bias"]
for _name, (_o, _n) in L_AT.items():
    C_AT[_name] = (C_AT["dil_bias"][0] + _o, _n)

STREAM = [("proj", 12), ("cmp", 4), ("gates", 12), ("w_p", 4), ("w_o", 4), ("up", 22), ("down", 11),
          ("conv_in", 8), ("qk", 4), ("v", 4), ("z_a", 4), ("o", 4), ("z_b", 4), ("even_out", 8),
          ("lora", 3), ("f_in", 2), ("w_uq", 3), ("w_uk", 1), ("w_uv", 1), ("z_c", 4), ("z_d", 2),
          ("w_fd", 1), ("odd_out", 6)]
FIRST, NU = {}, 0
for _name, _n in STREAM:
    FIRST[_name] = NU
    NU += _n
assert NU % RING == 0

JOBS = [("fox", h // 2, h % 2, 2 + h // 2, h * DH, h) for h in range(4)]
JOBS += [("dil", 4 + 2 * g, h, 5 + 2 * g, 256 + (2 * g + h) * DH, 2 * g + h)
         for h in range(2) for g in range(3)]
for _i in range(3):
    for _h in (_i, _i + 3):
        _g = _h // 3
        JOBS.append(("sel", 10 + _i, _g, 13, 640 + _g * DH, _h))
        JOBS.append(("win", 10 + _i, _g, 14, 768 + _g * DH, _h))
NJ = len(JOBS)
PT_LAG, PV_LAG = 4, 5
Y_TILE = [h // 2 if k == "fox" else 2 + h // 2 if k == "dil" else 5 + h % 3
          for k, _, _, _, _, h in JOBS]
Y_PLACE = {0: (0, 0, 0), 1: (0, 1, 0), 2: (1, 0, 0), 3: (1, 1, 0), 4: (0, 0, 1), 5: (1, 0, 2),
           6: (0, 0, 3), 7: (1, 0, 4)}
COPIES = [(0, (0, 1), 3), (1, (2, 3), 9), (0, (4,), 9), (1, (5,), 13), (0, (6,), 17), (1, (7,), 21)]
FAC = [j + 1 if j < 4 else 5 + (j - 4) // 3 if j < 10 else j - 3 for j in range(NJ)]

EVEN_STEPS = []
for _h in range(4):
    EVEN_STEPS += [("scores", _h)]
    if _h:
        EVEN_STEPS += [("pv", _h - 1), ("var", _h - 1)]
    EVEN_STEPS += [("gn", _h), ("z_b", _h), ("gn_var", _h), ("turn", _h)]
EVEN_STEPS += [("pv", 3), ("var", 3)]

UQ_DONE = {}
for _n in range(14):
    _u = FIRST["w_uq"] + (_n // 2 if _n < 6 else 3 + (_n - 6) // 4)
    _last = _n % 2 == 1 if _n < 6 else (_n - 6) % 4 == 3
    UQ_DONE[_n] = ("unit_used", _u + 1) if _last else \
        ("uq_part", 1 + sum(v[0] == "uq_part" for v in UQ_DONE.values()))


def program(nc, w, w_small, consts, late, vecs, rows, gains, x, positions, cmp_w2, out):
    ctx = ExitStack()
    with ctx:
        def sb(name, shape, dt=F32):
            return ctx.enter_context(nc.sbuf_tensor(name, shape, dt))

        sems = {}

        def sem(name):
            if name not in sems:
                sems[name] = ctx.enter_context(nc.semaphore(name.replace("[", "_").replace("]", "")))
            return sems[name]

        ring = sb("ring", [P, RING, UNIT])
        cn = sb("cn", [P, NC_])
        vc = sb("vc", [P, NV_])
        rw = sb("rw", [P, NR_])
        gB = sb("gB", [P, D])
        wsm = sb("wsm", [P, KD, 38])
        w2s = sb("w2s", [P, 2, 2, DH])
        xa = sb("xa", [P, TT, D])
        xb = sb("xb", [P, TT, D])
        xh = sb("xh", [P, TT, D])
        hT = sb("hT", [P, KD, S])
        BIG = sb("BIG", [P, 24, S])
        QK = sb("QK", [P, 16, S])
        V = sb("V", [P, TT, 1024])
        Y = sb("Y", [P, 16, S])
        PB = sb("PB", [P, 8, 384])
        SM = sb("SM", [P, 3, 512])
        PTS = sb("PTS", [P, 2, 512])
        T1 = sb("T1", [P, 2, 512])
        T2 = sb("T2", [P, 2, 512])
        UP = sb("UP", [P, 8, 286])
        stat = sb("stat", [P, 48])
        tiny = sb("tiny", [P, 640])
        eps_t = sb("eps_t", [P, 2])
        PS = ctx.enter_context(nc.psum_tensor("PS", [P, 8, 512], F32))

        def c(name, a=0, b=None):
            o, n = C_AT[name]
            return cn[:, o + a:o + (n if b is None else b)]

        def v(name, i=0, n=1):
            o, _ = V_AT[name]
            return vc[:, o + i:o + i + n]

        def r(name, a=0, b=None):
            o, n = R_AT[name]
            return rw[:, o + a:o + (n if b is None else b)]

        ident = c("ident")
        block = ctx.enter_context(nc.Block())
        G, SC, PT, AV, DEEP = (0, 1), (2, 3), (4, 5), (6, 7), 4

        ssq, rms = stat[:, 0:16], stat[:, 16:32]
        lsum, nmax, fac = tiny[:, 0:44], tiny[:, 44:88], tiny[:, 88:132]
        gnsa = tiny[:, 132:168]
        lfa = tiny[:, 168:192]
        small = tiny[:, 192:236].rearrange("p (t c) -> p t c", t=TT)
        gt2 = tiny[:, 236:268].rearrange("p (t c) -> p t c", t=TT)
        lf2 = tiny[:, 268:284].rearrange("p (t c) -> p t c", t=TT)
        lfx = tiny[:, 284:300].rearrange("p (t c) -> p t c", t=TT)
        half_b = tiny[:, 300:324]
        nF, nM, floor, den = (tiny[:, 324 + 16 * i:340 + 16 * i] for i in range(4))
        dil = tiny[:, 388:420]
        cst = tiny[:, 420:480]
        mmax, msum = tiny[:, 480:496], tiny[:, 496:512]
        den2 = tiny[:, 512:528]
        flat2 = PB[:, 0:3, :].rearrange("p a b -> p (a b)")[:, 0:960].rearrange(
            "p (i j c) -> p i j c", i=2, j=16)
        CM = SM[:, 2, 0:384]
        cmpPT = T2[:, 0, :].rearrange("p (g q) -> p g q", g=2)
        CH = T2[:, 1, 0:128].rearrange("p (i k c) -> p i k c", i=2, k=2)
        cvv = T2[:, 1, 128:256]
        ckT = T2[:, 1, 256:272]
        foxr = T1[:, 0, 0:256]
        PBF = PB[:, :, :].rearrange("p a b -> p (a b)")
        EB = PBF[:, 0:2048].rearrange("p (h i s) -> p h i s", h=2, i=4)
        WM = PBF[:, 2048:3072].rearrange("p (h s) -> p h s", h=2)
        GNU = SM[:, 0:2, :]
        erow = SM[:, 2, :]
        RSH, RSG, XC = xh[:, 0, 0:256], xh[:, 0, 512:1024], xh[:, 1, 0:512]
        QN, KN, ZC = BIG[:, 0:8, :], BIG[:, 8:16, :], BIG[:, 16:24, :]
        ZD, QR, LQ = QK[:, 0:4, :], QK[:, 4:8, :], QK[:, 8:14, :]
        KR = QK[:, 13:14, :]
        LS = xh[:, :, :].rearrange("p t d -> p (t d)")[:, 0:5 * S].rearrange("p (k q) -> p k q", k=5)
        RSL = T1[:, 0, :]
        CQ = UP[:, :, :].rearrange("p a b -> p (a b)")[:, 0:5 * S].rearrange("p (k q) -> p k q", k=5)
        MP = PBF[:, 0:2048].rearrange("p (h s) -> p h s", h=4)
        FT = Y[:, 12:16, :]
        F1 = BIG[:, 0:8, :].rearrange("p (g a) q -> p g (a q)", g=4)
        F2 = hT[:, 0:4, :]
        _o = C_AT["nsa_bias"][0]
        ropes = [cn[:, _o + i * S:_o + (i + 1) * S] for i in range(6)]

        def flat(i, j):
            return flat2[:, i, j, :]

        def cmph(i, k, g):
            return CH[:, i, k, g * 15:(g + 1) * 15]

        def cmpP(t, g):
            return CM[:, (g * 2 + t) * 96:(g * 2 + t + 1) * 96]

        WIDE = [u for s, n in STREAM if s not in ("cmp", "w_p", "down", "even_out", "w_uq", "w_uk", "w_uv",
                                                  "w_fd", "odd_out")
                for u in range(FIRST[s], FIRST[s] + n)]
        G_AT = {u: i for i, u in enumerate(WIDE)}

        def read(u):
            n = G_AT[u]
            return sem(f"bank_free[{n % 2}]"), n // 2 + 1

        @block.sync
        def _(sp):
            for src, dst, name in ((x, xa[:, :, :], "x_in"), (consts, cn[:, :], "consts_in"),
                                   (vecs, vc[:, :], "vecs_in"),
                                   (w_small, wsm[:, :, :], "w_small_in"),
                                   (cmp_w2, w2s[:, :, :, :], "cmp_w2_in")):
                nc.sync.dma_start(dst, src).then_inc(sem(name), 16)
            for s in range(RING):
                nc.sync.dma_start(ring[:, s, :], w[s]).then_inc(sem(f"unit_in[{s}]"), 16)
            nc.sync.dma_start(rw[:, :], rows.broadcast_to([P, NR_])).then_inc(sem("rows_in"), 16)
            with sp.Fori(1, NU // RING) as i:
                for s in range(RING):
                    sp.wait_ge(sem("unit_used"), i * RING + (s + 1 - RING))
                    nc.sync.dma_start(ring[:, s, :], w[bass.ds(i * RING + s, 1)].rearrange(
                        "o p n -> (o p) n")).then_inc(sem(f"unit_in[{s}]"), 16)
            for t in range(TT):
                sp.wait_ge(sem("out_ready"), t + 1)
                nc.sync.dma_start(out[t * P:(t + 1) * P, :], xb[:, t, :]).then_inc(sem("out_stored"), 16)
            sp.wait_ge(sem("out_stored"), 16 * TT)

        @block.tensor
        def _(pe):
            def unit_in(u):
                pe.wait_ge(sem(f"unit_in[{u % RING}]"), 16 * (u // RING + 1))
                return ring[:, u % RING, :]

            def mm(o, lhsT, rhs, start, stop):
                return nc.tensor.matmul(o, lhsT, rhs, start=start, stop=stop, skip_group_check=True)

            def g_bank(u):
                n = G_AT[u]
                if n >= 2:
                    pe.wait_ge(sem(f"bank_free[{n % 2}]"), n // 2)
                return PS[:, G[n % 2], :]

            def feature_tile(o, wt, col, src, kt=KD, width=256, last=True):
                for k in range(kt):
                    m = mm(o, wt[:, k * width + col:k * width + col + P], src[:, k, :], k == 0, k == kt - 1)
                return m

            def token_cols(o2, wt, a, b, src, kt=KD, width=256):
                for t in range(TT):
                    for k in range(kt):
                        m = mm(o2[t], src[:, k, t * P:(t + 1) * P], wt[:, k * width + a:k * width + b],
                               k == 0, k == kt - 1)
                return m

            def wide_b(u, src=hT):
                o, wt = g_bank(u), unit_in(u)
                feature_tile(o[:, 0:S], wt, 0, src)
                feature_tile(o[:, S:2 * S], wt, P, src).then_inc(sem("unit_used"), 1)

            def wide_a(u, src=hT):
                o, wt = g_bank(u), unit_in(u)
                token_cols([o[:, 0:256], o[:, 256:512]], wt, 0, 256, src).then_inc(sem("unit_used"), 1)

            def norm_transposes(n):
                for t in range(TT):
                    pe.wait_ge(sem("rows_scaled"), TT * n + t + 1)
                    for k in range(KD):
                        m = nc.tensor.transpose(
                            PS[:, 2 + k // 2, (k % 2) * S + t * P:(k % 2) * S + (t + 1) * P],
                            xh[:, t, k * P:(k + 1) * P], ident)
                m.then_inc(sem("rows_turned"), 1)

            def normed(n):
                pe.wait_ge(sem("hT_dve"), 4 * (n + 1))
                pe.wait_ge(sem("hT_act"), 4 * (n + 1))

            def deep(first, n, src):
                for i in range(n):
                    u = FIRST[first] + i
                    wt = unit_in(u)
                    for t in range(TT):
                        for kk in range(2):
                            k = 2 * i + kk
                            for h in range(2):
                                m = mm(PS[:, DEEP + 2 * t + h, :], src[:, k, t * P:(t + 1) * P],
                                       wt[:, kk * D + h * 512:kk * D + (h + 1) * 512],
                                       k == 0, k == 2 * n - 1)
                    m.then_inc(sem("unit_used"), 1)

            pe.wait_ge(sem("consts_in"), 16)
            norm_transposes(0)
            normed(0)
            pe.wait_ge(sem("w_small_in"), 16)
            for t in range(TT):
                for k in range(KD):
                    m = mm(PS[:, SC[0], t * 64:t * 64 + 22], hT[:, k, t * P:(t + 1) * P], wsm[:, k, 0:22],
                           k == 0, k == KD - 1)
            m.then_inc(sem("small_done"), 1)
            for i in range(8):
                wide_b(i)
            for i in range(8, 11):
                wide_a(i)
            o, wt = g_bank(11), unit_in(11)
            token_cols([o[:, 0:128], o[:, 128:256]], wt, 0, 128, hT)
            feature_tile(o[:, S:2 * S], wt, P, hT).then_inc(sem("unit_used"), 1)

            pe.wait_ge(sem("fox_logs"), 3)
            for half in range(2):
                for t in range(TT):
                    m = mm(PS[half * 64:half * 64 + 4, SC[0], 0:S], lfa[:, 16 + 4 * t:20 + 4 * t],
                           c("neg_upper", t * S, (t + 1) * S), t == 0, t == TT - 1)
            m.then_inc(sem("fox_rows"), 1)

            def cmp_hidden(i):
                for half in range(2):
                    u = FIRST["cmp"] + 2 * i + half
                    wt = unit_in(u)
                    pe.wait_ge(sem("flat_ready"), i + 1)
                    for k in range(8):
                        j = 8 * half + k
                        m = mm(PS[0:30, PT[i], 0:256], flat(i, j),
                               wt[:, k * 256:(k + 1) * 256], j == 0, j == 15)
                    m.then_inc(sem("unit_used"), 1)

            def cmp_out(i):
                pe.wait_ge(sem("cmp_gelu"), i + 1)
                for k in range(2):
                    m = nc.tensor.transpose(PS[:, AV[i], 32 * k:32 * k + 30],
                                            SM[0:30, i, k * P:(k + 1) * P], ident[0:30, 0:30])
                m.then_inc(sem("cmp_turned"), 1)
                pe.wait_ge(sem("cmp_hT"), i + 1)
                pe.wait_ge(sem("cmp_w2_in"), 16)
                for g in range(2):
                    for rep in range(3 if i else 1):
                        for k in range(2):
                            h = cmph(i, k, g)
                            if i == 0:
                                m = mm(PS[g * 64:g * 64 + 64, AV[0], 128:143], w2s[:, 0, k, :], h, k == 0, k == 1)
                            else:
                                m = mm(PS[32 * rep:32 * rep + 15, AV[1], 128 + g * 64:192 + g * 64], h,
                                       w2s[:, 1, k, :], k == 0, k == 1)
                m.then_inc(sem("cmp_done"), 1)

            def cmp_scores():
                pe.wait_ge(sem("cmp_kv"), 1)
                pe.wait_ge(*read(5))
                pe.wait_ge(*read(6))
                pe.wait_ge(sem("fox_rows_copied"), 2)
                for t in range(TT):
                    for h in range(6):
                        g = h // 3
                        m = mm(PS[:, SC[g], t * 96 + (h % 3) * 32:t * 96 + (h % 3) * 32 + 15],
                               QK[g * 64:g * 64 + 64, 10 + h % 3, t * P:(t + 1) * P],
                               ckT[g * 64:g * 64 + 64, 0:15], True, True)
                m.then_inc(sem("cmp_scores"), 1)

            def cmp_probs():
                pe.wait_ge(sem("cmp_probs"), 1)
                for t in range(TT):
                    for g in range(2):
                        m = nc.tensor.transpose(PS[0:96, PT[g], t * P:(t + 1) * P], cmpP(t, g), ident)
                m.then_inc(sem("cmp_probs_turned"), 1)

            def scores(j):
                kind, q, half, k, _, h = JOBS[j]
                last = 7 if kind in ("sel", "win") else 4
                pe.wait_ge(*read(last - 1))
                pe.wait_ge(*read(last))
                if j >= 2:
                    pe.wait_ge(sem("scores_read"), j - 1)
                else:
                    pe.wait_ge(sem("cmp_scores_read"), 1)
                if kind == "fox":
                    pe.wait_ge(sem("fox_rows_copied"), 2)
                b = SC[j % 2]
                lo = half * 64
                for t in range(TT):
                    o = PS[:, b, 0:P] if t == 0 else PS[:, b, P:P + S]
                    n = P * (t + 1)
                    m = mm(o, QK[lo:lo + 64, q, t * P:(t + 1) * P], QK[lo:lo + 64, k, 0:n],
                           True, kind != "fox")
                    if kind == "fox":
                        a, _ = C_AT["rows"]
                        m = mm(o, cn[lo:lo + 4, a + h * P:a + (h + 1) * P], foxr[lo:lo + 4, 0:n], False, True)
                m.then_inc(sem("scores"), 1)

            def turn(j):
                pe.wait_ge(sem("probs_scaled"), j + 1)
                if j >= 2:
                    pe.wait_ge(sem("probs_copied"), j - 1)
                else:
                    pe.wait_ge(sem("cmp_probs_copied"), 2)
                p, b = PB[:, j % 8, :], PT[j % 2]
                nc.tensor.transpose(PS[:, b, 0:P], p[:, 0:P], ident)
                nc.tensor.transpose(PS[:, b, P:2 * P], p[:, P:2 * P], ident)
                nc.tensor.transpose(PS[:, b, 2 * P:3 * P], p[:, 2 * P:3 * P], ident)\
                    .then_inc(sem("probs_turned"), 1)

            def pv(j):
                kind, _, half, _, col, h = JOBS[j]
                yt = Y_TILE[j]
                b, hb, copied = Y_PLACE[yt]
                pe.wait_ge(sem("y_copied"), copied) if copied else pe.wait_ge(sem("cmp_kv"), 2)
                bank = AV[b]
                lo = (h // 3 if kind in ("sel", "win") else h % 2) * 64
                o = PS[lo:lo + 64, bank, hb * S:(hb + 1) * S]
                first = kind != "win"
                if kind == "sel":
                    i = h % 3
                    pe.wait_ge(sem("cmp_probs_copied"), 2)
                    mm(o, cvv[32 * i:32 * i + 15, (h // 3) * 64:(h // 3 + 1) * 64],
                       cmpPT[32 * i:32 * i + 15, h // 3, :], True, False)
                    first = False
                for u in {"fox": (8,), "dil": (9, 10)}.get(kind, (10, 11)):
                    pe.wait_ge(*read(u))
                pe.wait_ge(sem("probs_copied"), j + 1)
                mm(o, V[:, 0, col:col + DH], PTS[:, j % 2, 0:S], first, False)
                m = mm(PS[lo:lo + 64, bank, hb * S + P:(hb + 1) * S], V[:, 1, col:col + DH], PTS[:, j % 2, S:S + P], False,
                       kind != "sel")
                m.then_inc(sem("pv_done"), 1)

            def step(j):
                if j < NJ:
                    scores(j)
                if 0 <= j - PT_LAG < NJ:
                    turn(j - PT_LAG)
                if 0 <= j - PV_LAG < NJ:
                    pv(j - PV_LAG)

            cmp_hidden(0)
            cmp_hidden(1)
            wide_b(FIRST["gates"])
            cmp_out(0)
            wide_b(FIRST["gates"] + 1)
            cmp_out(1)
            wide_b(FIRST["gates"] + 2)
            cmp_scores()
            wide_b(FIRST["gates"] + 3)
            cmp_probs()
            for j in range(NJ + PV_LAG):
                if j % 3 == 0 and 4 + j // 3 < 12:
                    wide_b(FIRST["gates"] + 4 + j // 3)
                step(j)

            pe.wait_ge(sem("y_copied"), len(COPIES))
            for i in range(8):
                u = FIRST["w_p"] + i // 2
                wt = unit_in(u)
                if i >= 2:
                    pe.wait_ge(sem("merged"), i - 1)
                o = (PS[:, 2 + 2 * (i % 2), 0:S], PS[:, 2 + 2 * (i % 2), S:2 * S], PS[:, 3 + 2 * (i % 2), 0:S])
                for s, (a, b) in enumerate(((0, 2), (2, 5), (5, 8))):
                    for k in range(a, b):
                        m = mm(o[s], wt[:, k * 256 + (i % 2) * P:k * 256 + (i % 2 + 1) * P], Y[:, k, :],
                               k == a, k == b - 1)
                if i % 2:
                    m.then_inc(sem("unit_used"), 1)
                else:
                    m.then_inc(sem("w_p_even"), 1)
            pe.wait_ge(sem("merged"), 8)
            for i in range(4):
                wide_a(FIRST["w_o"] + i, Y[:, 8:16, :])

            norm_transposes(1)
            normed(1)
            for i in range(NF):
                wide_b(FIRST["up"] + i)
            pe.wait_ge(*read(FIRST["up"] + NF - 2))
            pe.wait_ge(*read(FIRST["up"] + NF - 1))
            deep("down", 11, BIG)

            norm_transposes(2)
            normed(2)
            for t in range(TT):
                for k in range(KD):
                    m = mm(PS[:, SC[0], t * 64:t * 64 + 16], hT[:, k, t * P:(t + 1) * P], wsm[:, k, 22:38],
                           k == 0, k == KD - 1)
            m.then_inc(sem("small_done"), 1)
            for i in range(8):
                wide_b(FIRST["conv_in"] + i)
            for i in range(4):
                wide_b(FIRST["qk"] + i)
            for i in range(4):
                wide_a(FIRST["v"] + i)
            for i in range(4):
                wide_b(FIRST["z_a"] + i)
            for i in range(4):
                wide_b(FIRST["o"] + i)

            pe.wait_ge(sem("lstm_logs"), 4)
            for d, (tri, f0, i0) in enumerate((("neg_upper", 0, 0), ("neg_lower", 4, 8))):
                for t in range(TT):
                    mm(PS[0:4, SC[1], d * S:(d + 1) * S], lf2[:, t, f0:f0 + 4], c(tri, t * S, (t + 1) * S),
                       t == 0, False)
                for t in range(TT):
                    m = mm(PS[0:4, SC[1], d * S + t * P:d * S + (t + 1) * P], gt2[:, t, i0:i0 + 4], ident,
                           False, t == TT - 1)
            for d, (tri, f0) in enumerate((("neg_upper", 0), ("neg_lower", 4))):
                for t in range(TT):
                    for j in range(TT):
                        m = mm(PS[:, SC[0], 128 + 8 * d + 4 * t:132 + 8 * d + 4 * t],
                               c(tri, j * S + t * P, j * S + (t + 1) * P), lf2[:, j, f0:f0 + 4],
                               j == 0, j == TT - 1)
            m.then_inc(sem("lstm_rows"), 1)

            def lstm_scores(h):
                pe.wait_ge(sem("lstm_rows_copied"), 2)
                pe.wait_ge(*read(FIRST["qk"] + h))
                if h >= 1:
                    pe.wait_ge(sem("lstm_decay_read"), 4 * h)
                a, _ = C_AT["rows"]
                mm(PS[:, SC[0], :], cn[0:4, a + h * P:a + (h + 1) * P], erow[0:4, :], True, True)\
                    .then_inc(sem("lstm_decay"), 1)
                if h >= 1:
                    pe.wait_ge(sem("lstm_scores_read"), 4 * h)
                for t in range(TT):
                    m = mm(PS[:, SC[1], t * S:(t + 1) * S], QK[:, 2 * h, t * P:(t + 1) * P],
                           QK[:, 2 * h + 1, :], True, True)
                m.then_inc(sem("lstm_scores"), 1)

            def lstm_turn(h):
                pe.wait_ge(sem("lstm_w"), h + 1)
                if h >= 1:
                    pe.wait_ge(sem("lstm_wT"), h)
                for t in range(TT):
                    for s in range(TT):
                        m = nc.tensor.transpose(PS[:, PT[0], s * S + t * P:s * S + (t + 1) * P],
                                                WM[:, h % 2, t * S + s * P:t * S + (s + 1) * P], ident)
                m.then_inc(sem("lstm_turned"), 1)

            def lstm_pv(h):
                pe.wait_ge(sem("lstm_wT"), h + 1)
                pe.wait_ge(*read(FIRST["v"] + h))
                if h >= 1:
                    pe.wait_ge(sem("yb_done"), h)
                for e in range(2):
                    for s in range(TT):
                        m = mm(PS[:, AV[0], e * S:(e + 1) * S], V[:, s, h * 256 + e * P:h * 256 + (e + 1) * P],
                               PTS[:, h % 2, s * S:(s + 1) * S], s == 0, s == TT - 1)
                m.then_inc(sem("lstm_h"), 1)

            def lstm_var(h):
                pe.wait_ge(sem("lstm_sq"), h + 1)
                for e in range(2):
                    m = mm(PS[:, AV[1], 0:S], c("mean", P, 2 * P), T1[:, 0, e * S:(e + 1) * S], e == 0, e == 1)
                m.then_inc(sem("lstm_var"), 1)

            def gn(i):
                pe.wait_ge(sem("gn_u"), i + 1)
                if i >= 1:
                    pe.wait_ge(sem("gn_done"), i)
                mm(PS[:, PT[1], :], c("mean", 0, P), GNU[:, i % 2, :], True, True).then_inc(sem("gn_mean"), 1)

            def gn_var(i):
                pe.wait_ge(sem("gn_sq"), i + 1)
                mm(PS[:, PT[1], :], c("mean", 0, P), T2[:, 0, :], True, True).then_inc(sem("gn_var"), 1)

            for kind, n in EVEN_STEPS:
                if kind == "z_b":
                    wide_b(FIRST["z_b"] + n)
                elif kind == "scores":
                    lstm_scores(n)
                elif kind == "turn":
                    lstm_turn(n)
                elif kind == "pv":
                    lstm_pv(n)
                elif kind == "var":
                    lstm_var(n)
                elif kind == "gn":
                    gn(n)
                elif kind == "gn_var":
                    gn_var(n)
            pe.wait_ge(sem("gn_done"), 4)
            pe.wait_ge(sem("yb_done"), 4)
            deep("even_out", 8, Y)

            norm_transposes(3)
            normed(3)
            for i in range(3):
                wide_b(FIRST["lora"] + i)
            pe.wait_ge(sem("lora_sq"), 1)
            for k in range(3):
                mm(PS[:, SC[0], 0:S], c("mean", 256, 384), LS[:, k, :], k == 0, k == 2)
            for k in range(2):
                m = mm(PS[:, SC[0], S:2 * S], c("mean", P, 2 * P), LS[:, 3 + k, :], k == 0, k == 1)
            m.then_inc(sem("lora_var"), 1)
            for i in range(2):
                wide_b(FIRST["f_in"] + i)

            def rope_swap(n, src):
                pe.wait_ge(*((sem(f"uq_read[{n}]"), 3) if n < 2 else read(FIRST["lora"] + 2)))
                if n >= 1:
                    pe.wait_ge(sem("rope_swapped_read"), n)
                w_ = 512 if n < 2 else 256
                mm(PS[:, SC[1], 0:w_], c("rope_swap"), src, True, True).then_inc(sem("rope_swapped"), 1)

            def uq_bank(n):
                if n >= 2:
                    pe.wait_ge(sem(f"uq_read[{n % 2}]"), n // 2)

            def uq_done(m, n):
                m.then_inc(sem(UQ_DONE[n][0]), 1)

            pe.wait_ge(sem("lora_ready"), 5)
            for i in range(3):
                u = FIRST["w_uq"] + i
                for half in range(2):
                    n = 2 * i + half
                    uq_bank(n)
                    wt = unit_in(u)
                    for j in range(2):
                        for k in range(3):
                            m = mm(PS[:, PT[n % 2], j * S:(j + 1) * S],
                                   wt[:, (2 * half + j) * 384 + k * P:(2 * half + j) * 384 + (k + 1) * P],
                                   CQ[:, k, :], k == 0, k == 2)
                    uq_done(m, n)
            pe.wait_ge(sem("late_in"), 16)
            rope_swap(0, QR[:, 0:2, :])
            wt = unit_in(FIRST["w_uk"])
            for n in range(4):
                uq_bank(6 + n)
                for j in range(2):
                    i = 2 * n + j
                    for k in range(2):
                        m = mm(PS[:, PT[n % 2], j * S:(j + 1) * S], wt[:, i * 256 + k * P:i * 256 + (k + 1) * P],
                               CQ[:, 3 + k, :], k == 0, k == 1)
                uq_done(m, 6 + n)
                if n == 1:
                    rope_swap(1, QR[:, 2:4, :])
            rope_swap(2, KR[:, 0, :])
            wt = unit_in(FIRST["w_uv"])
            for n in range(4):
                uq_bank(10 + n)
                t, h = n // 2, n % 2
                for k in range(2):
                    m = mm(PS[:, PT[n % 2], :], CQ[:, 3 + k, t * P:(t + 1) * P],
                           wt[:, k * D + h * 512:k * D + (h + 1) * 512], k == 0, k == 1)
                uq_done(m, 10 + n)

            def mla_scores(h):
                if h == 0:
                    pe.wait_ge(sem("uq_read[0]"), 7)
                    pe.wait_ge(sem("uq_read[1]"), 7)
                    pe.wait_ge(sem("rope_ready"), 3)
                if h >= 2:
                    pe.wait_ge(sem("mla_probs"), 2 * (h - 1))
                lo = 64 * (h % 2)
                for t in range(TT):
                    mm(PS[:, SC[h % 2], t * S:(t + 1) * S], QN[:, h, t * P:(t + 1) * P], KN[:, h, :], True, False)
                    m = mm(PS[:, SC[h % 2], t * S:(t + 1) * S], QR[lo:lo + 64, h // 2, t * P:(t + 1) * P],
                           KR[lo:lo + 64, 0, :], False, True)
                m.then_inc(sem("mla_scores"), 1)

            def mla_turn(h):
                pe.wait_ge(sem("mla_scaled"), h + 1)
                if h >= 2:
                    pe.wait_ge(sem("mla_copied"), h - 1)
                for t in range(TT):
                    for s in range(TT):
                        m = nc.tensor.transpose(PS[:, PT[h % 2], s * S + t * P:s * S + (t + 1) * P],
                                                MP[:, h % 4, t * S + s * P:t * S + (s + 1) * P], ident)
                m.then_inc(sem("mla_turned"), 1)

            def mla_pv(h):
                pe.wait_ge(sem("mla_copied"), h + 1)
                if h >= 2:
                    pe.wait_ge(sem("yc_done"), h - 1)
                for s in range(TT):
                    m = mm(PS[:, AV[h % 2], 0:S], V[:, s, h * P:(h + 1) * P], PTS[:, h % 2, s * S:(s + 1) * S],
                           s == 0, s == TT - 1)
                m.then_inc(sem("mla_out"), 1)

            for i in range(8 + 3):
                if i < 8:
                    mla_scores(i)
                if i < 4:
                    wide_b(FIRST["z_c"] + i)
                elif i < 6:
                    wide_b(FIRST["z_d"] + i - 4)
                if 2 <= i < 10:
                    mla_turn(i - 2)
                if i >= 3:
                    mla_pv(i - 3)

            pe.wait_ge(*read(FIRST["f_in"]))
            pe.wait_ge(*read(FIRST["f_in"] + 1))
            for g in range(4):
                for t in range(TT):
                    n = 2 * g + t
                    if n % 2 == 0 and n >= 4:
                        pe.wait_ge(sem("fft1_copied"), n // 2 - 1)
                    if n == 0:
                        pe.wait_ge(sem("mla_scaled"), 8)
                    m = mm(PS[:, SC[g % 2], t * S:(t + 1) * S], FT[:, g, t * P:(t + 1) * P], c("dft_ch"), True, True)
                m.then_inc(sem("fft1"), 1)
            for g in range(4):
                pe.wait_ge(sem("fft1_copied"), g + 1)
                if g == 0:
                    pe.wait_ge(sem("mla_copied"), 8)
                o = PS[:, PT[g // 2], (g % 2) * S:(g % 2 + 1) * S]
                for t in range(TT):
                    mm(o, F1[:, g, t * S:t * S + P], c("dft_cos", t * S, (t + 1) * S), t == 0, False)
                for t in range(TT):
                    m = mm(o, F1[:, g, t * S + P:(t + 1) * S], c("dft_nsin", t * S, (t + 1) * S), False, t == 1)
                if g % 2:
                    m.then_inc(sem("fft2"), 1)
            wt = unit_in(FIRST["w_fd"])
            pe.wait_ge(sem("fft2_copied"), 2)
            pe.wait_ge(sem("yc_done"), 8)
            for j in range(4):
                for k in range(4):
                    m = mm(PS[:, AV[j // 2], (j % 2) * S:(j % 2 + 1) * S], wt[:, k * 512 + j * P:k * 512 + (j + 1) * P],
                           F2[:, k, :], k == 0, k == 3)
            m.then_inc(sem("unit_used"), 1)
            pe.wait_ge(sem("yd_done"), 2)
            deep("odd_out", 6, Y)

        def done(u):
            return sem("unit_used"), u + 1

        def bank_of(u):
            return PS[:, G[G_AT[u] % 2], :]

        def freed(ins, u):
            return ins.then_inc(sem(f"bank_free[{G_AT[u] % 2}]"), 1)

        def cols2(ap, n=2):
            return ap.rearrange("p (t c) -> p t c", t=n)

        def uq_dest(n):
            if n < 4:
                return QN[:, 2 * n:2 * n + 2, :]
            if n < 6:
                return QR[:, 2 * n - 8:2 * n - 6, :]
            if n < 10:
                return KN[:, 2 * n - 12:2 * n - 10, :]
            return V[:, (n - 10) // 2, (n % 2) * 512:(n % 2 + 1) * 512]

        def add_pe(eng, i):
            return eng.tensor_tensor(flat2[:, i], flat2[:, i], v("pe", 0, 16).unsqueeze(2).broadcast_to(
                [P, 16, 30]), ALU.add)

        @block.scalar
        def _(act):
            A = nc.scalar.activation

            def row_stat(m, t, src):
                A(cols2(T1[:, :, :].rearrange("p a b -> p (a b)")), src, ACT.Square, scale=D ** -0.5,
                  accum_out=ssq[:, TT * m + t:TT * m + t + 1]).then_inc(sem("row_ssq"), 1)
                act.wait_ge(sem("row_ssq"), TT * m + t + 1)
                A(rms[:, TT * m + t:TT * m + t + 1], ssq[:, TT * m + t:TT * m + t + 1], ACT.Sqrt,
                  bias=eps_t[:, 0:1]).then_inc(sem("row_rms"), 1)

            def turned_evac(n, gain):
                act.wait_ge(sem("rows_turned"), n + 1)
                for k in range(4, 8):
                    A(hT[:, k, :], PS[:, 2 + k // 2, (k % 2) * S:(k % 2 + 1) * S], ACT.Copy,
                      scale=v(gain, k)).then_inc(sem("hT_act"), 1)

            def flat_copies(i, u, col, bias):
                act.wait_ge(*done(u))
                b = G[G_AT[u] % 2]
                for g in range(2):
                    src = PS[g * 64:g * 64 + 64, b, col:col + S].rearrange("p (c j r) -> p j c r", c=16, j=8)
                    for par in range(2):
                        for a in range(2):
                            ins = A(flat2[par * 64:par * 64 + 64, i, a * 8:a * 8 + 8, g * 15:g * 15 + 15],
                                    src[:, :, a:a + 15, par], ACT.Identity,
                                    bias=v("b_feat", bias)[g * 64:g * 64 + 64, :])
                return ins

            for name in ("x_in", "vecs_in"):
                act.wait_ge(sem(name), 16)
            act.wait_ge(sem("eps_set"), 2)
            nc.scalar.dma_start(gB[:, :], gains[0:1, :].broadcast_to([P, D])).then_inc(sem("gains_in"), 16)
            for t in range(TT):
                row_stat(0, t, cols2(xa[:, t, :]))
            turned_evac(0, "g1")
            act.wait_ge(sem("fox_logs"), 1)
            e1 = lfa[:, 0:8]
            A(e1, e1, ACT.Exp, scale=-1.0).then_inc(sem("fox_exp"), 1)
            act.wait_ge(sem("fox_exp"), 1)
            A(e1, e1, ACT.Ln, bias=1.0).then_inc(sem("fox_exp"), 1)
            A(cols2(gnsa), small[:, :, 4:22], ACT.Tanh, scale=0.5).then_inc(sem("nsa_tanh"), 1)

            for i in range(7):
                act.wait_ge(*done(i))
                for j in range(2):
                    ins = A(QK[:, 2 * i + j, :], bank_of(i)[:, j * S:(j + 1) * S], ACT.Identity,
                            bias=v("b_feat", 2 * i + j))
                freed(ins, i)
            act.wait_ge(*done(7))
            A(QK[:, 14, :], bank_of(7)[:, 0:S], ACT.Identity, bias=v("b_feat", 14))
            freed(flat_copies(0, 7, S, 15), 7)
            flat_copies(1, 11, S, 16).then_inc(sem("vc_flat"), 1)
            act.wait_ge(sem("fox_rows"), 1)
            for half in range(2):
                lo = 64 * half
                A(foxr[lo:lo + 4, :], PS[lo:lo + 4, SC[0], 0:S], ACT.Copy).then_inc(sem("fox_rows_copied"), 1)

            def gate(i):
                u = FIRST["gates"] + i
                act.wait_ge(*done(u))
                for j in range(2):
                    ins = A(BIG[:, 2 * i + j, :], bank_of(u)[:, j * S:(j + 1) * S], ACT.Tanh, scale=0.5,
                            bias=half_b[:, 2 * i + j:2 * i + j + 1])
                freed(ins, u)

            def cmp_gelu(i):
                act.wait_ge(*done(FIRST["cmp"] + 2 * i + 1))
                A(SM[0:30, i, 0:256], PS[0:30, PT[i], 0:256], ACT.Gelu_apprx_tanh).then_inc(sem("cmp_gelu"), 1)

            def cmp_kv(i):
                act.wait_ge(sem("cmp_turned"), i + 1)
                A(CH[:, i, :, 0:30], cols2(PS[:, AV[i], 0:64])[:, :, 0:30], ACT.Copy).then_inc(sem("cmp_hT"), 1)
                act.wait_ge(sem("cmp_done"), i + 1)
                if i == 0:
                    ins = A(ckT[:, 0:15], PS[:, AV[0], 128:143], ACT.Copy)
                else:
                    for rep in range(3):
                        ins = A(cvv[32 * rep:32 * rep + 15, :], PS[32 * rep:32 * rep + 15, AV[1], 128:256],
                                ACT.Copy)
                ins.then_inc(sem("cmp_kv"), 1)

            act.wait_ge(sem("half_bias"), 1)
            cmp_gelu(0)
            cmp_gelu(1)
            cmp_kv(0)
            gate(0)
            cmp_kv(1)
            gate(1)
            gate(2)
            act.wait_ge(sem("cmp_centred"), 1)
            cm12 = cols2(CM, 12)[:, :, 0:15]
            A(cm12, cm12, ACT.Exp).then_inc(sem("cmp_exp"), 1)
            gate(3)
            act.wait_ge(sem("cmp_probs_turned"), 1)
            for g in range(2):
                A(cmpPT[0:96, g, :], PS[0:96, PT[g], 0:S], ACT.Copy).then_inc(sem("cmp_probs_copied"), 1)

            def exp_job(j):
                act.wait_ge(sem("scores_read"), j + 1)
                if j >= 8:
                    act.wait_ge(sem("probs_turned"), j - 7)
                for t in range(TT):
                    a, b = (0, P) if t == 0 else (P, 3 * P)
                    A(PB[:, j % 8, a:b], SM[:, j % 3, a:b], ACT.Exp, scale=-1.0,
                      bias=nmax[:, 2 * j + t:2 * j + t + 1],
                      accum_out=lsum[:, 2 * j + t:2 * j + t + 1]).then_inc(sem("att_exp"), 1)

            def dil_exp(n):
                act.wait_ge(sem("dil_diff"), n + 1)
                A(dil[:, 0:6], dil[:, 0:6], ACT.Exp).then_inc(sem("dil_exp"), 1)

            def probs_copy(j):
                act.wait_ge(sem("probs_turned"), j + 1)
                if j >= 2:
                    act.wait_ge(sem("pv_done"), j - 1)
                A(PTS[:, j % 2, 0:384], PS[:, PT[j % 2], 0:384], ACT.Copy).then_inc(sem("probs_copied"), 1)

            for j in range(NJ + PV_LAG):
                if j % 3 == 0 and 4 + j // 3 < 12:
                    gate(4 + j // 3)
                if j < NJ:
                    exp_job(j)
                    if j in (6, 9):
                        dil_exp((j - 6) // 3)
                if 0 <= j - PT_LAG < NJ:
                    probs_copy(j - PT_LAG)
            act.wait_ge(sem("scores_read"), NJ)
            nc.scalar.dma_start(cn[:, C_AT["dil_bias"][0]:C_AT["dil_bias"][0] + NL_], late).then_inc(sem("late_in"), 16)
            nc.scalar.dma_start(ropes[5].bitcast(I32), positions.broadcast_to([P, S]))\
                .then_inc(sem("positions_in"), 16)

            for i in range(2):
                act.wait_ge(*read(FIRST["w_o"] + 2 + i))
            for t in range(TT):
                row_stat(1, t, cols2(xb[:, t, :]))
            turned_evac(1, "g2")
            CV = T2
            for i in range(NF):
                u = FIRST["up"] + i
                act.wait_ge(*done(u))
                A(CV[:, i % 2, 0:S], bank_of(u)[:, 0:S], ACT.Identity, scale=v("conv_w", 2 * NF + i),
                  bias=v("conv_b", i)).then_inc(sem("ffn_tap"), 1)
                act.wait_ge(sem("ffn_conv"), i + 1)
                A(CV[:, i % 2, S:2 * S], CV[:, i % 2, 0:S], ACT.Gelu_apprx_tanh).then_inc(sem("ffn_gelu"), 1)
            act.wait_ge(sem("angles"), 1)
            A(ropes[0], ropes[0], ACT.Sin).then_inc(sem("rope_tables"), 1)
            A(ropes[1], ropes[1], ACT.Sin).then_inc(sem("rope_tables"), 1)
            for t in range(TT):
                act.wait_ge(sem("x2_ready"), t + 1)
                row_stat(2, t, cols2(xa[:, t, :]))
            for t in range(TT):
                act.wait_ge(sem("x3_ready"), t + 1)
                row_stat(3, t, cols2(xb[:, t, :]))
            nc.scalar.dma_start(gB[:, :], gains[1:2, :].broadcast_to([P, D])).then_inc(sem("gains_in"), 16)

            turned_evac(2, "g3")
            act.wait_ge(sem("lstm_logs"), 2)
            A(lfx, lfx, ACT.Exp, scale=-1.0).then_inc(sem("lstm_exp"), 1)
            act.wait_ge(sem("lstm_exp"), 1)
            A(lfx, lfx, ACT.Ln, bias=1.0).then_inc(sem("lstm_exp"), 1)
            for i in range(8):
                u = FIRST["conv_in"] + i
                act.wait_ge(*done(u))
                A(T1[:, i % 2, 0:S], bank_of(u)[:, S:2 * S], ACT.Tanh, scale=0.5).then_inc(sem("a_gate"), 1)
            for i in range(4):
                u = FIRST["qk"] + i
                act.wait_ge(*done(u))
                freed(A(QK[:, 2 * i:2 * i + 2, :], cols2(bank_of(u)), ACT.Copy), u)
            for i in range(4):
                u = FIRST["v"] + i
                act.wait_ge(*done(u))
                freed(A(V[:, :, i * 256:(i + 1) * 256], cols2(bank_of(u)), ACT.Copy), u)
            for i in range(4):
                u = FIRST["z_a"] + i
                act.wait_ge(*done(u))
                freed(A(BIG[:, 2 * i:2 * i + 2, :], cols2(bank_of(u)), ACT.Silu), u)
            for i in range(4):
                u = FIRST["o"] + i
                act.wait_ge(*done(u))
                freed(A(BIG[:, 8 + 2 * i:10 + 2 * i, :], cols2(bank_of(u)), ACT.Tanh, scale=0.5), u)
            act.wait_ge(sem("lstm_rows"), 1)
            A(erow[0:4, :], PS[0:4, SC[1], :], ACT.Copy).then_inc(sem("lstm_rows_copied"), 1)
            A(nF, PS[:, SC[0], 128:144], ACT.Copy).then_inc(sem("lstm_rows_copied"), 1)

            for kind, n in EVEN_STEPS:
                if kind == "scores":
                    for i, (a, b) in enumerate(LSTM_COLS):
                        act.wait_ge(sem("lstm_decay_read"), 4 * n + i + 1)
                        A(EB[:, n % 2, i, a:b], EB[:, n % 2, i, a:b], ACT.Exp, scale=-1.0,
                          bias=nM[:, 4 * n + i:4 * n + i + 1]).then_inc(sem("lstm_dw"), 1)
                    act.wait_ge(sem("lstm_arg"), n + 1)
                    A(floor[:, 4 * n:4 * n + 4], floor[:, 4 * n:4 * n + 4], ACT.Exp).then_inc(sem("lstm_floor"), 1)
                elif kind == "z_b":
                    u = FIRST["z_b"] + n
                    act.wait_ge(*done(u))
                    A(T1[:, 1, :], bank_of(u), ACT.Tanh, scale=0.5).then_inc(sem("zb_tanh"), 1)
                elif kind == "turn":
                    act.wait_ge(sem("lstm_turned"), n + 1)
                    A(PTS[:, n % 2, :], PS[:, PT[0], :], ACT.Copy).then_inc(sem("lstm_wT"), 1)
                elif kind == "pv":
                    act.wait_ge(sem("lstm_h"), n + 1)
                    A(T1[:, 0, :], PS[:, AV[0], :], ACT.Square).then_inc(sem("lstm_sq"), 1)
                elif kind == "var":
                    act.wait_ge(sem("lstm_var"), n + 1)
                    A(RSH, PS[:, AV[1], 0:S], ACT.Ln, bias=eps_t[:, 0:1]).then_inc(sem("lstm_rs"), 1)
                    act.wait_ge(sem("lstm_rs"), 2 * n + 1)
                    A(RSH, RSH, ACT.Exp, scale=-0.5).then_inc(sem("lstm_rs"), 1)
                elif kind == "gn":
                    act.wait_ge(sem("gn_xc"), n + 1)
                    A(T2[:, 0, :], XC, ACT.Square).then_inc(sem("gn_sq"), 1)
                elif kind == "gn_var":
                    act.wait_ge(sem("gn_var"), n + 1)
                    A(RSG, PS[:, PT[1], :], ACT.Ln, bias=eps_t[:, 1:2]).then_inc(sem("gn_rs"), 1)
                    act.wait_ge(sem("gn_rs"), 2 * n + 1)
                    A(RSG, RSG, ACT.Exp, scale=-0.5).then_inc(sem("gn_rs"), 1)
                    act.wait_ge(sem("gn_xg"), n + 1)
                    A(T2[:, 1, :], XC, ACT.Tanh, scale=0.5).then_inc(sem("gn_tanh"), 1)
            act.wait_ge(*done(FIRST["even_out"] + 7))
            for t in range(TT):
                row_stat(4, t, PS[:, DEEP + 2 * t:DEEP + 2 * t + 2, :])
            for t in range(TT):
                act.wait_ge(sem("x4_ready"), t + 1)
                row_stat(5, t, cols2(xa[:, t, :]))
            nc.scalar.dma_start(gB[:, :], gains[2:3, :].broadcast_to([P, D])).then_inc(sem("gains_in"), 16)

            turned_evac(3, "g4")
            for i in range(3):
                u = FIRST["lora"] + i
                act.wait_ge(*done(u))
                freed(A(LQ[:, 2 * i:2 * i + 2, :], cols2(bank_of(u)), ACT.Copy), u)
            act.wait_ge(*read(FIRST["lora"] + 1))
            act.wait_ge(*read(FIRST["lora"] + 2))
            A(LS, LQ[:, 0:5, :], ACT.Square).then_inc(sem("lora_sq"), 1)
            act.wait_ge(sem("lora_var"), 1)
            A(RSL, PS[:, SC[0], :], ACT.Ln, bias=eps_t[:, 0:1]).then_inc(sem("lora_rs"), 1)
            act.wait_ge(sem("lora_rs"), 1)
            A(RSL, RSL, ACT.Exp, scale=-0.5).then_inc(sem("lora_rs"), 1)
            for i in range(2):
                u = FIRST["f_in"] + i
                act.wait_ge(*done(u))
                freed(A(FT[:, 2 * i:2 * i + 2, :], cols2(bank_of(u)), ACT.Copy), u)
            for n in range(0, 14, 2):
                name, value = UQ_DONE[n]
                act.wait_ge(sem(name), value)
                A(uq_dest(n), cols2(PS[:, PT[0], :]) if n < 10 else PS[:, PT[0], :], ACT.Copy)\
                    .then_inc(sem("uq_read[0]"), 1)

            for i in range(8 + 3):
                if i < 8:
                    act.wait_ge(sem("mla_max"), i + 1)
                    if i >= 4:
                        act.wait_ge(sem("mla_turned"), i - 3)
                    for t in range(TT):
                        A(MP[:, i % 4, t * S:(t + 1) * S], PS[:, SC[i % 2], t * S:(t + 1) * S], ACT.Exp,
                          scale=MLA_SCALE, bias=mmax[:, 2 * i + t:2 * i + t + 1],
                          accum_out=msum[:, 2 * i + t:2 * i + t + 1]).then_inc(sem("mla_probs"), 1)
                if i < 6:
                    u = (FIRST["z_c"] if i < 4 else FIRST["z_d"] - 4) + i
                    act.wait_ge(*done(u))
                    A(T1[:, i % 2, :], bank_of(u), ACT.Tanh, scale=0.5).then_inc(sem("zcd_tanh"), 1)
                if 2 <= i < 10:
                    h = i - 2
                    act.wait_ge(sem("mla_turned"), h + 1)
                    if h >= 2:
                        act.wait_ge(sem("mla_out"), h - 1)
                    A(PTS[:, h % 2, :], PS[:, PT[h % 2], :], ACT.Copy).then_inc(sem("mla_copied"), 1)
            for g in range(4):
                act.wait_ge(sem("fft1"), g + 1)
                A(F1[:, g, :], PS[:, SC[g % 2], :], ACT.Copy).then_inc(sem("fft1_copied"), 1)
            act.wait_ge(*done(FIRST["odd_out"] + 5))
            for t in range(TT):
                row_stat(6, t, PS[:, DEEP + 2 * t:DEEP + 2 * t + 2, :])

        @block.vector
        def _(dve):
            TTn, TS, STT = nc.vector.tensor_tensor, nc.vector.tensor_scalar, nc.vector.scalar_tensor_tensor
            steps = {"n": 0}

            def own(ins):
                steps["n"] += 1
                return ins.then_inc(sem("dve_step"), 1)

            def settled():
                dve.wait_ge(sem("dve_step"), steps["n"])

            def row_rstd(m, t):
                dve.wait_ge(sem("row_rms"), TT * m + t + 1)
                q = rms[:, TT * m + t:TT * m + t + 1]
                own(nc.vector.reciprocal(q, q))
                settled()
                return q

            def rows_scale(m, src):
                for t in range(TT):
                    TS(xh[:, t, :], src[:, t, :], row_rstd(m, t), None, ALU.mult).then_inc(sem("rows_scaled"), 1)

            def turned_evac(n, gain):
                dve.wait_ge(sem("rows_turned"), n + 1)
                for k in range(4):
                    TS(hT[:, k, :], PS[:, 2 + k // 2, (k % 2) * S:(k % 2 + 1) * S], v(gain, k), None,
                       ALU.mult).then_inc(sem("hT_dve"), 1)

            nc.vector.memset(eps_t[:, 0:1], EPS).then_inc(sem("eps_set"), 1)
            nc.vector.memset(eps_t[:, 1:2], LN_EPS).then_inc(sem("eps_set"), 1)
            for name in ("x_in", "vecs_in"):
                dve.wait_ge(sem(name), 16)
            TS(half_b, v("b_gates", 0, 24), 0.5, None, ALU.mult).then_inc(sem("half_bias"), 1)
            rows_scale(0, xa)
            turned_evac(0, "g1")
            dve.wait_ge(sem("small_done"), 1)
            dve.wait_ge(sem("rows_in"), 16)
            own(TTn(small, cols2(PS[:, SC[0], 0:128])[:, :, 0:22],
                    r("b_small").unsqueeze(1).broadcast_to([P, TT, 22]), ALU.add))
            settled()
            f = small[:, :, 0:4]
            STT(cols2(lfa[:, 0:8]), f, -1.0, f, ALU.mult, ALU.max).then_inc(sem("fox_logs"), 1)
            dve.wait_ge(sem("fox_exp"), 2)
            STT(cols2(lfa[:, 8:16]), f, 0.0, cols2(lfa[:, 0:8]), ALU.min, ALU.subtract).then_inc(sem("fox_logs"), 1)
            dve.wait_ge(sem("fox_logs"), 2)
            TS(lfa[:, 16:24], lfa[:, 8:16], 8.0, None, ALU.mult).then_inc(sem("fox_logs"), 1)
            dve.wait_ge(sem("nsa_tanh"), 1)
            TS(gnsa, gnsa, 1.0, 0.5, ALU.add, ALU.mult).then_inc(sem("nsa_gates"), 1)

            for i in range(8, 12):
                dve.wait_ge(*done(i))
                if i == 11:
                    dve.wait_ge(sem("vc_flat"), 1)
                a = (i - 8) * 256
                n = 256 if i < 11 else 128
                b = cols2(bank_of(i)[:, 0:2 * n])
                freed(TTn(V[:, :, a:a + n], b, r("b_v", a, a + n).unsqueeze(1).broadcast_to([P, TT, n]),
                          ALU.add), i)
                if i == 8:
                    dve.wait_ge(*read(7))
                    add_pe(nc.vector, 0).then_inc(sem("flat_ready"), 1)
            dve.wait_ge(sem("vc_flat"), 1)
            add_pe(nc.vector, 1).then_inc(sem("flat_ready"), 1)

            dve.wait_ge(sem("cmp_scores"), 1)
            dve.wait_ge(sem("cm_zero"), 1)
            for g in range(2):
                view = [cols2(q, 6)[:, :, 0:15] for q in
                        (CM[:, g * 192:g * 192 + 192], PS[:, SC[g], 0:192], c("cmp_bias", g * 192, g * 192 + 192))]
                STT(view[0], view[1], DH ** -0.5, view[2], ALU.mult, ALU.add).then_inc(sem("cmp_scores_read"), 1)
            dve.wait_ge(sem("cmp_scores_read"), 2)
            cm12 = cols2(CM, 12)[:, :, 0:15]
            own(nc.vector.tensor_reduce(cst[:, 0:12], cm12, AX.X, ALU.max))
            settled()
            TTn(cm12, cm12, cst[:, 0:12].unsqueeze(2).broadcast_to([P, 12, 15]), ALU.subtract)\
                .then_inc(sem("cmp_centred"), 1)
            dve.wait_ge(sem("cmp_exp"), 1)
            own(TTn(cm12, cm12, cols2(c("cmp_mask"), 12)[:, :, 0:15], ALU.mult))
            settled()
            own(nc.vector.tensor_reduce(cst[:, 12:24], cm12, AX.X, ALU.add))
            settled()
            own(TS(cst[:, 12:24], cst[:, 12:24], 1e-30, None, ALU.max))
            settled()
            own(nc.vector.reciprocal(cst[:, 24:36], cst[:, 12:24]))
            settled()
            gates3 = cols2(gnsa).rearrange("p t (h b) -> p t h b", b=3)
            dve.wait_ge(sem("nsa_gates"), 1)
            for g in range(2):
                own(TTn(cols2(cst[:, 36 + 6 * g:42 + 6 * g]), cols2(cst[:, 24 + 6 * g:30 + 6 * g]),
                        gates3[:, :, 3 * g:3 * g + 3, 0], ALU.mult))
            settled()
            TTn(cm12, cm12, cst[:, 36:48].unsqueeze(2).broadcast_to([P, 12, 15]), ALU.mult)\
                .then_inc(sem("cmp_probs"), 1)

            def scores_in(j):
                kind, h = JOBS[j][0], JOBS[j][5]
                dve.wait_ge(sem("scores"), j + 1)
                if j >= 3:
                    dve.wait_ge(sem("att_exp"), 2 * (j - 2))
                tab = "causal" if kind == "fox" else "dil_bias" if kind == "dil" else "nsa_bias"
                o = 0 if kind == "fox" else h * S
                for t in range(TT):
                    a, b, q = (0, P, o + P) if t == 0 else (P, 3 * P, o)
                    ins = nc.vector.tensor_tensor_reduce(
                        SM[:, j % 3, a:b], PS[:, SC[j % 2], a:b], c(tab, q, q + b - a), -DH ** -0.5, 3e38,
                        ALU.add, ALU.min, nmax[:, 2 * j + t:2 * j + t + 1])
                ins.then_inc(sem("scores_read"), 1)

            def factor(j):
                kind, h = JOBS[j][0], JOBS[j][5]
                if kind != "dil":
                    dve.wait_ge(sem("att_exp"), 2 * j + 2)
                    fj = fac[:, 2 * j:2 * j + 2]
                    if kind == "fox":
                        nc.vector.reciprocal(fj, lsum[:, 2 * j:2 * j + 2]).then_inc(sem("fac_ready"), 1)
                        return
                    own(nc.vector.reciprocal(fj, lsum[:, 2 * j:2 * j + 2]))
                    settled()
                    TTn(fj, fj, gates3[:, :, h, 1 if kind == "sel" else 2], ALU.mult)\
                        .then_inc(sem("fac_ready"), 1)
                elif j in (6, 9):
                    a = 2 * (j - 2)
                    nm = cols2(nmax[:, a:a + 6], 3)
                    dve.wait_ge(sem("scores_read"), j + 1)
                    own(TTn(dil[:, 6:8], nm[:, 0, :], nm[:, 1, :], ALU.min))
                    settled()
                    own(TTn(dil[:, 6:8], dil[:, 6:8], nm[:, 2, :], ALU.min))
                    settled()
                    n = (j - 6) // 3
                    TTn(cols2(dil[:, 0:6], 3), dil[:, 6:8].unsqueeze(1).broadcast_to([P, 3, 2]), nm,
                        ALU.subtract).then_inc(sem("dil_diff"), 1)
                    dve.wait_ge(sem("dil_exp"), n + 1)
                    dve.wait_ge(sem("att_exp"), 2 * j + 2)
                    own(TTn(dil[:, 8:14], dil[:, 0:6], lsum[:, a:a + 6], ALU.mult))
                    settled()
                    own(TTn(dil[:, 14:16], dil[:, 8:10], dil[:, 10:12], ALU.add))
                    settled()
                    own(TTn(dil[:, 14:16], dil[:, 14:16], dil[:, 12:14], ALU.add))
                    settled()
                    own(nc.vector.reciprocal(dil[:, 16:18], dil[:, 14:16]))
                    settled()
                    TTn(cols2(fac[:, a:a + 6], 3), cols2(dil[:, 0:6], 3),
                        dil[:, 16:18].unsqueeze(1).broadcast_to([P, 3, 2]), ALU.mult)\
                        .then_inc(sem("fac_ready"), 1)

            for j in range(NJ + PV_LAG):
                if j < NJ:
                    scores_in(j)
                if 1 <= j <= NJ and JOBS[j - 1][0] != "dil":
                    factor(j - 1)
                if j in (6, 9):
                    factor(j)
                for bank, tiles, last in COPIES:
                    if last == j - PV_LAG:
                        dve.wait_ge(sem("pv_done"), last + 1)
                        n = len(tiles)
                        nc.vector.tensor_copy(Y[:, tiles[0]:tiles[0] + n, :],
                                              cols2(PS[:, AV[bank], 0:n * S], n)).then_inc(sem("y_copied"), 1)

            for i in range(8):
                if i % 2:
                    dve.wait_ge(*done(FIRST["w_p"] + i // 2))
                else:
                    dve.wait_ge(sem("w_p_even"), i // 2 + 1)
                b = 2 + 2 * (i % 2)
                if i < 2:
                    for q in (10, 11):
                        dve.wait_ge(*read(FIRST["gates"] + q))
                srcs = (PS[:, b, 0:S], PS[:, b, S:2 * S], PS[:, b + 1, 0:S])
                dsts = (T1[:, i % 2, 0:S], T1[:, i % 2, S:2 * S], T2[:, i % 2, 0:S])
                for q in range(3):
                    own(STT(dsts[q], BIG[:, 8 * q + i, :], 1.0, srcs[q], ALU.add, ALU.mult))
                settled()
                own(TTn(dsts[0], dsts[0], dsts[1], ALU.add))
                settled()
                TTn(Y[:, 8 + i, :], dsts[0], dsts[2], ALU.add).then_inc(sem("merged"), 1)
            for i in range(4):
                u = FIRST["w_o"] + i
                dve.wait_ge(*done(u))
                q = slice(i * 256, (i + 1) * 256)
                freed(STT(xb[:, :, q], cols2(bank_of(u)), 0.5, xa[:, :, q], ALU.mult, ALU.add), u)
            for i in range(2):
                dve.wait_ge(*read(FIRST["w_o"] + 2 + i))
            rows_scale(1, xb)
            turned_evac(1, "g2")
            for i in range(NF):
                u = FIRST["up"] + i
                dve.wait_ge(sem("ffn_tap"), i + 1)
                a, cv = bank_of(u)[:, 0:S], T2[:, i % 2, 0:S]
                own(STT(cv[:, 1:S], a[:, 0:S - 1], v("conv_w", NF + i), cv[:, 1:S], ALU.mult, ALU.add))
                settled()
                STT(cv[:, 2:S], a[:, 0:S - 2], v("conv_w", i), cv[:, 2:S], ALU.mult, ALU.add)\
                    .then_inc(sem("ffn_conv"), 1)
                dve.wait_ge(sem("ffn_gelu"), i + 1)
                freed(TTn(BIG[:, i, :], T2[:, i % 2, S:2 * S], bank_of(u)[:, S:2 * S], ALU.mult), u)

            dve.wait_ge(sem("positions_in"), 16)
            own(nc.vector.tensor_copy(ropes[4], ropes[5].bitcast(I32)))
            settled()
            own(TS(ropes[2], ropes[4], c("inv_freq"), None, ALU.mult))
            settled()
            own(TS(ropes[3], ropes[2], 1 / (2 * np.pi), 0.25, ALU.mult, ALU.add))
            own(TS(ropes[4], ropes[2], 1 / (2 * np.pi), MAGIC, ALU.mult, ALU.add))
            settled()
            own(TS(ropes[3], ropes[3], MAGIC, MAGIC, ALU.add, ALU.subtract))
            own(TS(ropes[4], ropes[4], MAGIC, None, ALU.subtract))
            settled()
            for part in range(3):
                for q in range(2):
                    src = ropes[2] if part == 0 else ropes[q]
                    own(STT(ropes[q], ropes[3 + q], -TURN[part], src, ALU.mult, ALU.add))
                settled()
            own(TS(ropes[0], ropes[0], float(np.pi / 2), PI_IN, ALU.add, ALU.min))
            own(TS(ropes[1], ropes[1], -PI_IN, PI_IN, ALU.max, ALU.min))
            settled()
            TS(ropes[0], ropes[0], -PI_IN, None, ALU.max).then_inc(sem("angles"), 1)

            dve.wait_ge(*done(FIRST["down"] + 10))
            for t in range(TT):
                TTn(cols2(xa[:, t, :]), PS[:, DEEP + 2 * t:DEEP + 2 * t + 2, :], cols2(xb[:, t, :]), ALU.add)\
                    .then_inc(sem("x2_ready"), 1)
            dve.wait_ge(sem("gains_in"), 16)
            dve.wait_ge(sem("x2_ready"), TT)
            for t in range(TT):
                q = row_rstd(2, t)
                STT(xb[:, t, :], xa[:, t, :], q, gB[:, :], ALU.mult, ALU.mult).then_inc(sem("x3_ready"), 1)
            dve.wait_ge(sem("x3_ready"), TT)
            rows_scale(3, xb)

            turned_evac(2, "g3")
            dve.wait_ge(sem("small_done"), 2)
            own(TTn(gt2, cols2(PS[:, SC[0], 0:128])[:, :, 0:16],
                    r("b_gate").unsqueeze(1).broadcast_to([P, TT, 16]), ALU.add))
            settled()
            for d in range(2):
                f = gt2[:, :, 4 + 8 * d:8 + 8 * d]
                STT(lfx[:, :, 4 * d:4 * d + 4], f, -1.0, f, ALU.mult, ALU.max).then_inc(sem("lstm_logs"), 1)
            dve.wait_ge(sem("lstm_exp"), 2)
            for d in range(2):
                f = gt2[:, :, 4 + 8 * d:8 + 8 * d]
                STT(lf2[:, :, 4 * d:4 * d + 4], f, 0.0, lfx[:, :, 4 * d:4 * d + 4], ALU.min, ALU.subtract)\
                    .then_inc(sem("lstm_logs"), 1)

            def conv_in(i):
                u = FIRST["conv_in"] + i
                dve.wait_ge(sem("a_gate"), i + 1)
                freed(STT(UP[:, i, 15:15 + S], T1[:, i % 2, 0:S], 1.0, bank_of(u)[:, 0:S], ALU.add, ALU.mult), u)

            def taps(group, a, b):
                for k in range(a, b):
                    for j in range(4):
                        i = 4 * group + j
                        src, acc, wk = UP[:, i, k:k + S], BIG[:, 16 + i, :], v("taps", i * 31 + k)
                        if k == 0:
                            ins = TS(acc, src, wk, None, ALU.mult)
                        else:
                            dve.wait_ge(sem("conv_tap"), 124 * group + 4 * (k - 1) + j + 1)
                            ins = STT(acc, src, wk, acc, ALU.mult, ALU.add)
                        ins.then_inc(sem("conv_tap"), 1)

            dve.wait_ge(sem("conv_pads"), 2)
            for i in range(4):
                conv_in(i)
            dve.wait_ge(*read(FIRST["conv_in"] + 2))
            dve.wait_ge(*read(FIRST["conv_in"] + 3))
            for i in range(4):
                conv_in(4 + i)
                taps(0, 5 * i, 5 * i + 5)
            dve.wait_ge(*read(FIRST["conv_in"] + 6))
            dve.wait_ge(*read(FIRST["conv_in"] + 7))
            taps(0, 20, 31)
            taps(1, 0, 31)
            dve.wait_ge(sem("conv_tap"), 248)

            for kind, n in EVEN_STEPS:
                if kind == "scores":
                    dve.wait_ge(sem("lstm_decay"), n + 1)
                    for i, (a, b) in enumerate(LSTM_COLS):
                        d, t = i // 2, i % 2
                        tab = c("causal", P if t == 0 else 0, S) if d == 0 else c("anti", 0, S if t == 0 else P)
                        nc.vector.tensor_tensor_reduce(
                            EB[:, n % 2, i, a:b], PS[:, SC[0], d * S + a:d * S + b], tab, -1.0, 0.0, ALU.add,
                            ALU.min, nM[:, 4 * n + i:4 * n + i + 1]).then_inc(sem("lstm_decay_read"), 1)
                    dve.wait_ge(sem("lstm_decay_read"), 4 * n + 4)
                    dve.wait_ge(sem("lstm_rows_copied"), 2)
                    q = slice(4 * n, 4 * n + 4)
                    TTn(floor[:, q], nF.rearrange("p (i h) -> p i h", h=4)[:, :, n], nM[:, q], ALU.add)\
                        .then_inc(sem("lstm_arg"), 1)
                    dve.wait_ge(sem("lstm_scores"), n + 1)
                    for i, (a, b) in enumerate(LSTM_COLS):
                        dve.wait_ge(sem("lstm_dw"), 4 * n + i + 1)
                        t = i % 2
                        nc.vector.tensor_tensor_reduce(
                            EB[:, n % 2, i, a:b], PS[:, SC[1], t * S + a:t * S + b], EB[:, n % 2, i, a:b],
                            P ** -0.5, 0.0, ALU.mult, ALU.add, den[:, 4 * n + i:4 * n + i + 1])\
                            .then_inc(sem("lstm_scores_read"), 1)
                    dve.wait_ge(sem("lstm_scores_read"), 4 * n + 4)
                    own(STT(den2[:, q], den[:, q], -1.0, den[:, q], ALU.mult, ALU.max))
                    settled()
                    dve.wait_ge(sem("lstm_floor"), n + 1)
                    own(TTn(den2[:, q], den2[:, q], floor[:, q], ALU.max))
                    settled()
                    own(nc.vector.reciprocal(den2[:, q], den2[:, q]))
                    settled()
                    w_, eb = WM[:, n % 2, :], EB[:, n % 2]
                    k = 4 * n
                    own(TS(w_[:, 0:S], eb[:, 2, 0:S], den2[:, k + 2:k + 3], None, ALU.mult))
                    own(TS(w_[:, S:2 * S], eb[:, 1, 0:S], den2[:, k + 1:k + 2], None, ALU.mult))
                    settled()
                    STT(w_[:, 0:P], eb[:, 0, 0:P], den2[:, k:k + 1], w_[:, 0:P], ALU.mult, ALU.add)
                    STT(w_[:, S + P:2 * S], eb[:, 3, P:S], den2[:, k + 3:k + 4], w_[:, S + P:2 * S], ALU.mult,
                        ALU.add).then_inc(sem("lstm_w"), 1)
                elif kind == "z_b":
                    u = FIRST["z_b"] + n
                    dve.wait_ge(sem("zb_tanh"), n + 1)
                    freed(STT(T1[:, 1, :], T1[:, 1, :], 1.0, bank_of(u), ALU.add, ALU.mult), u)
                    dve.wait_ge(*read(u))
                    oz = BIG[:, 8 + 2 * n:10 + 2 * n, :]
                    dve.wait_ge(*read(FIRST["o"] + n))
                    STT(oz, oz, 1.0, cols2(T1[:, 1, :]), ALU.add, ALU.mult).then_inc(sem("oz_ready"), 1)
                elif kind == "var":
                    dve.wait_ge(sem("lstm_rs"), 2 * n + 2)
                    dve.wait_ge(sem("oz_ready"), n + 1)
                    for e in range(2):
                        own(STT(Y[:, 8 + 2 * n + e, :], PS[:, AV[0], e * S:(e + 1) * S], v("hn_g", 2 * n + e),
                                BIG[:, 8 + 2 * n + e, :], ALU.mult, ALU.mult))
                    settled()
                    y = Y[:, 8 + 2 * n:10 + 2 * n, :]
                    STT(y, y, 0.25, RSH.unsqueeze(1).broadcast_to([P, 2, S]), ALU.mult, ALU.mult)\
                        .then_inc(sem("yb_done"), 1)
                elif kind == "gn":
                    for e in range(2):
                        ins = TS(GNU[:, n % 2, e * S:(e + 1) * S], BIG[:, 16 + 2 * n + e, :], 0.5,
                                 v("tap_b", 2 * n + e), ALU.mult, ALU.add)
                    ins.then_inc(sem("gn_u"), 1)
                    dve.wait_ge(sem("gn_u"), n + 1)
                    dve.wait_ge(sem("gn_mean"), n + 1)
                    TTn(XC, GNU[:, n % 2, :], PS[:, PT[1], :], ALU.subtract).then_inc(sem("gn_xc"), 1)
                elif kind == "gn_var":
                    dve.wait_ge(sem("gn_rs"), 2 * n + 2)
                    own(TTn(XC, XC, RSG, ALU.mult))
                    settled()
                    for e in range(2):
                        q = XC[:, e * S:(e + 1) * S]
                        ins = TS(q, q, v("gn_g", 2 * n + e), v("gn_b", 2 * n + e), ALU.mult, ALU.add)
                    ins.then_inc(sem("gn_xg"), 1)
                    dve.wait_ge(sem("gn_tanh"), n + 1)
                    own(STT(T2[:, 1, :], T2[:, 1, :], 1.0, XC, ALU.add, ALU.mult))
                    settled()
                    STT(Y[:, 2 * n:2 * n + 2, :], cols2(T2[:, 1, :]), 0.5, BIG[:, 2 * n:2 * n + 2, :], ALU.mult,
                        ALU.mult).then_inc(sem("gn_done"), 1)

            def post_norm(m, base, dst, name):
                dve.wait_ge(sem("gains_in"), 32 if m == 4 else 48)
                for t in range(TT):
                    q = row_rstd(m, t)
                    own(STT(cols2(xh[:, t, :]), PS[:, DEEP + 2 * t:DEEP + 2 * t + 2, :], q, cols2(gB[:, :]),
                            ALU.mult, ALU.mult))
                    settled()
                    TTn(dst[:, t, :], xh[:, t, :], base[:, t, :], ALU.add).then_inc(sem(name), 1)

            post_norm(4, xb, xa, "x4_ready")
            dve.wait_ge(sem("x4_ready"), TT)
            rows_scale(5, xa)

            turned_evac(3, "g4")
            dve.wait_ge(sem("lora_rs"), 2)
            for k in range(5):
                STT(CQ[:, k, :], LQ[:, k, :], v("g_q", k) if k < 3 else v("g_kv", k - 3),
                    RSL[:, 0:S] if k < 3 else RSL[:, S:2 * S], ALU.mult, ALU.mult).then_inc(sem("lora_ready"), 1)

            def rotate(n, src):
                tiles = 2 if n < 2 else 1
                dve.wait_ge(sem("rope_tables"), 2)
                if n < 2:
                    dve.wait_ge(sem(f"uq_read[{n}]"), 3)
                dve.wait_ge(sem("rope_swapped"), n + 1)
                a, b = T2[:, 0, 0:tiles * S], T2[:, 1, 0:tiles * S]
                if n:
                    dve.wait_ge(sem("rope_ready"), n)
                own(TTn(cols2(a, tiles), src, ropes[0].unsqueeze(1).broadcast_to([P, tiles, S]), ALU.mult))
                TTn(cols2(b, tiles), cols2(PS[:, SC[1], 0:tiles * S], tiles),
                    ropes[1].unsqueeze(1).broadcast_to([P, tiles, S]), ALU.mult)\
                    .then_inc(sem("rope_swapped_read"), 1)
                settled()
                dve.wait_ge(sem("rope_swapped_read"), n + 1)
                TTn(src, cols2(a, tiles), cols2(b, tiles), ALU.add).then_inc(sem("rope_ready"), 1)

            for n in range(1, 14, 2):
                name, value = UQ_DONE[n]
                dve.wait_ge(sem(name), value)
                nc.vector.tensor_copy(uq_dest(n), cols2(PS[:, PT[1], :]) if n < 10 else PS[:, PT[1], :])\
                    .then_inc(sem("uq_read[1]"), 1)
                if n == 5:
                    rotate(0, QR[:, 0:2, :])
                if n == 9:
                    rotate(1, QR[:, 2:4, :])
                    rotate(2, KR[:, :, :])

            for i in range(8 + 3):
                if i < 8:
                    dve.wait_ge(sem("mla_scores"), i + 1)
                    q = mmax[:, 2 * i:2 * i + 2]
                    own(nc.vector.tensor_reduce(q, cols2(PS[:, SC[i % 2], :]), AX.X, ALU.max))
                    settled()
                    TS(q, q, -MLA_SCALE, None, ALU.mult).then_inc(sem("mla_max"), 1)
                if i < 6:
                    u = (FIRST["z_c"] if i < 4 else FIRST["z_d"] - 4) + i
                    dve.wait_ge(sem("zcd_tanh"), i + 1)
                    o = ZC[:, 2 * i:2 * i + 2, :] if i < 4 else ZD[:, 2 * i - 8:2 * i - 6, :]
                    freed(STT(o, cols2(T1[:, i % 2, :]), 1.0, cols2(bank_of(u)), ALU.add, ALU.mult), u)
                if 1 <= i < 9:
                    h = i - 1
                    dve.wait_ge(sem("mla_probs"), 2 * h + 2)
                    q = msum[:, 2 * h:2 * h + 2]
                    nc.vector.reciprocal(q, q).then_inc(sem("mla_rec"), 1)
                if i >= 3:
                    h = i - 3
                    dve.wait_ge(sem("mla_out"), h + 1)
                    if h % 2 == 0:
                        dve.wait_ge(*read(FIRST["z_c"] + h // 2))
                    STT(Y[:, h, :], PS[:, AV[h % 2], 0:S], 0.5, ZC[:, h, :], ALU.mult, ALU.mult)\
                        .then_inc(sem("yc_done"), 1)
            for m in range(2):
                dve.wait_ge(sem("fft2"), m + 1)
                nc.vector.tensor_copy(F2[:, 2 * m:2 * m + 2, :], cols2(PS[:, PT[m], :]))\
                    .then_inc(sem("fft2_copied"), 1)
            dve.wait_ge(*done(FIRST["w_fd"]))
            for m in range(2):
                dve.wait_ge(*read(FIRST["z_d"] + m))
                STT(Y[:, 8 + 2 * m:10 + 2 * m, :], cols2(PS[:, AV[m], :]), 0.5, ZD[:, 2 * m:2 * m + 2, :],
                    ALU.mult, ALU.mult).then_inc(sem("yd_done"), 1)
            post_norm(6, xa, xb, "out_ready")

        @block.gpsimd
        def _(pool):
            nc.gpsimd.memset(CM, 0.0).then_inc(sem("cm_zero"), 1)
            nc.gpsimd.memset(UP[:, :, 0:15], 0.0).then_inc(sem("conv_pads"), 1)
            nc.gpsimd.memset(UP[:, :, 15 + S:286], 0.0).then_inc(sem("conv_pads"), 1)
            for j in range(NJ):
                pool.wait_ge(sem("fac_ready"), FAC[j])
                for t in range(TT):
                    q = PB[:, j % 8, 0:P] if t == 0 else PB[:, j % 8, P:3 * P]
                    ins = nc.gpsimd.tensor_scalar(q, q, fac[:, 2 * j + t:2 * j + t + 1], None, ALU.mult)
                ins.then_inc(sem("probs_scaled"), 1)
            for h in range(8):
                pool.wait_ge(sem("mla_rec"), h + 1)
                for t in range(TT):
                    q = MP[:, h % 4, t * S:(t + 1) * S]
                    ins = nc.gpsimd.tensor_scalar(q, q, msum[:, 2 * h + t:2 * h + t + 1], None, ALU.mult)
                ins.then_inc(sem("mla_scaled"), 1)


def slope(i):
    return np.exp2(-8.0 * i / 12)


def constant_tables():
    p = np.arange(P)[:, None]
    s = np.arange(S)[None, :]
    masked = np.float64(MASKED)
    out = np.zeros((P, NC_), np.float32)
    late = np.zeros((P, NL_), np.float32)

    def put(name, a):
        o, n = C_AT[name]
        out[:, o:o + n] = np.asarray(a, np.float64).reshape(P, n)

    put("ident", np.eye(P))
    put("mean", np.concatenate([np.full((P, P), 1.0 / n) for n in (128, 256, 384)], 1))
    put("neg_upper", np.concatenate([-1.0 * (p + t * P <= s) for t in range(TT)], 1))
    put("neg_lower", np.concatenate([-1.0 * (p + t * P >= s) for t in range(TT)], 1))
    dist = p + P - s
    causal = np.where(dist >= 0, 0.0, masked)
    put("causal", causal)
    put("anti", np.where(s >= p, 0.0, masked))
    dil = []
    for g, (w, rate) in enumerate(((128, 1), (512, 4), (2048, 16))):
        for h in range(2):
            ok = (dist >= 0) & (dist <= w) & (dist % rate == 0)
            dil.append(np.where(ok, -8.0 * slope(2 * (2 * g + h) + 1) * dist, masked))
    put("dil_bias", np.concatenate(dil, 1))
    put("nsa_bias", np.concatenate([np.where(dist >= 0, -8.0 * slope(2 * h + 2) * dist, masked)
                                    for h in range(6)], 1))
    bias, mask = np.zeros((P, 2, TT, 3, 32)), np.zeros((P, 2, TT, 3, 32))
    end = np.arange(15) * 16 + 31
    for g in range(2):
        for t in range(TT):
            for h in range(3):
                far = p + t * P - end[None, :]
                bias[:, g, t, h, :15] = np.where(far >= 0, -slope(2 * (3 * g + h) + 2) * far, masked)
                mask[:, g, t, h, :15] = far >= 0
    put("cmp_bias", bias)
    put("cmp_mask", mask)
    rows = np.zeros((P, 4, P))
    for h in range(4):
        rows[h, h], rows[64 + h, h] = 1.0, 1.0
    put("rows", rows)
    inv = (10000.0 ** (-np.arange(0, 64, 2, dtype=np.float32) / np.float32(64))).astype(np.float32)
    put("inv_freq", np.tile(inv, 4)[:, None])

    def put_late(name, a):
        o, n = L_AT[name]
        late[:, o:o + n] = np.asarray(a, np.float64).reshape(P, n)

    ch = 2 * np.pi * ((np.arange(P)[:, None] * np.arange(P)[None, :]) % P) / P
    put_late("dft_ch", np.concatenate([np.cos(ch), np.sin(ch)], 1) / np.sqrt(P))
    tk = 2 * np.pi * ((np.arange(S)[:, None] * np.arange(S)[None, :]) % S) / S
    put_late("dft_cos", np.concatenate([np.cos(tk)[t * P:(t + 1) * P] for t in range(TT)], 1) / np.sqrt(S))
    put_late("dft_nsin", np.concatenate([-np.sin(tk)[t * P:(t + 1) * P] for t in range(TT)], 1) / np.sqrt(S))
    swap = np.zeros((P, P))
    for m in range(P):
        if m % 64 < 32:
            swap[m + 32, m] = -1.0
        else:
            swap[m - 32, m] = 1.0
    put_late("rope_swap", swap)
    return out, late


def wide(w, k):
    n = w.shape[1] // 256
    return w.reshape(k, P, n, 256).transpose(2, 1, 0, 3).reshape(n, P, k * 256)


def deep_units(w):
    n = w.shape[0] // 256
    return w.reshape(n, 2, P, D).transpose(0, 2, 1, 3).reshape(n, P, 2 * D)


def packed(w, k, tiles):
    a = w.reshape(k, P, tiles, P).transpose(1, 2, 0, 3).reshape(P, tiles * k * P)
    out = np.zeros((1, P, UNIT), np.float32)
    out[0, :, :a.shape[1]] = a
    return out


def columns(v, n):
    return v.reshape(n, P).T


def kernel(**inputs):
    import concourse.bacc as bacc
    from concourse.bass_utils import run_bass_kernel_spmd

    a = {k: np.asarray(q) for k, q in inputs.items()}
    w_in, b_in = a["w_in"][0], a["b_in"][0]
    at = np.cumsum([0, 256, 256, 256, 4, 384, 384, 384, 384, 128, 128, 128, 128, 128, 128, 18, 3072])
    (qa, ka, va, fa, qb, kb, vb, qc, kc, vcm, ks, vs, kw, vw, gc, gates) = (
        np.arange(i, j) for i, j in zip(at[:-1], at[1:]))
    qc = np.concatenate([qc[h * DH:(h + 1) * DH] for i in range(3) for h in (i, i + 3)])
    cols = [qa, ka]
    for g in range(3):
        cols += [qb[g * P:(g + 1) * P], kb[g * P:(g + 1) * P]]
    cols += [qc, ks, kw, kc]
    feat = np.concatenate(cols)
    vcols = np.concatenate([va, vb, vs, vw])
    order = np.concatenate([feat, vcols, vcm])
    w_pc = np.concatenate([a["w_pc"][0][h * DH:(h + 1) * DH] for i in range(3) for h in (i, i + 3)])
    up = a["w_up"][0].reshape(D, 2, NF, P).transpose(0, 2, 1, 3).reshape(D, 2 * DFF)
    ew = a["even_w_in_2"][0]
    e_at = np.cumsum([0, 1024, 1024, 1024, 512, 512, 1024, 1024, 1024, 16])
    a_val, a_gate, z_a, eq, ek, ev, eo, z_b, eg = (ew[:, i:j] for i, j in zip(e_at[:-1], e_at[1:]))

    def pair(x_, y_, n):
        return np.stack([x_.reshape(D, n, P), y_.reshape(D, n, P)], 2).reshape(D, 2 * n * P)

    ow = a["odd_w_in_2"][0]
    o_at = np.cumsum([0, 384, 256, 64, 512, 1024, 512])
    cq, ckv, kr, f_in, z_c, z_d = (ow[:, i:j] for i, j in zip(o_at[:-1], o_at[1:]))
    uq = a["odd_w_uq_2"][0].reshape(384, 8, 192)
    uq = np.concatenate([uq[:, :, :128].reshape(384, 1024), uq[:, :, 128:].reshape(384, 512)], 1)
    ukv = a["odd_w_ukv_2"][0].reshape(256, 8, 256)
    units = {
        "proj": wide(w_in[:, order], KD), "gates": wide(w_in[:, gates], KD),
        "cmp": np.concatenate([a[n][0].reshape(2, 8, P, 256).transpose(0, 2, 1, 3).reshape(2, P, UNIT)
                               for n in ("cmp_k_w1", "cmp_v_w1")]),
        "w_p": wide(np.concatenate([a["w_pa"][0], a["w_pb"][0], w_pc]), KD),
        "w_o": wide(a["w_o"][0], KD), "up": wide(up, KD), "down": deep_units(a["w_down"][0]),
        "conv_in": wide(pair(a_val, a_gate, 8), KD), "z_a": wide(z_a, KD), "qk": wide(pair(eq, ek, 4), KD),
        "v": wide(ev, KD), "o": wide(eo, KD), "z_b": wide(z_b, KD),
        "even_out": deep_units(a["even_w_out_2"][0]),
        "lora": wide(np.concatenate([cq, ckv, kr, kr], 1), KD), "f_in": wide(f_in, KD),
        "w_uq": np.concatenate([packed(uq[:, i * 512:(i + 1) * 512], 3, 4) for i in range(3)]),
        "w_uk": packed(ukv[:, :, :128].reshape(256, 1024), 2, 8),
        "w_uv": deep_units(ukv[:, :, 128:].reshape(256, 1024)),
        "z_c": wide(z_c, KD), "z_d": wide(z_d, KD),
        "w_fd": a["odd_w_fd_2"][0].reshape(1, 4, P, 512).transpose(0, 2, 1, 3).reshape(1, P, UNIT),
        "odd_out": deep_units(a["odd_w_out_2"][0]),
    }
    w = np.concatenate([units[name] for name, n in STREAM])
    small = np.concatenate([w_in[:, fa], w_in[:, gc], eg], 1)
    w_small = small.reshape(KD, P, 38).transpose(1, 0, 2)
    cmp_w2 = np.stack([a[n][0].reshape(2, P, DH).transpose(1, 0, 2) for n in ("cmp_k_w2", "cmp_v_w2")], 1)

    vecs = np.zeros((P, NV_), np.float32)

    def put(name, x_):
        o, n = V_AT[name]
        vecs[:, o:o + x_.shape[1]] = x_

    put("g1", columns(a["norm1_g"][0], 8))
    put("b_feat", columns(np.concatenate([b_in[feat], b_in[vcm]]), 17))
    put("b_gates", columns(b_in[gates], 24))
    put("pe", a["cmp_pe"][0].reshape(16, P).T)
    put("g2", columns(a["norm2_g"][0], 8))
    put("conv_w", columns(a["conv_w"][0].reshape(-1), 66))
    put("conv_b", columns(a["conv_b"][0], 22))
    put("g3", columns(a["even_g_pre_2"][0], 8))
    put("taps", a["even_conv_w_2"][0].reshape(31, 8, P).transpose(2, 1, 0).reshape(P, 248))
    put("tap_b", columns(a["even_conv_b_2"][0], 8))
    put("gn_g", columns(a["even_gn_g_2"][0], 8))
    put("gn_b", columns(a["even_gn_b_2"][0], 8))
    put("hn_g", columns(a["even_hn_g_2"][0], 8))
    put("g4", columns(a["odd_g_pre_2"][0], 8))
    put("g_q", columns(a["odd_g_q_2"][0], 3))
    put("g_kv", columns(a["odd_g_kv_2"][0], 2))
    rows = np.concatenate([b_in[vcols], b_in[fa], b_in[gc], a["even_b_gate_2"][0]])[None, :]
    gains = np.stack([a["final_g"], a["even_g_post_2"][0], a["odd_g_post_2"][0]])
    consts, late = constant_tables()
    arrays = {"w": w, "w_small": w_small, "consts": consts, "late": late, "vecs": vecs, "rows": rows,
              "gains": gains, "x": a["x"][0].reshape(TT, P, D).transpose(1, 0, 2),
              "positions": a["positions_2"].astype(np.int32), "cmp_w2": cmp_w2}
    arrays = {k: np.ascontiguousarray(q) for k, q in arrays.items()}
    nc = bacc.Bacc("TRN2", target_bir_lowering=False, num_devices=1)
    args = {k: nc.dram_tensor(k, q.shape, mybir.dt.from_np(q.dtype), kind="ExternalInput").ap()
            for k, q in arrays.items()}
    out = nc.dram_tensor("out", (S, D), F32, kind="ExternalOutput").ap()
    program(nc, out=out, **args)
    r = run_bass_kernel_spmd(nc, [arrays], core_ids=[0])
    return r.results[0]["out"].reshape(1, S, D)
```

```python
from contextlib import ExitStack

import numpy as np

import concourse.bass as bass
from concourse import mybir

P = 128
S = 256
TT = S // P
D = 1024
KD = D // P
DFF = 2816
NF = DFF // P
DH = 64
EPS, LN_EPS = 1e-6, 1e-5
MASKED = -1e30
RING = 3
SPLITS = 3
HALF = 1024
UNIT = 2048
MLA_SCALE = 192 ** -0.5
TURN = (6.28125, 0.0019350051879882812, 3.0199159795074593e-07)
MAGIC = 1.5 * 2.0 ** 23
PI_IN = 3.1415925
LSTM_COLS = ((0, P), (0, S), (0, S), (P, S))

F32 = mybir.dt.float32
F32R = mybir.dt.float32r
I32 = mybir.dt.int32
ALU = mybir.AluOpType
ACT = mybir.ActivationFunctionType
AX = mybir.AxisListType

CONST = dict(ident=128, mean=3 * 128, neg_upper=2 * 256, neg_lower=2 * 256, causal=256, anti=256,
             dil_bias=6 * 256, nsa_bias=6 * 256, cmp_bias=12 * 32, cmp_mask=12 * 32, rows=4 * 128,
             inv_freq=1)
LATE = dict(dft_ch=256, dft_cos=2 * 256, dft_nsin=2 * 256, rope_swap=128)
VECS = dict(g1=8, b_feat=18, b_gates=24, pe=16, g2=8, conv_w=66, conv_b=22, g3=8, taps=8 * 31,
            tap_b=8, gn_g=8, gn_b=8, hn_g=8, g4=8, g_q=3, g_kv=2)
ROWS = dict(b_v=896, b_small=22, b_gate=16)


def offsets(table):
    at, out = 0, {}
    for name, n in table.items():
        out[name] = (at, n)
        at += n
    return out, at


C_AT, NC_ = offsets(CONST)
V_AT, NV_ = offsets(VECS)
R_AT, NR_ = offsets(ROWS)
L_AT, NL_ = offsets(LATE)
assert NL_ <= CONST["dil_bias"]
for _name, (_o, _n) in L_AT.items():
    C_AT[_name] = (C_AT["dil_bias"][0] + _o, _n)

STREAM = [("proj", 12), ("cmp", 4), ("gates", 12), ("w_p", 4), ("w_o", 4), ("up", 22), ("down", 11),
          ("conv_in", 8), ("qk", 4), ("v", 4), ("z_a", 4), ("o", 4), ("z_b", 4), ("even_out", 8),
          ("lora", 3), ("f_in", 2), ("z_c", 4), ("z_d", 2), ("w_uq", 3), ("w_uk", 1), ("w_uv", 1),
          ("w_fd", 1), ("odd_out", 6)]
FIRST, NU = {}, 0
for _name, _n in STREAM:
    FIRST[_name] = NU
    NU += _n

CMP0, CMP1 = FIRST["cmp"], FIRST["cmp"] + 4


def half_at(u):
    return 2 * (u if u < CMP0 else u - 4)


def half_of(name):
    return half_at(FIRST[name])


def unit_of(q):
    return q // 2 if q // 2 < CMP0 else q // 2 + 4


HALVES = half_at(NU)

JOBS = [("fox", h // 2, h % 2, 2 + h // 2, h * DH, h) for h in range(4)]
JOBS += [("dil", 4 + 2 * g, h, 5 + 2 * g, 256 + (2 * g + h) * DH, 2 * g + h)
         for h in range(2) for g in range(3)]
for _i in range(3):
    for _h in (_i, _i + 3):
        _g = _h // 3
        JOBS.append(("sel", 10 + _i, _g, 13, 640 + _g * DH, _h))
        JOBS.append(("win", 10 + _i, _g, 14, 768 + _g * DH, _h))
NJ = len(JOBS)
PT_LAG, PV_LAG = 4, 5
Y_TILE = [h // 2 if k == "fox" else 2 + h // 2 if k == "dil" else 5 + h % 3
          for k, _, _, _, _, h in JOBS]
Y_PLACE = {0: (0, 0, 0), 1: (0, 1, 0), 2: (1, 0, 0), 3: (1, 1, 0), 4: (0, 0, 1), 5: (1, 0, 2),
           6: (0, 0, 3), 7: (1, 0, 4)}
COPIES = [(0, (0, 1), 3), (1, (2, 3), 9), (0, (4,), 9), (1, (5,), 13), (0, (6,), 17), (1, (7,), 21)]
Y_SPLIT_AT = {NJ: (0, 1, 2, 3), NJ + 1: (4,), NJ + PV_LAG - 1: (5,)}
FAC = [j + 1 if j < 4 else 5 + (j - 4) // 3 if j < 10 else j - 3 for j in range(NJ)]

EVEN_STEPS = []
for _h in range(4):
    EVEN_STEPS += [("scores", _h)]
    if _h:
        EVEN_STEPS += [("pv", _h - 1), ("var", _h - 1)]
    EVEN_STEPS += [("gn", _h), ("z_b", _h), ("gn_var", _h), ("turn", _h)]
EVEN_STEPS += [("pv", 3), ("var", 3)]

UQ_HALF = [half_of("w_uq") + n if n < 6 else half_of("w_uk") + (n - 6) // 2 for n in range(14)]
UQ_DONE = [("uq_part", (n - 4) // 2) if n >= 6 and n % 2 == 0 else ("half_used", UQ_HALF[n] + 1)
           for n in range(14)]

DOWN = [k for k in range(NF)]
EVEN_OUT = [k for k in range(16)]
ODD_OUT = [8, 9, 10, 11, 0, 1, 2, 3, 4, 5, 6, 7]
DEEP0 = {"down": 0, "even_out": NF, "odd_out": NF + 16}
CONV_POOL = 2
CONV_W = S + 30
CONV_DVE = ((2, 3, 4), (5, 6, 7))


def gn_pair(n):
    return (n + 1) % 4


def program(nc, w, w_small, consts, late, vecs, rows, gains, x, positions, cmp_w2, out):
    ctx = ExitStack()
    with ctx:
        def sb(name, shape, dt=F32):
            return ctx.enter_context(nc.sbuf_tensor(name, shape, dt))

        sems = {}

        def sem(name):
            if name not in sems:
                sems[name] = ctx.enter_context(nc.semaphore(name.replace("[", "_").replace("]", "")))
            return sems[name]

        ring = sb("ring", [P, RING, UNIT])
        cn = sb("cn", [P, NC_])
        vc = sb("vc", [P, NV_])
        rw = sb("rw", [P, NR_ - ROWS["b_v"]])
        wh, wl = sb("wh", [P, SPLITS, HALF], F32R), sb("wl", [P, SPLITS, HALF], F32R)
        hh, hl = sb("hh", [P, KD, S], F32R), sb("hl", [P, KD, S], F32R)
        wsh, wsl = sb("wsh", [P, KD, 38], F32R), sb("wsl", [P, KD, 38], F32R)
        w2s = sb("w2s", [P, 2, 2, DH])
        xa = sb("xa", [P, TT, D])
        xb = sb("xb", [P, TT, D])
        BIG = sb("BIG", [P, 24, S])
        QK = sb("QK", [P, 16, S])
        V = sb("V", [P, TT, 1024])
        Y = sb("Y", [P, 16, S])
        PB = sb("PB", [P, 8, 384])
        SM = sb("SM", [P, 3, 512])
        PTS = sb("PTS", [P, 2, 512])
        T1 = sb("T1", [P, 2, 512])
        T2 = sb("T2", [P, 2, 512])
        stat = sb("stat", [P, 48])
        tiny = sb("tiny", [P, 640])
        eps_t = sb("eps_t", [P, 2])
        PS = ctx.enter_context(nc.psum_tensor("PS", [P, 8, 512], F32))

        def c(name, a=0, b=None):
            o, n = C_AT[name]
            return cn[:, o + a:o + (n if b is None else b)]

        b_v = BIG[:, 20:24, :].rearrange("p a b -> p (a b)")[:, 0:ROWS["b_v"]]

        def v(name, i=0, n=1):
            o, _ = V_AT[name]
            return vc[:, o + i:o + i + n]

        def r(name, a=0, b=None):
            o, n = R_AT[name]
            b = n if b is None else b
            return b_v[:, a:b] if name == "b_v" else rw[:, o - ROWS["b_v"] + a:o - ROWS["b_v"] + b]

        ident = c("ident")
        block = ctx.enter_context(nc.Block())
        G, SC, PT, AV, DEEP = (0, 1), (2, 3), (4, 5), (6, 7), 4

        ssq, rms = stat[:, 0:16], stat[:, 16:32]
        lsum, nmax, fac = tiny[:, 0:44], tiny[:, 44:88], tiny[:, 88:132]
        gnsa = tiny[:, 132:168]
        lfa = tiny[:, 168:192]
        small = tiny[:, 192:236].rearrange("p (t c) -> p t c", t=TT)
        gt2 = tiny[:, 236:268].rearrange("p (t c) -> p t c", t=TT)
        lf2 = tiny[:, 268:284].rearrange("p (t c) -> p t c", t=TT)
        lfx = tiny[:, 284:300].rearrange("p (t c) -> p t c", t=TT)
        half_b = tiny[:, 300:324]
        nF, nM, floor, den = (tiny[:, 324 + 16 * i:340 + 16 * i] for i in range(4))
        dil = tiny[:, 388:420]
        cst = tiny[:, 420:480]
        mmax, msum = tiny[:, 480:496], tiny[:, 496:512]
        den2 = tiny[:, 512:528]
        flat2 = PB[:, 0:3, :].rearrange("p a b -> p (a b)")[:, 0:960].rearrange(
            "p (i j c) -> p i j c", i=2, j=16)
        PBF = PB[:, :, :].rearrange("p a b -> p (a b)")
        YF = Y[:, :, :].rearrange("p a b -> p (a b)")
        xh = PBF[:, 0:TT * D].rearrange("p (t d) -> p t d", t=TT)
        gB = V[:, 0, :]
        wsm = T2[:, :, :].rearrange("p a b -> p (a b)")[:, 0:KD * 38]
        UP_DVE = YF[:, 0:6 * CONV_W].rearrange("p (i c) -> p i c", i=6)
        UP_POOL = xa[:, 0, 0:CONV_POOL * CONV_W].rearrange("p (i c) -> p i c", i=CONV_POOL)
        POOL_TMP = xa[:, 1, 0:CONV_POOL * S].rearrange("p (i c) -> p i c", i=CONV_POOL)
        CM = SM[:, 2, 0:384]
        cmpPT = T2[:, 0, :].rearrange("p (g q) -> p g q", g=2)
        CH = T2[:, 1, 0:128].rearrange("p (i k c) -> p i k c", i=2, k=2)
        cvv = T2[:, 1, 128:256]
        ckT = T2[:, 1, 256:272]
        foxr = T1[:, 0, 0:256]
        EB = PBF[:, 0:2048].rearrange("p (h i s) -> p h i s", h=2, i=4)
        WM = PBF[:, 2048:3072].rearrange("p (h s) -> p h s", h=2)
        GNU = SM[:, 0:2, :]
        erow = SM[:, 2, :]
        QKF = QK[:, :, :].rearrange("p a b -> p (a b)")
        RSH, RSG, XC = QKF[:, 2048:2304], QKF[:, 2560:3072], QKF[:, 3072:3584]
        QN, KN, ZC = BIG[:, 0:8, :], BIG[:, 8:16, :], BIG[:, 16:24, :]
        ZD, QR, LQ = QK[:, 0:4, :], QK[:, 4:8, :], QK[:, 8:14, :]
        KR = QK[:, 13:14, :]
        LS = PBF[:, 0:5 * S].rearrange("p (k q) -> p k q", k=5)
        RSL = T2[:, 0, :]
        MP = PBF[:, 0:2048].rearrange("p (h s) -> p h s", h=4)
        FT = Y[:, 12:16, :]
        F1 = Y[:, 0:8, :].rearrange("p (g a) q -> p g (a q)", g=4)
        _o = C_AT["nsa_bias"][0]
        ropes = [cn[:, _o + i * S:_o + (i + 1) * S] for i in range(6)]

        def up_in(i, a, b):
            return UP_POOL[:, i, a:b] if i < CONV_POOL else UP_DVE[:, i - CONV_POOL, a:b]

        def flat(i, j):
            return flat2[:, i, j, :]

        def cmph(i, k, g):
            return CH[:, i, k, g * 15:(g + 1) * 15]

        def cmpP(t, g):
            return CM[:, (g * 2 + t) * 96:(g * 2 + t + 1) * 96]

        WIDE = [u for s, n in STREAM if s not in ("cmp", "w_p", "down", "even_out", "w_uq", "w_uk", "w_uv",
                                                  "w_fd", "odd_out")
                for u in range(FIRST[s], FIRST[s] + n)]
        G_AT = {u: i for i, u in enumerate(WIDE)}

        def read(u):
            n = G_AT[u]
            return sem(f"bank_free[{n % 2}]"), n // 2 + 1

        @block.sync
        def _(sp):
            for src, dst, name in ((x, xa[:, :, :], "x_in"), (consts, cn[:, :], "consts_in"),
                                   (vecs, vc[:, :], "vecs_in"), (w_small, wsm, "w_small_in")):
                nc.sync.dma_start(dst, src).then_inc(sem(name), 16)
            for s in range(RING):
                nc.sync.dma_start(ring[:, s, :], w[s]).then_inc(sem(f"unit_in[{s}]"), 16)
            nc.sync.dma_start(w2s[:, :, :, :], cmp_w2).then_inc(sem("cmp_w2_in"), 16)
            n = ROWS["b_v"]
            nc.sync.dma_start(rw[:, :], rows[:, n:].broadcast_to([P, NR_ - n])).then_inc(sem("rows_in"), 16)
            nc.sync.dma_start(b_v, rows[:, 0:n].broadcast_to([P, n])).then_inc(sem("rows_in"), 16)

            def refill(u):
                v_ = u - RING
                if CMP0 <= v_ < CMP1:
                    sp.wait_ge(sem("cmp_units"), v_ - CMP0 + 1)
                else:
                    sp.wait_ge(sem("split_done"), half_at(v_) + 2)
                nc.sync.dma_start(ring[:, u % RING, :], w[u]).then_inc(sem(f"unit_in[{u % RING}]"), 16)

            def refills(a, b, skipped):
                with sp.Fori(a // RING, b // RING) as i:
                    for s in range(RING):
                        sp.wait_ge(sem("split_done"), i * (2 * RING) + 2 * (s + 1 - RING - skipped))
                        nc.sync.dma_start(ring[:, s, :], w[bass.ds(i * RING + s, 1)].rearrange(
                            "o p n -> (o p) n")).then_inc(sem(f"unit_in[{s}]"), 16)

            first = CMP0 + RING
            turns = -(-(CMP1 + RING) // RING) * RING
            last = NU // RING * RING
            refills(RING, first // RING * RING, 0)
            for u in range(first // RING * RING, turns):
                refill(u)
            refills(turns, last, CMP1 - CMP0)
            for u in range(last, NU):
                refill(u)
            for t in range(TT):
                sp.wait_ge(sem("out_ready"), t + 1)
                nc.sync.dma_start(out[t * P:(t + 1) * P, :], xb[:, t, :]).then_inc(sem("out_stored"), 16)
            sp.wait_ge(sem("out_stored"), 16 * TT)

        @block.tensor
        def _(pe):
            def unit_in(u):
                pe.wait_ge(sem(f"unit_in[{u % RING}]"), 16 * (u // RING + 1))
                return ring[:, u % RING, :]

            def mm(o, lhsT, rhs, start, stop):
                return nc.tensor.matmul(o, lhsT, rhs, start=start, stop=stop, skip_group_check=True)

            def g_bank(u):
                n = G_AT[u]
                if n >= 2:
                    pe.wait_ge(sem(f"bank_free[{n % 2}]"), n // 2)
                return PS[:, G[n % 2], :]

            def half_in(q):
                pe.wait_ge(sem("split_done"), q + 1)
                return wh[:, q % SPLITS, :], wl[:, q % SPLITS, :]

            def half_out(m):
                m.then_inc(sem("half_used"), 1)

            def three(o, lh, ll, rh, rl, start):
                mm(o, lh, rh, start, False)
                mm(o, lh, rl, False, False)
                return mm(o, ll, rh, False, True)

            def wide_b(u):
                o = g_bank(u)
                for half in range(2):
                    a, b = half_in(half_at(u) + half)
                    act_in(half)
                    for j in range(2):
                        for k in range(4):
                            c_ = slice(k * 256 + j * P, k * 256 + (j + 1) * P)
                            kk = 4 * half + k
                            m = three(o[:, j * S:(j + 1) * S], a[:, c_], b[:, c_], hh[:, kk, :], hl[:, kk, :],
                                      kk == 0 and j == 0)
                    half_out(m)

            def wide_a(u, split=None):
                o = g_bank(u)
                n = split or 256
                for half in range(2):
                    a, b = half_in(half_at(u) + half)
                    act_in(half)
                    for k in range(4):
                        kk, c_ = 4 * half + k, slice(k * 256, k * 256 + n)
                        for t in range(TT):
                            q = slice(t * P, (t + 1) * P)
                            m = three(o[:, t * n:(t + 1) * n], hh[:, kk, q], hl[:, kk, q], a[:, c_], b[:, c_],
                                      kk == 0 and t == 0)
                        if split:
                            c_ = slice(k * 256 + P, (k + 1) * 256)
                            m = three(o[:, S:2 * S], a[:, c_], b[:, c_], hh[:, kk, :], hl[:, kk, :], False)
                    half_out(m)

            act_waits = []

            def act_in(half):
                if len(act_waits) == 2 - half:
                    name, value = act_waits.pop(0)
                    pe.wait_ge(sem(name), value)

            def activations(name, value):
                act_waits[:] = [(name, value - 4), (name, value)]

            def norm_transposes(n):
                for t in range(TT):
                    pe.wait_ge(sem("rows_scaled"), TT * n + t + 1)
                    for k in range(KD):
                        m = nc.tensor.transpose(
                            PS[:, 2 + k // 2, (k % 2) * S + t * P:(k % 2) * S + (t + 1) * P],
                            xh[:, t, k * P:(k + 1) * P], ident)
                m.then_inc(sem("rows_turned"), 1)

            def normed(n):
                activations("h_split", 8 * n + 8)

            def deep(first, n, i0):
                for k in range(2 * n):
                    a, b = half_in(half_of(first) + k)
                    pe.wait_ge(sem("deep_split"), i0 + k + 1)
                    for t in range(TT):
                        q = slice(t * P, (t + 1) * P)
                        for h in range(2):
                            c_ = slice(h * 512, (h + 1) * 512)
                            m = three(PS[:, DEEP + 2 * t + h, :], hh[:, k % 8, q], hl[:, k % 8, q], a[:, c_],
                                      b[:, c_], k == 0)
                    half_out(m)

            def smalls(a, n):
                for name, value in act_waits:
                    pe.wait_ge(sem(name), value)
                act_waits.clear()
                pe.wait_ge(sem("w_small_split"), 1)
                for t in range(TT):
                    for k in range(KD):
                        q = slice(t * P, (t + 1) * P)
                        m = three(PS[:, SC[0], t * 64:t * 64 + n], hh[:, k, q], hl[:, k, q],
                                  wsh[:, k, a:a + n], wsl[:, k, a:a + n], k == 0)
                m.then_inc(sem("small_done"), 1)

            pe.wait_ge(sem("consts_in"), 16)
            norm_transposes(0)
            normed(0)
            for i in range(2):
                wide_b(i)
            smalls(0, 22)
            for i in range(2, 8):
                wide_b(i)
            for i in range(8, 11):
                wide_a(i)
            wide_a(11, split=P)

            pe.wait_ge(sem("fox_logs"), 3)
            for half in range(2):
                for t in range(TT):
                    m = mm(PS[half * 64:half * 64 + 4, SC[0], 0:S], lfa[:, 16 + 4 * t:20 + 4 * t],
                           c("neg_upper", t * S, (t + 1) * S), t == 0, t == TT - 1)
            m.then_inc(sem("fox_rows"), 1)

            def cmp_hidden(i):
                pe.wait_ge(sem("flat_ready"), i + 1)
                for half in range(2):
                    u = FIRST["cmp"] + 2 * i + half
                    wt = unit_in(u)
                    for m_ in range(2):
                        for k in range(8):
                            j = 8 * half + k
                            m = mm(PS[:, PT[i], 32 * m_:32 * m_ + 30],
                                   wt[:, k * 256 + m_ * P:k * 256 + (m_ + 1) * P], flat(i, j),
                                   j == 0 and m_ == 0, j == 15)
                    m.then_inc(sem("cmp_units"), 1)

            def cmp_out(i):
                pe.wait_ge(sem("cmp_gelu"), i + 1)
                pe.wait_ge(sem("cmp_w2_in"), 16)
                for g in range(2):
                    for rep in range(3 if i else 1):
                        for k in range(2):
                            h = cmph(i, k, g)
                            if i == 0:
                                m = mm(PS[g * 64:g * 64 + 64, AV[0], 128:143], w2s[:, 0, k, :], h, k == 0, k == 1)
                            else:
                                m = mm(PS[32 * rep:32 * rep + 15, AV[1], 128 + g * 64:192 + g * 64], h,
                                       w2s[:, 1, k, :], k == 0, k == 1)
                m.then_inc(sem("cmp_done"), 1)

            def cmp_scores():
                pe.wait_ge(sem("cmp_kv"), 1)
                pe.wait_ge(*read(5))
                pe.wait_ge(*read(6))
                pe.wait_ge(sem("fox_rows_copied"), 2)
                for t in range(TT):
                    for h in range(6):
                        g = h // 3
                        m = mm(PS[:, SC[g], t * 96 + (h % 3) * 32:t * 96 + (h % 3) * 32 + 15],
                               QK[g * 64:g * 64 + 64, 10 + h % 3, t * P:(t + 1) * P],
                               ckT[g * 64:g * 64 + 64, 0:15], True, True)
                m.then_inc(sem("cmp_scores"), 1)

            def cmp_probs():
                pe.wait_ge(sem("cmp_probs"), 1)
                for t in range(TT):
                    for g in range(2):
                        m = nc.tensor.transpose(PS[0:96, PT[g], t * P:(t + 1) * P], cmpP(t, g), ident)
                m.then_inc(sem("cmp_probs_turned"), 1)

            def scores(j):
                kind, q, half, k, _, h = JOBS[j]
                last = 7 if kind in ("sel", "win") else 4
                pe.wait_ge(*read(last - 1))
                pe.wait_ge(*read(last))
                if j >= 2:
                    pe.wait_ge(sem("scores_read"), j - 1)
                else:
                    pe.wait_ge(sem("cmp_scores_read"), 1)
                if kind == "fox":
                    pe.wait_ge(sem("fox_rows_copied"), 2)
                b = SC[j % 2]
                lo = half * 64
                for t in range(TT):
                    o = PS[:, b, 0:P] if t == 0 else PS[:, b, P:P + S]
                    n = P * (t + 1)
                    m = mm(o, QK[lo:lo + 64, q, t * P:(t + 1) * P], QK[lo:lo + 64, k, 0:n],
                           True, kind != "fox")
                    if kind == "fox":
                        a, _ = C_AT["rows"]
                        m = mm(o, cn[lo:lo + 4, a + h * P:a + (h + 1) * P], foxr[lo:lo + 4, 0:n], False, True)
                m.then_inc(sem("scores"), 1)

            def turn(j):
                pe.wait_ge(sem("probs_scaled"), j + 1)
                if j >= 2:
                    pe.wait_ge(sem("probs_copied"), j - 1)
                else:
                    pe.wait_ge(sem("cmp_probs_copied"), 2)
                p, b = PB[:, j % 8, :], PT[j % 2]
                nc.tensor.transpose(PS[:, b, 0:P], p[:, 0:P], ident)
                nc.tensor.transpose(PS[:, b, P:2 * P], p[:, P:2 * P], ident)
                nc.tensor.transpose(PS[:, b, 2 * P:3 * P], p[:, 2 * P:3 * P], ident)\
                    .then_inc(sem("probs_turned"), 1)

            def pv(j):
                kind, _, half, _, col, h = JOBS[j]
                yt = Y_TILE[j]
                b, hb, copied = Y_PLACE[yt]
                pe.wait_ge(sem("y_copied"), copied) if copied else pe.wait_ge(sem("cmp_kv"), 2)
                bank = AV[b]
                lo = (h // 3 if kind in ("sel", "win") else h % 2) * 64
                o = PS[lo:lo + 64, bank, hb * S:(hb + 1) * S]
                first = kind != "win"
                if kind == "sel":
                    i = h % 3
                    pe.wait_ge(sem("cmp_probs_copied"), 2)
                    mm(o, cvv[32 * i:32 * i + 15, (h // 3) * 64:(h // 3 + 1) * 64],
                       cmpPT[32 * i:32 * i + 15, h // 3, :], True, False)
                    first = False
                for u in {"fox": (8,), "dil": (9, 10)}.get(kind, (10, 11)):
                    pe.wait_ge(*read(u))
                pe.wait_ge(sem("probs_copied"), j + 1)
                mm(o, V[:, 0, col:col + DH], PTS[:, j % 2, 0:S], first, False)
                m = mm(PS[lo:lo + 64, bank, hb * S + P:(hb + 1) * S], V[:, 1, col:col + DH], PTS[:, j % 2, S:S + P], False,
                       kind != "sel")
                m.then_inc(sem("pv_done"), 1)

            def step(j):
                if j < NJ:
                    scores(j)
                if 0 <= j - PT_LAG < NJ:
                    turn(j - PT_LAG)
                if 0 <= j - PV_LAG < NJ:
                    pv(j - PV_LAG)

            cmp_hidden(0)
            cmp_hidden(1)
            wide_b(FIRST["gates"])
            cmp_out(0)
            wide_b(FIRST["gates"] + 1)
            cmp_out(1)
            wide_b(FIRST["gates"] + 2)
            cmp_scores()
            wide_b(FIRST["gates"] + 3)
            cmp_probs()
            for j in range(NJ + PV_LAG):
                if j % 3 == 0 and 4 + j // 3 < 12:
                    wide_b(FIRST["gates"] + 4 + j // 3)
                step(j)

            for i in range(8):
                a, b = half_in(half_of("w_p") + i)
                if i == 0:
                    pe.wait_ge(sem("y_split"), len(COPIES))
                if i >= 2:
                    pe.wait_ge(sem("merged"), i - 1)
                o = (PS[:, 2 + 2 * (i % 2), 0:S], PS[:, 2 + 2 * (i % 2), S:2 * S], PS[:, 3 + 2 * (i % 2), 0:S])
                for s_, (k0, k1) in enumerate(((0, 2), (2, 5), (5, 8))):
                    for k in range(k0, k1):
                        c_ = slice(k * P, (k + 1) * P)
                        m = three(o[s_], a[:, c_], b[:, c_], hh[:, k, :], hl[:, k, :], k == k0)
                half_out(m)
            activations("merged_split", 8)
            for i in range(4):
                wide_a(FIRST["w_o"] + i)

            norm_transposes(1)
            normed(1)
            for i in range(NF):
                wide_b(FIRST["up"] + i)
            pe.wait_ge(*read(FIRST["up"] + NF - 2))
            pe.wait_ge(*read(FIRST["up"] + NF - 1))
            deep("down", 11, 0)

            norm_transposes(2)
            normed(2)
            for i in range(8):
                wide_b(FIRST["conv_in"] + i)
            smalls(22, 16)
            for i in range(4):
                wide_b(FIRST["qk"] + i)
            for i in range(4):
                wide_a(FIRST["v"] + i)
            for i in range(4):
                wide_b(FIRST["z_a"] + i)
            for i in range(4):
                wide_b(FIRST["o"] + i)

            pe.wait_ge(sem("lstm_logs"), 4)
            for d, (tri, f0, i0) in enumerate((("neg_upper", 0, 0), ("neg_lower", 4, 8))):
                for t in range(TT):
                    mm(PS[0:4, SC[1], d * S:(d + 1) * S], lf2[:, t, f0:f0 + 4], c(tri, t * S, (t + 1) * S),
                       t == 0, False)
                for t in range(TT):
                    m = mm(PS[0:4, SC[1], d * S + t * P:d * S + (t + 1) * P], gt2[:, t, i0:i0 + 4], ident,
                           False, t == TT - 1)
            for d, (tri, f0) in enumerate((("neg_upper", 0), ("neg_lower", 4))):
                for t in range(TT):
                    for j in range(TT):
                        m = mm(PS[:, SC[0], 128 + 8 * d + 4 * t:132 + 8 * d + 4 * t],
                               c(tri, j * S + t * P, j * S + (t + 1) * P), lf2[:, j, f0:f0 + 4],
                               j == 0, j == TT - 1)
            m.then_inc(sem("lstm_rows"), 1)

            def lstm_scores(h):
                pe.wait_ge(sem("lstm_rows_copied"), 2)
                pe.wait_ge(*read(FIRST["qk"] + h))
                if h >= 1:
                    pe.wait_ge(sem("lstm_decay_read"), 4 * h)
                a, _ = C_AT["rows"]
                mm(PS[:, SC[0], :], cn[0:4, a + h * P:a + (h + 1) * P], erow[0:4, :], True, True)\
                    .then_inc(sem("lstm_decay"), 1)
                if h >= 1:
                    pe.wait_ge(sem("lstm_scores_read"), 4 * h)
                for t in range(TT):
                    m = mm(PS[:, SC[1], t * S:(t + 1) * S], QK[:, 2 * h, t * P:(t + 1) * P],
                           QK[:, 2 * h + 1, :], True, True)
                m.then_inc(sem("lstm_scores"), 1)

            def lstm_turn(h):
                pe.wait_ge(sem("lstm_w"), h + 1)
                if h >= 1:
                    pe.wait_ge(sem("lstm_wT"), h)
                for t in range(TT):
                    for s in range(TT):
                        m = nc.tensor.transpose(PS[:, PT[0], s * S + t * P:s * S + (t + 1) * P],
                                                WM[:, h % 2, t * S + s * P:t * S + (s + 1) * P], ident)
                m.then_inc(sem("lstm_turned"), 1)

            def lstm_pv(h):
                pe.wait_ge(sem("lstm_wT"), h + 1)
                pe.wait_ge(*read(FIRST["v"] + h))
                if h >= 1:
                    pe.wait_ge(sem("yb_done"), h)
                for e in range(2):
                    for s in range(TT):
                        m = mm(PS[:, AV[0], e * S:(e + 1) * S], V[:, s, h * 256 + e * P:h * 256 + (e + 1) * P],
                               PTS[:, h % 2, s * S:(s + 1) * S], s == 0, s == TT - 1)
                m.then_inc(sem("lstm_h"), 1)

            def lstm_var(h):
                pe.wait_ge(sem("lstm_sq"), h + 1)
                for e in range(2):
                    m = mm(PS[:, AV[1], 0:S], c("mean", P, 2 * P), T1[:, 0, e * S:(e + 1) * S], e == 0, e == 1)
                m.then_inc(sem("lstm_var"), 1)

            def gn(i):
                pe.wait_ge(sem("gn_u"), i + 1)
                if i >= 1:
                    pe.wait_ge(sem("gn_done"), i)
                mm(PS[:, PT[1], :], c("mean", 0, P), GNU[:, i % 2, :], True, True).then_inc(sem("gn_mean"), 1)

            def gn_var(i):
                pe.wait_ge(sem("gn_sq"), i + 1)
                mm(PS[:, PT[1], :], c("mean", 0, P), T2[:, 0, :], True, True).then_inc(sem("gn_var"), 1)

            for kind, n in EVEN_STEPS:
                if kind == "z_b":
                    wide_b(FIRST["z_b"] + n)
                elif kind == "scores":
                    lstm_scores(n)
                elif kind == "turn":
                    lstm_turn(n)
                elif kind == "pv":
                    lstm_pv(n)
                elif kind == "var":
                    lstm_var(n)
                elif kind == "gn":
                    gn(n)
                elif kind == "gn_var":
                    gn_var(n)
            pe.wait_ge(sem("gn_done"), 4)
            pe.wait_ge(sem("yb_done"), 4)
            deep("even_out", 8, NF)

            norm_transposes(3)
            normed(3)
            for i in range(3):
                wide_b(FIRST["lora"] + i)
            for i in range(2):
                wide_b(FIRST["f_in"] + i)
            pe.wait_ge(sem("lora_sq"), 1)
            for k in range(3):
                mm(PS[:, SC[0], 0:S], c("mean", 256, 384), LS[:, k, :], k == 0, k == 2)
            for k in range(2):
                m = mm(PS[:, SC[0], S:2 * S], c("mean", P, 2 * P), LS[:, 3 + k, :], k == 0, k == 1)
            m.then_inc(sem("lora_var"), 1)
            for i in range(4):
                wide_b(FIRST["z_c"] + i)
            for i in range(2):
                wide_b(FIRST["z_d"] + i)

            pe.wait_ge(sem("late_in"), 16)
            pe.wait_ge(sem("lora_rs"), 1)
            pe.wait_ge(*read(FIRST["f_in"]))
            pe.wait_ge(*read(FIRST["f_in"] + 1))
            for g in range(4):
                for t in range(TT):
                    n = 2 * g + t
                    if n % 2 == 0 and n >= 4:
                        pe.wait_ge(sem("fft1_copied"), n // 2 - 1)
                    m = mm(PS[:, SC[g % 2], t * S:(t + 1) * S], FT[:, g, t * P:(t + 1) * P], c("dft_ch"), True, True)
                m.then_inc(sem("fft1"), 1)
            for g in range(4):
                pe.wait_ge(sem("fft1_copied"), g + 1)
                o = PS[:, PT[g // 2], (g % 2) * S:(g % 2 + 1) * S]
                for t in range(TT):
                    mm(o, F1[:, g, t * S:t * S + P], c("dft_cos", t * S, (t + 1) * S), t == 0, False)
                for t in range(TT):
                    m = mm(o, F1[:, g, t * S + P:(t + 1) * S], c("dft_nsin", t * S, (t + 1) * S), False, t == 1)
                if g % 2:
                    m.then_inc(sem("fft2"), 1)
            def rope_swap(n, src):
                pe.wait_ge(*((sem(f"uq_read[{n}]"), 3) if n < 2 else read(FIRST["lora"] + 2)))
                if n >= 1:
                    pe.wait_ge(sem("rope_swapped_read"), n)
                w_ = 512 if n < 2 else 256
                mm(PS[:, SC[1], 0:w_], c("rope_swap"), src, True, True).then_inc(sem("rope_swapped"), 1)

            def uq_bank(n):
                if n < 2:
                    pe.wait_ge(sem("fft2_copied"), n + 1)
                else:
                    pe.wait_ge(sem(f"uq_read[{n % 2}]"), n // 2)

            pe.wait_ge(sem("lora_ready"), 5)
            for n in range(6):
                uq_bank(n)
                a, b = half_in(half_of("w_uq") + n)
                for j in range(2):
                    for k in range(3):
                        c_ = slice((3 * j + k) * P, (3 * j + k + 1) * P)
                        m = three(PS[:, PT[n % 2], j * S:(j + 1) * S], a[:, c_], b[:, c_], hh[:, k, :],
                                  hl[:, k, :], k == 0)
                half_out(m)
            rope_swap(0, QR[:, 0:2, :])
            for n in range(6, 10):
                uq_bank(n)
                if n % 2 == 0:
                    a, b = half_in(half_of("w_uk") + (n - 6) // 2)
                for j in range(2):
                    for k in range(2):
                        c_ = slice(((n % 2) * 4 + 2 * j + k) * P, ((n % 2) * 4 + 2 * j + k + 1) * P)
                        m = three(PS[:, PT[n % 2], j * S:(j + 1) * S], a[:, c_], b[:, c_], hh[:, 3 + k, :],
                                  hl[:, 3 + k, :], k == 0)
                m.then_inc(sem(UQ_DONE[n][0]), 1)
                if n == 7:
                    rope_swap(1, QR[:, 2:4, :])
            rope_swap(2, KR[:, 0, :])
            for n in range(10, 14):
                uq_bank(n)
                t, h = n % 2, (n - 10) // 2
                if t == 0:
                    a, b = half_in(half_of("w_uv") + h)
                for k in range(2):
                    q, c_ = slice(t * P, (t + 1) * P), slice(k * 512, (k + 1) * 512)
                    m = three(PS[:, PT[n % 2], :], hh[:, 3 + k, q], hl[:, 3 + k, q], a[:, c_], b[:, c_], k == 0)
                m.then_inc(sem(UQ_DONE[n][0]), 1)

            for half in range(2):
                a, b = half_in(half_of("w_fd") + half)
                pe.wait_ge(sem("fft2_split"), 2 * half + 2)
                for j in range(4):
                    for k in range(2):
                        kk, c_ = 2 * half + k, slice(k * 512 + j * P, k * 512 + (j + 1) * P)
                        m = three(PS[:, AV[j // 2], (j % 2) * S:(j % 2 + 1) * S], a[:, c_], b[:, c_],
                                  hh[:, (5 + kk) % 8, :],
                                  hl[:, (5 + kk) % 8, :], kk == 0 and j % 2 == 0)
                half_out(m)

            def mla_scores(h):
                if h == 0:
                    pe.wait_ge(sem("uq_read[0]"), 7)
                    pe.wait_ge(sem("uq_read[1]"), 7)
                    pe.wait_ge(sem("rope_ready"), 3)
                if h >= 2:
                    pe.wait_ge(sem("mla_probs"), 2 * (h - 1))
                lo = 64 * (h % 2)
                for t in range(TT):
                    mm(PS[:, SC[h % 2], t * S:(t + 1) * S], QN[:, h, t * P:(t + 1) * P], KN[:, h, :], True, False)
                    m = mm(PS[:, SC[h % 2], t * S:(t + 1) * S], QR[lo:lo + 64, h // 2, t * P:(t + 1) * P],
                           KR[lo:lo + 64, 0, :], False, True)
                m.then_inc(sem("mla_scores"), 1)

            def mla_turn(h):
                pe.wait_ge(sem("mla_scaled"), h + 1)
                if h >= 2:
                    pe.wait_ge(sem("mla_copied"), h - 1)
                for t in range(TT):
                    for s in range(TT):
                        m = nc.tensor.transpose(PS[:, PT[h % 2], s * S + t * P:s * S + (t + 1) * P],
                                                MP[:, h % 4, t * S + s * P:t * S + (s + 1) * P], ident)
                m.then_inc(sem("mla_turned"), 1)

            def mla_pv(h):
                pe.wait_ge(sem("mla_copied"), h + 1)
                if h < 2:
                    pe.wait_ge(sem("yd_done"), h + 1)
                else:
                    pe.wait_ge(sem("yc_done"), h - 1)
                for s in range(TT):
                    m = mm(PS[:, AV[h % 2], 0:S], V[:, s, h * P:(h + 1) * P], PTS[:, h % 2, s * S:(s + 1) * S],
                           s == 0, s == TT - 1)
                m.then_inc(sem("mla_out"), 1)

            for i in range(8 + 3):
                if i < 8:
                    mla_scores(i)
                if 2 <= i < 10:
                    mla_turn(i - 2)
                if i >= 3:
                    mla_pv(i - 3)

            pe.wait_ge(sem("yc_done"), 8)
            deep("odd_out", 6, NF + 16)

        def ahead(split_half):
            at = {"next": 0}

            def halves(n):
                for q in range(at["next"], min(n, HALVES)):
                    split_half(q)
                at["next"] = max(at["next"], min(n, HALVES))
            return halves

        def bank_of(u):
            return PS[:, G[G_AT[u] % 2], :]

        def freed(ins, u):
            return ins.then_inc(sem(f"bank_free[{G_AT[u] % 2}]"), 1)

        def cols2(ap, n=2):
            return ap.rearrange("p (t c) -> p t c", t=n)

        def uq_dest(n):
            if n < 4:
                return QN[:, 2 * n:2 * n + 2, :]
            if n < 6:
                return QR[:, 2 * n - 8:2 * n - 6, :]
            if n < 10:
                return KN[:, 2 * n - 12:2 * n - 10, :]
            return V[:, n % 2, (n - 10) // 2 * 512:((n - 10) // 2 + 1) * 512]

        def add_pe(eng, i):
            return eng.tensor_tensor(flat2[:, i], flat2[:, i], v("pe", 0, 16).unsqueeze(2).broadcast_to(
                [P, 16, 30]), ALU.add)

        @block.scalar
        def _(act):
            A = nc.scalar.activation

            def split_half(q):
                u = unit_of(q)
                act.wait_ge(sem(f"unit_in[{u % RING}]"), 16 * (u // RING + 1))
                if q >= SPLITS:
                    act.wait_ge(sem("half_used"), q + 1 - SPLITS)
                e = q % 2 * HALF
                A(wh[:, q % SPLITS, :], ring[:, u % RING, e:e + HALF], ACT.Copy).then_inc(sem("hi_ready"), 1)

            halves = ahead(split_half)

            def multiplied(q):
                halves(q + SPLITS)
                act.wait_ge(sem("half_used"), q + 1)
                halves(q + SPLITS + 1)

            def unit(u):
                multiplied(half_at(u) + 1)

            def unit_before_cmp(u):
                halves(half_at(u) + 2)
                act.wait_ge(sem("half_used"), half_at(u) + 2)

            def high(k, src, name, **scale):
                A(hh[:, k, :], src, ACT.Copy, **scale).then_inc(sem(name), 1)

            def deep_high(first, buf, tiles, k):
                if k >= 8:
                    act.wait_ge(sem("half_used"), half_of(first) + k - 7)
                high(k % 8, buf[:, tiles[k], :], "deep_hi")

            def row_stat(m, t, src):
                A(cols2(T1[:, :, :].rearrange("p a b -> p (a b)")), src, ACT.Square, scale=D ** -0.5,
                  accum_out=ssq[:, TT * m + t:TT * m + t + 1]).then_inc(sem("row_ssq"), 1)
                act.wait_ge(sem("row_ssq"), TT * m + t + 1)
                A(rms[:, TT * m + t:TT * m + t + 1], ssq[:, TT * m + t:TT * m + t + 1], ACT.Sqrt,
                  bias=eps_t[:, 0:1]).then_inc(sem("row_rms"), 1)

            def turned_evac(n, gain):
                act.wait_ge(sem("rows_turned"), n + 1)
                for k in range(KD):
                    high(k, PS[:, 2 + k // 2, (k % 2) * S:(k % 2 + 1) * S], "h_hi", scale=v(gain, k))

            def flat_copies(i, u, col, bias):
                b = G[G_AT[u] % 2]
                for g in range(2):
                    src = PS[g * 64:g * 64 + 64, b, col:col + S].rearrange("p (c j r) -> p j c r", c=16, j=8)
                    for par in range(2):
                        for a in range(2):
                            ins = A(flat2[par * 64:par * 64 + 64, i, a * 8:a * 8 + 8, g * 15:g * 15 + 15],
                                    src[:, :, a:a + 15, par], ACT.Identity,
                                    bias=v("b_feat", bias)[g * 64:g * 64 + 64, :])
                return ins

            for name in ("x_in", "vecs_in"):
                act.wait_ge(sem(name), 16)
            act.wait_ge(sem("eps_set"), 2)
            for t in range(TT):
                row_stat(0, t, cols2(xa[:, t, :]))
            act.wait_ge(sem("w_small_in"), 16)
            A(wsh[:, :, :], cols2(wsm, KD), ACT.Copy).then_inc(sem("w_small_hi"), 1)
            halves(SPLITS)
            turned_evac(0, "g1")
            unit(0)
            for j in range(2):
                ins = A(QK[:, j, :], bank_of(0)[:, j * S:(j + 1) * S], ACT.Identity, bias=v("b_feat", j))
            freed(ins, 0)
            unit(1)
            act.wait_ge(sem("fox_logs"), 1)
            e1 = lfa[:, 0:8]
            A(e1, e1, ACT.Exp, scale=-1.0).then_inc(sem("fox_exp"), 1)
            act.wait_ge(sem("fox_exp"), 1)
            A(e1, e1, ACT.Ln, bias=1.0).then_inc(sem("fox_exp"), 1)
            A(cols2(gnsa), small[:, :, 4:22], ACT.Tanh, scale=0.5).then_inc(sem("nsa_tanh"), 1)

            for i in range(1, 7):
                unit(i)
                for j in range(2):
                    ins = A(QK[:, 2 * i + j, :], bank_of(i)[:, j * S:(j + 1) * S], ACT.Identity,
                            bias=v("b_feat", 2 * i + j))
                freed(ins, i)
            unit(7)
            A(QK[:, 14, :], bank_of(7)[:, 0:S], ACT.Identity, bias=v("b_feat", 14))
            freed(flat_copies(0, 7, S, 15), 7)
            unit_before_cmp(11)
            flat_copies(1, 11, S, 16).then_inc(sem("vc_flat"), 1)
            act.wait_ge(sem("fox_rows"), 1)
            for half in range(2):
                lo = 64 * half
                A(foxr[lo:lo + 4, :], PS[lo:lo + 4, SC[0], 0:S], ACT.Copy).then_inc(sem("fox_rows_copied"), 1)

            def gate(i):
                u = FIRST["gates"] + i
                unit(u)
                for j in range(2):
                    ins = A(BIG[:, 2 * i + j, :], bank_of(u)[:, j * S:(j + 1) * S], ACT.Tanh, scale=0.5,
                            bias=half_b[:, 2 * i + j:2 * i + j + 1])
                freed(ins, u)

            def cmp_gelu(i):
                act.wait_ge(sem("cmp_units"), 2 * i + 2)
                A(CH[:, i, :, 0:30], cols2(PS[:, PT[i], 0:64])[:, :, 0:30], ACT.Gelu_apprx_tanh)\
                    .then_inc(sem("cmp_gelu"), 1)

            def cmp_kv(i):
                act.wait_ge(sem("cmp_done"), i + 1)
                if i == 0:
                    ins = A(ckT[:, 0:15], PS[:, AV[0], 128:143], ACT.Copy)
                else:
                    for rep in range(3):
                        ins = A(cvv[32 * rep:32 * rep + 15, :], PS[32 * rep:32 * rep + 15, AV[1], 128:256],
                                ACT.Copy)
                ins.then_inc(sem("cmp_kv"), 1)

            act.wait_ge(sem("half_bias"), 1)
            halves(half_of("gates") + SPLITS)
            cmp_gelu(0)
            cmp_gelu(1)
            cmp_kv(0)
            gate(0)
            cmp_kv(1)
            gate(1)
            gate(2)
            act.wait_ge(sem("cmp_centred"), 1)
            cm12 = cols2(CM, 12)[:, :, 0:15]
            A(cm12, cm12, ACT.Exp).then_inc(sem("cmp_exp"), 1)
            gate(3)
            act.wait_ge(sem("cmp_probs_turned"), 1)
            for g in range(2):
                A(cmpPT[0:96, g, :], PS[0:96, PT[g], 0:S], ACT.Copy).then_inc(sem("cmp_probs_copied"), 1)

            def exp_job(j):
                act.wait_ge(sem("scores_read"), j + 1)
                if j >= 8:
                    act.wait_ge(sem("probs_turned"), j - 7)
                for t in range(TT):
                    a, b = (0, P) if t == 0 else (P, 3 * P)
                    A(PB[:, j % 8, a:b], SM[:, j % 3, a:b], ACT.Exp, scale=-1.0,
                      bias=nmax[:, 2 * j + t:2 * j + t + 1],
                      accum_out=lsum[:, 2 * j + t:2 * j + t + 1]).then_inc(sem("att_exp"), 1)

            def dil_exp(n):
                act.wait_ge(sem("dil_diff"), n + 1)
                A(dil[:, 0:6], dil[:, 0:6], ACT.Exp).then_inc(sem("dil_exp"), 1)

            def probs_copy(j):
                act.wait_ge(sem("probs_turned"), j + 1)
                if j >= 2:
                    act.wait_ge(sem("pv_done"), j - 1)
                A(PTS[:, j % 2, 0:384], PS[:, PT[j % 2], 0:384], ACT.Copy).then_inc(sem("probs_copied"), 1)

            for j in range(NJ + PV_LAG):
                if j % 3 == 0 and 4 + j // 3 < 12:
                    gate(4 + j // 3)
                if j < NJ:
                    exp_job(j)
                    if j in (6, 9):
                        dil_exp((j - 6) // 3)
                if 0 <= j - PT_LAG < NJ:
                    probs_copy(j - PT_LAG)
                for n in Y_SPLIT_AT.get(j, ()):
                    act.wait_ge(sem("y_copied"), n + 1)
                    a, b = COPIES[n][1][0], COPIES[n][1][-1] + 1
                    A(hh[:, a:b, :], Y[:, a:b, :], ACT.Copy).then_inc(sem("y_hi"), 1)
            act.wait_ge(sem("scores_read"), NJ)
            nc.scalar.dma_start(cn[:, C_AT["dil_bias"][0]:C_AT["dil_bias"][0] + NL_], late).then_inc(sem("late_in"), 16)
            nc.scalar.dma_start(ropes[5].bitcast(I32), positions.broadcast_to([P, S]))\
                .then_inc(sem("positions_in"), 16)

            nc.scalar.dma_start(gB[:, :], gains[0:1, :].broadcast_to([P, D])).then_inc(sem("gains_in"), 16)
            multiplied(half_of("w_p") + 7)
            for k in range(KD):
                act.wait_ge(sem("merged"), k + 1)
                high(k, Y[:, 8 + k, :], "merged_hi")
            for i in range(4):
                unit(FIRST["w_o"] + i)
            for i in range(2):
                act.wait_ge(*read(FIRST["w_o"] + 2 + i))
            for t in range(TT):
                row_stat(1, t, cols2(xb[:, t, :]))
            turned_evac(1, "g2")
            CV = T2
            for i in range(NF):
                u = FIRST["up"] + i
                unit(u)
                A(CV[:, i % 2, 0:S], bank_of(u)[:, 0:S], ACT.Identity, scale=v("conv_w", 2 * NF + i),
                  bias=v("conv_b", i)).then_inc(sem("ffn_tap"), 1)
                act.wait_ge(sem("ffn_conv"), i + 1)
                A(CV[:, i % 2, S:2 * S], CV[:, i % 2, 0:S], ACT.Gelu_apprx_tanh).then_inc(sem("ffn_gelu"), 1)
            for k in range(NF):
                if k in (0, NF // 2):
                    for i in range(2):
                        act.wait_ge(*read(FIRST["up"] + NF - 2 + i))
                deep_high("down", BIG, DOWN, k)
                halves(half_of("down") + k + 1)
                if k == 16:
                    act.wait_ge(sem("angles"), 1)
                    A(ropes[0], ropes[0], ACT.Sin).then_inc(sem("rope_tables"), 1)
                    A(ropes[1], ropes[1], ACT.Sin).then_inc(sem("rope_tables"), 1)
            multiplied(half_of("down") + NF - 1)
            for t in range(TT):
                act.wait_ge(sem("x2_ready"), t + 1)
                row_stat(2, t, cols2(xa[:, t, :]))
            for t in range(TT):
                act.wait_ge(sem("x3_ready"), t + 1)
                row_stat(3, t, cols2(xb[:, t, :]))

            turned_evac(2, "g3")
            for i in range(8):
                u = FIRST["conv_in"] + i
                unit(u)
                A(T1[:, i % 2, 0:S], bank_of(u)[:, S:2 * S], ACT.Tanh, scale=0.5).then_inc(sem("a_gate"), 1)
            for i in range(4):
                u = FIRST["qk"] + i
                unit(u)
                freed(A(QK[:, 2 * i:2 * i + 2, :], cols2(bank_of(u)), ACT.Copy), u)
                if i == 1:
                    act.wait_ge(sem("lstm_logs"), 2)
                    A(lfx, lfx, ACT.Exp, scale=-1.0).then_inc(sem("lstm_exp"), 1)
                    act.wait_ge(sem("lstm_exp"), 1)
                    A(lfx, lfx, ACT.Ln, bias=1.0).then_inc(sem("lstm_exp"), 1)
            for i in range(4):
                u = FIRST["v"] + i
                unit(u)
                freed(A(V[:, :, i * 256:(i + 1) * 256], cols2(bank_of(u)), ACT.Copy), u)
            for i in range(4):
                u = FIRST["z_a"] + i
                unit(u)
                freed(A(BIG[:, 2 * i:2 * i + 2, :], cols2(bank_of(u)), ACT.Silu), u)
            for i in range(4):
                u = FIRST["o"] + i
                unit(u)
                freed(A(BIG[:, 8 + 2 * i:10 + 2 * i, :], cols2(bank_of(u)), ACT.Tanh, scale=0.5), u)
            act.wait_ge(sem("lstm_rows"), 1)
            A(erow[0:4, :], PS[0:4, SC[1], :], ACT.Copy).then_inc(sem("lstm_rows_copied"), 1)
            A(nF, PS[:, SC[0], 128:144], ACT.Copy).then_inc(sem("lstm_rows_copied"), 1)

            for kind, n in EVEN_STEPS:
                if kind == "scores":
                    for i, (a, b) in enumerate(LSTM_COLS):
                        act.wait_ge(sem("lstm_decay_read"), 4 * n + i + 1)
                        A(EB[:, n % 2, i, a:b], EB[:, n % 2, i, a:b], ACT.Exp, scale=-1.0,
                          bias=nM[:, 4 * n + i:4 * n + i + 1]).then_inc(sem("lstm_dw"), 1)
                    act.wait_ge(sem("lstm_arg"), n + 1)
                    A(floor[:, 4 * n:4 * n + 4], floor[:, 4 * n:4 * n + 4], ACT.Exp).then_inc(sem("lstm_floor"), 1)
                elif kind == "z_b":
                    u = FIRST["z_b"] + n
                    unit(u)
                    A(T1[:, 1, :], bank_of(u), ACT.Tanh, scale=0.5).then_inc(sem("zb_tanh"), 1)
                elif kind == "turn":
                    act.wait_ge(sem("lstm_turned"), n + 1)
                    A(PTS[:, n % 2, :], PS[:, PT[0], :], ACT.Copy).then_inc(sem("lstm_wT"), 1)
                elif kind == "pv":
                    act.wait_ge(sem("lstm_h"), n + 1)
                    A(T1[:, 0, :], PS[:, AV[0], :], ACT.Square).then_inc(sem("lstm_sq"), 1)
                elif kind == "var":
                    act.wait_ge(sem("lstm_var"), n + 1)
                    A(RSH, PS[:, AV[1], 0:S], ACT.Ln, bias=eps_t[:, 0:1]).then_inc(sem("lstm_rs"), 1)
                    act.wait_ge(sem("lstm_rs"), 2 * n + 1)
                    A(RSH, RSH, ACT.Exp, scale=-0.5).then_inc(sem("lstm_rs"), 1)
                elif kind == "gn":
                    act.wait_ge(sem("gn_xc"), n + 1)
                    A(T2[:, 0, :], XC, ACT.Square).then_inc(sem("gn_sq"), 1)
                elif kind == "gn_var":
                    act.wait_ge(sem("gn_var"), n + 1)
                    A(RSG, PS[:, PT[1], :], ACT.Ln, bias=eps_t[:, 1:2]).then_inc(sem("gn_rs"), 1)
                    act.wait_ge(sem("gn_rs"), 2 * n + 1)
                    A(RSG, RSG, ACT.Exp, scale=-0.5).then_inc(sem("gn_rs"), 1)
                    act.wait_ge(sem("gn_xg"), n + 1)
                    A(T2[:, 1, :], XC, ACT.Tanh, scale=0.5).then_inc(sem("gn_tanh"), 1)
            nc.scalar.dma_start(gB[:, :], gains[1:2, :].broadcast_to([P, D])).then_inc(sem("gains_in"), 16)
            for k in range(16):
                if k == 0:
                    act.wait_ge(sem("gn_done"), 4)
                if k == 8:
                    act.wait_ge(sem("yb_done"), 4)
                deep_high("even_out", Y, EVEN_OUT, k)
                halves(half_of("even_out") + k + 1)
            multiplied(half_of("even_out") + 15)
            for t in range(TT):
                row_stat(4, t, PS[:, DEEP + 2 * t:DEEP + 2 * t + 2, :])
            for t in range(TT):
                act.wait_ge(sem("x4_ready"), t + 1)
                row_stat(5, t, cols2(xa[:, t, :]))

            turned_evac(3, "g4")
            for i in range(3):
                u = FIRST["lora"] + i
                unit(u)
                freed(A(LQ[:, 2 * i:2 * i + 2, :], cols2(bank_of(u)), ACT.Copy), u)
            act.wait_ge(*read(FIRST["lora"] + 1))
            act.wait_ge(*read(FIRST["lora"] + 2))
            A(LS, LQ[:, 0:5, :], ACT.Square).then_inc(sem("lora_sq"), 1)
            for i in range(2):
                u = FIRST["f_in"] + i
                unit(u)
                freed(A(FT[:, 2 * i:2 * i + 2, :], cols2(bank_of(u)), ACT.Copy), u)
            act.wait_ge(sem("lora_var"), 1)
            A(RSL, PS[:, SC[0], :], ACT.Ln, bias=eps_t[:, 0:1]).then_inc(sem("lora_rs"), 1)
            act.wait_ge(sem("lora_rs"), 1)
            A(RSL, RSL, ACT.Exp, scale=-0.5).then_inc(sem("lora_rs"), 1)
            for i in range(6):
                u = FIRST["z_c"] + i
                unit(u)
                A(T1[:, i % 2, :], bank_of(u), ACT.Tanh, scale=0.5).then_inc(sem("zcd_tanh"), 1)
            for g in range(4):
                act.wait_ge(sem("fft1"), g + 1)
                A(F1[:, g, :], PS[:, SC[g % 2], :], ACT.Copy).then_inc(sem("fft1_copied"), 1)
            for k in range(5):
                act.wait_ge(sem("lora_scaled"), k + 1)
                high(k, LQ[:, k, :], "lora_hi")
            for n in range(0, 14, 2):
                halves(UQ_HALF[n] + SPLITS)
                name, value = UQ_DONE[n]
                act.wait_ge(sem(name), value)
                A(uq_dest(n), cols2(PS[:, PT[0], :]) if n < 10 else PS[:, PT[0], :], ACT.Copy)\
                    .then_inc(sem("uq_read[0]"), 1)
                if n == 8:
                    act.wait_ge(sem("fft2_copied"), 2)
                    for k in range(4):
                        high((5 + k) % 8, Y[:, 8 + k, :], "fft2_hi")
            halves(half_of("odd_out") + SPLITS)

            for i in range(8 + 3):
                if i < 8:
                    act.wait_ge(sem("mla_max"), i + 1)
                    if i >= 4:
                        act.wait_ge(sem("mla_turned"), i - 3)
                    for t in range(TT):
                        A(MP[:, i % 4, t * S:(t + 1) * S], PS[:, SC[i % 2], t * S:(t + 1) * S], ACT.Exp,
                          scale=MLA_SCALE, bias=mmax[:, 2 * i + t:2 * i + t + 1],
                          accum_out=msum[:, 2 * i + t:2 * i + t + 1]).then_inc(sem("mla_probs"), 1)
                if 2 <= i < 10:
                    h = i - 2
                    act.wait_ge(sem("mla_turned"), h + 1)
                    if h >= 2:
                        act.wait_ge(sem("mla_out"), h - 1)
                    A(PTS[:, h % 2, :], PS[:, PT[h % 2], :], ACT.Copy).then_inc(sem("mla_copied"), 1)
                if i < 4:
                    act.wait_ge(sem("yd_done"), 2)
                    deep_high("odd_out", Y, ODD_OUT, i)
                elif i < 8:
                    act.wait_ge(sem("yc_done"), i - 3)
                    deep_high("odd_out", Y, ODD_OUT, i)
            act.wait_ge(sem("mla_out"), 8)
            nc.scalar.dma_start(gB[:, :], gains[2:3, :].broadcast_to([P, D])).then_inc(sem("gains_in"), 16)
            for k in range(8, 12):
                act.wait_ge(sem("yc_done"), k - 3)
                deep_high("odd_out", Y, ODD_OUT, k)
                halves(half_of("odd_out") + k + 1)
            multiplied(half_of("odd_out") + 11)
            for t in range(TT):
                row_stat(6, t, PS[:, DEEP + 2 * t:DEEP + 2 * t + 2, :])

        @block.vector
        def _(dve):
            TTn, TS, STT = nc.vector.tensor_tensor, nc.vector.tensor_scalar, nc.vector.scalar_tensor_tensor
            steps = {"n": 0}

            def own(ins):
                steps["n"] += 1
                return ins.then_inc(sem("dve_step"), 1)

            def settled():
                dve.wait_ge(sem("dve_step"), steps["n"])

            def split_half(q):
                dve.wait_ge(sem("hi_ready"), q + 1)
                e = q % 2 * HALF
                TTn(wl[:, q % SPLITS, :], ring[:, unit_of(q) % RING, e:e + HALF],
                    wh[:, q % SPLITS, :].bitcast(F32), ALU.subtract).then_inc(sem("split_done"), 1)

            halves = ahead(split_half)

            def multiplied(q):
                halves(q + SPLITS)
                dve.wait_ge(sem("half_used"), q + 1)
                halves(q + SPLITS + 1)

            def unit(u):
                multiplied(half_at(u) + 1)

            def unit_before_cmp(u):
                halves(half_at(u) + 2)
                dve.wait_ge(sem("half_used"), half_at(u) + 2)

            def keep_up(u):
                halves(half_at(u) + SPLITS + 2)

            def low(k, src, hi, i, name):
                dve.wait_ge(sem(hi), i + 1)
                TTn(hl[:, k, :], src, hh[:, k, :].bitcast(F32), ALU.subtract).then_inc(sem(name), 1)

            def deep_low(first, buf, tiles, k):
                low(k % 8, buf[:, tiles[k], :], "deep_hi", DEEP0[first] + k, "deep_split")

            def row_rstd(m, t):
                dve.wait_ge(sem("row_rms"), TT * m + t + 1)
                q = rms[:, TT * m + t:TT * m + t + 1]
                own(nc.vector.reciprocal(q, q))
                settled()
                return q

            def rows_scale(m, src):
                for t in range(TT):
                    TS(xh[:, t, :], src[:, t, :], row_rstd(m, t), None, ALU.mult).then_inc(sem("rows_scaled"), 1)

            def turned_evac(n, gain):
                for k in range(KD):
                    dve.wait_ge(sem("h_hi"), KD * n + k // 2 * 2 + 2)
                    STT(hl[:, k, :], PS[:, 2 + k // 2, (k % 2) * S:(k % 2 + 1) * S], v(gain, k),
                        hh[:, k, :].bitcast(F32), ALU.mult, ALU.subtract).then_inc(sem("h_split"), 1)

            nc.vector.memset(eps_t[:, 0:1], EPS).then_inc(sem("eps_set"), 1)
            nc.vector.memset(eps_t[:, 1:2], LN_EPS).then_inc(sem("eps_set"), 1)
            for name in ("x_in", "vecs_in"):
                dve.wait_ge(sem(name), 16)
            TS(half_b, v("b_gates", 0, 24), 0.5, None, ALU.mult).then_inc(sem("half_bias"), 1)
            rows_scale(0, xa)
            dve.wait_ge(sem("w_small_hi"), 1)
            TTn(wsl[:, :, :], cols2(wsm, KD), wsh[:, :, :].bitcast(F32), ALU.subtract)\
                .then_inc(sem("w_small_split"), 1)
            halves(SPLITS)
            turned_evac(0, "g1")
            keep_up(0)
            keep_up(1)
            dve.wait_ge(sem("small_done"), 1)
            dve.wait_ge(sem("rows_in"), 32)
            own(TTn(small, cols2(PS[:, SC[0], 0:128])[:, :, 0:22],
                    r("b_small").unsqueeze(1).broadcast_to([P, TT, 22]), ALU.add))
            settled()
            f = small[:, :, 0:4]
            STT(cols2(lfa[:, 0:8]), f, -1.0, f, ALU.mult, ALU.max).then_inc(sem("fox_logs"), 1)
            dve.wait_ge(sem("fox_exp"), 2)
            STT(cols2(lfa[:, 8:16]), f, 0.0, cols2(lfa[:, 0:8]), ALU.min, ALU.subtract).then_inc(sem("fox_logs"), 1)
            dve.wait_ge(sem("fox_logs"), 2)
            TS(lfa[:, 16:24], lfa[:, 8:16], 8.0, None, ALU.mult).then_inc(sem("fox_logs"), 1)
            dve.wait_ge(sem("nsa_tanh"), 1)
            TS(gnsa, gnsa, 1.0, 0.5, ALU.add, ALU.mult).then_inc(sem("nsa_gates"), 1)

            for i in range(8, 12):
                if i < 11:
                    unit(i)
                else:
                    unit_before_cmp(i)
                    dve.wait_ge(sem("vc_flat"), 1)
                a = (i - 8) * 256
                n = 256 if i < 11 else 128
                b = cols2(bank_of(i)[:, 0:2 * n])
                freed(TTn(V[:, :, a:a + n], b, r("b_v", a, a + n).unsqueeze(1).broadcast_to([P, TT, n]),
                          ALU.add), i)
                if i == 8:
                    dve.wait_ge(*read(7))
                    add_pe(nc.vector, 0).then_inc(sem("flat_ready"), 1)
            dve.wait_ge(sem("vc_flat"), 1)
            add_pe(nc.vector, 1).then_inc(sem("flat_ready"), 1)

            for i in range(3):
                keep_up(FIRST["gates"] + i)
            dve.wait_ge(sem("cmp_scores"), 1)
            dve.wait_ge(sem("cm_zero"), 1)
            for g in range(2):
                view = [cols2(q, 6)[:, :, 0:15] for q in
                        (CM[:, g * 192:g * 192 + 192], PS[:, SC[g], 0:192], c("cmp_bias", g * 192, g * 192 + 192))]
                STT(view[0], view[1], DH ** -0.5, view[2], ALU.mult, ALU.add).then_inc(sem("cmp_scores_read"), 1)
            dve.wait_ge(sem("cmp_scores_read"), 2)
            cm12 = cols2(CM, 12)[:, :, 0:15]
            own(nc.vector.tensor_reduce(cst[:, 0:12], cm12, AX.X, ALU.max))
            settled()
            TTn(cm12, cm12, cst[:, 0:12].unsqueeze(2).broadcast_to([P, 12, 15]), ALU.subtract)\
                .then_inc(sem("cmp_centred"), 1)
            dve.wait_ge(sem("cmp_exp"), 1)
            own(TTn(cm12, cm12, cols2(c("cmp_mask"), 12)[:, :, 0:15], ALU.mult))
            settled()
            own(nc.vector.tensor_reduce(cst[:, 12:24], cm12, AX.X, ALU.add))
            settled()
            own(TS(cst[:, 12:24], cst[:, 12:24], 1e-30, None, ALU.max))
            settled()
            own(nc.vector.reciprocal(cst[:, 24:36], cst[:, 12:24]))
            settled()
            gates3 = cols2(gnsa).rearrange("p t (h b) -> p t h b", b=3)
            dve.wait_ge(sem("nsa_gates"), 1)
            for g in range(2):
                own(TTn(cols2(cst[:, 36 + 6 * g:42 + 6 * g]), cols2(cst[:, 24 + 6 * g:30 + 6 * g]),
                        gates3[:, :, 3 * g:3 * g + 3, 0], ALU.mult))
            settled()
            TTn(cm12, cm12, cst[:, 36:48].unsqueeze(2).broadcast_to([P, 12, 15]), ALU.mult)\
                .then_inc(sem("cmp_probs"), 1)

            def scores_in(j):
                kind, h = JOBS[j][0], JOBS[j][5]
                dve.wait_ge(sem("scores"), j + 1)
                if j >= 3:
                    dve.wait_ge(sem("att_exp"), 2 * (j - 2))
                tab = "causal" if kind == "fox" else "dil_bias" if kind == "dil" else "nsa_bias"
                o = 0 if kind == "fox" else h * S
                for t in range(TT):
                    a, b, q = (0, P, o + P) if t == 0 else (P, 3 * P, o)
                    ins = nc.vector.tensor_tensor_reduce(
                        SM[:, j % 3, a:b], PS[:, SC[j % 2], a:b], c(tab, q, q + b - a), -DH ** -0.5, 3e38,
                        ALU.add, ALU.min, nmax[:, 2 * j + t:2 * j + t + 1])
                ins.then_inc(sem("scores_read"), 1)

            def factor(j):
                kind, h = JOBS[j][0], JOBS[j][5]
                if kind != "dil":
                    dve.wait_ge(sem("att_exp"), 2 * j + 2)
                    fj = fac[:, 2 * j:2 * j + 2]
                    if kind == "fox":
                        nc.vector.reciprocal(fj, lsum[:, 2 * j:2 * j + 2]).then_inc(sem("fac_ready"), 1)
                        return
                    own(nc.vector.reciprocal(fj, lsum[:, 2 * j:2 * j + 2]))
                    settled()
                    TTn(fj, fj, gates3[:, :, h, 1 if kind == "sel" else 2], ALU.mult)\
                        .then_inc(sem("fac_ready"), 1)
                elif j in (6, 9):
                    a = 2 * (j - 2)
                    nm = cols2(nmax[:, a:a + 6], 3)
                    dve.wait_ge(sem("scores_read"), j + 1)
                    own(TTn(dil[:, 6:8], nm[:, 0, :], nm[:, 1, :], ALU.min))
                    settled()
                    own(TTn(dil[:, 6:8], dil[:, 6:8], nm[:, 2, :], ALU.min))
                    settled()
                    n = (j - 6) // 3
                    TTn(cols2(dil[:, 0:6], 3), dil[:, 6:8].unsqueeze(1).broadcast_to([P, 3, 2]), nm,
                        ALU.subtract).then_inc(sem("dil_diff"), 1)
                    dve.wait_ge(sem("dil_exp"), n + 1)
                    dve.wait_ge(sem("att_exp"), 2 * j + 2)
                    own(TTn(dil[:, 8:14], dil[:, 0:6], lsum[:, a:a + 6], ALU.mult))
                    settled()
                    own(TTn(dil[:, 14:16], dil[:, 8:10], dil[:, 10:12], ALU.add))
                    settled()
                    own(TTn(dil[:, 14:16], dil[:, 14:16], dil[:, 12:14], ALU.add))
                    settled()
                    own(nc.vector.reciprocal(dil[:, 16:18], dil[:, 14:16]))
                    settled()
                    TTn(cols2(fac[:, a:a + 6], 3), cols2(dil[:, 0:6], 3),
                        dil[:, 16:18].unsqueeze(1).broadcast_to([P, 3, 2]), ALU.mult)\
                        .then_inc(sem("fac_ready"), 1)

            keep_up(FIRST["gates"] + 3)
            for j in range(NJ + PV_LAG):
                if j % 3 == 0 and 4 + j // 3 < 12:
                    keep_up(FIRST["gates"] + 4 + j // 3)
                if j < NJ:
                    scores_in(j)
                if 1 <= j <= NJ and JOBS[j - 1][0] != "dil":
                    factor(j - 1)
                if j in (6, 9):
                    factor(j)
                for bank, tiles, last in COPIES:
                    if last == j - PV_LAG:
                        dve.wait_ge(sem("pv_done"), last + 1)
                        n = len(tiles)
                        nc.vector.tensor_copy(Y[:, tiles[0]:tiles[0] + n, :],
                                              cols2(PS[:, AV[bank], 0:n * S], n)).then_inc(sem("y_copied"), 1)
                for n in Y_SPLIT_AT.get(j, ()):
                    a, b = COPIES[n][1][0], COPIES[n][1][-1] + 1
                    dve.wait_ge(sem("y_hi"), n + 1)
                    TTn(hl[:, a:b, :], Y[:, a:b, :], hh[:, a:b, :].bitcast(F32), ALU.subtract)\
                        .then_inc(sem("y_split"), 1)

            for i in range(8):
                multiplied(half_of("w_p") + i)
                b = 2 + 2 * (i % 2)
                if i < 2:
                    for q in (10, 11):
                        dve.wait_ge(*read(FIRST["gates"] + q))
                srcs = (PS[:, b, 0:S], PS[:, b, S:2 * S], PS[:, b + 1, 0:S])
                dsts = (T1[:, i % 2, 0:S], T1[:, i % 2, S:2 * S], T2[:, i % 2, 0:S])
                for q in range(3):
                    own(STT(dsts[q], BIG[:, 8 * q + i, :], 1.0, srcs[q], ALU.add, ALU.mult))
                settled()
                own(TTn(dsts[0], dsts[0], dsts[1], ALU.add))
                settled()
                TTn(Y[:, 8 + i, :], dsts[0], dsts[2], ALU.add).then_inc(sem("merged"), 1)
            for k in range(KD):
                low(k, Y[:, 8 + k, :], "merged_hi", k, "merged_split")
            for i in range(4):
                u = FIRST["w_o"] + i
                unit(u)
                q = slice(i * 256, (i + 1) * 256)
                freed(STT(xb[:, :, q], cols2(bank_of(u)), 0.5, xa[:, :, q], ALU.mult, ALU.add), u)
            for i in range(2):
                dve.wait_ge(*read(FIRST["w_o"] + 2 + i))
            rows_scale(1, xb)
            turned_evac(1, "g2")
            for i in range(NF):
                u = FIRST["up"] + i
                keep_up(u)
                dve.wait_ge(sem("ffn_tap"), i + 1)
                a, cv = bank_of(u)[:, 0:S], T2[:, i % 2, 0:S]
                own(STT(cv[:, 1:S], a[:, 0:S - 1], v("conv_w", NF + i), cv[:, 1:S], ALU.mult, ALU.add))
                settled()
                STT(cv[:, 2:S], a[:, 0:S - 2], v("conv_w", i), cv[:, 2:S], ALU.mult, ALU.add)\
                    .then_inc(sem("ffn_conv"), 1)
                dve.wait_ge(sem("ffn_gelu"), i + 1)
                freed(TTn(BIG[:, i, :], T2[:, i % 2, S:2 * S], bank_of(u)[:, S:2 * S], ALU.mult), u)

            for k in range(16):
                deep_low("down", BIG, DOWN, k)
                halves(half_of("down") + k + 1)
            dve.wait_ge(sem("positions_in"), 16)
            own(nc.vector.tensor_copy(ropes[4], ropes[5].bitcast(I32)))
            settled()
            own(TS(ropes[2], ropes[4], c("inv_freq"), None, ALU.mult))
            settled()
            own(TS(ropes[3], ropes[2], 1 / (2 * np.pi), 0.25, ALU.mult, ALU.add))
            own(TS(ropes[4], ropes[2], 1 / (2 * np.pi), MAGIC, ALU.mult, ALU.add))
            settled()
            own(TS(ropes[3], ropes[3], MAGIC, MAGIC, ALU.add, ALU.subtract))
            own(TS(ropes[4], ropes[4], MAGIC, None, ALU.subtract))
            settled()
            for part in range(3):
                for q in range(2):
                    src = ropes[2] if part == 0 else ropes[q]
                    own(STT(ropes[q], ropes[3 + q], -TURN[part], src, ALU.mult, ALU.add))
                settled()
            own(TS(ropes[0], ropes[0], float(np.pi / 2), PI_IN, ALU.add, ALU.min))
            own(TS(ropes[1], ropes[1], -PI_IN, PI_IN, ALU.max, ALU.min))
            settled()
            TS(ropes[0], ropes[0], -PI_IN, None, ALU.max).then_inc(sem("angles"), 1)

            for k in range(16, NF):
                deep_low("down", BIG, DOWN, k)
                halves(half_of("down") + k + 1)
            multiplied(half_of("down") + NF - 1)
            for t in range(TT):
                TTn(cols2(xa[:, t, :]), PS[:, DEEP + 2 * t:DEEP + 2 * t + 2, :], cols2(xb[:, t, :]), ALU.add)\
                    .then_inc(sem("x2_ready"), 1)
            dve.wait_ge(sem("gains_in"), 16)
            dve.wait_ge(sem("x2_ready"), TT)
            for t in range(TT):
                q = row_rstd(2, t)
                STT(xb[:, t, :], xa[:, t, :], q, gB[:, :], ALU.mult, ALU.mult).then_inc(sem("x3_ready"), 1)
            dve.wait_ge(sem("x3_ready"), TT)
            rows_scale(3, xb)

            turned_evac(2, "g3")
            def conv_in(i):
                u = FIRST["conv_in"] + i
                keep_up(u)
                dve.wait_ge(sem("a_gate"), i + 1)
                freed(STT(up_in(i, 15, 15 + S), T1[:, i % 2, 0:S], 1.0, bank_of(u)[:, 0:S], ALU.add, ALU.mult), u)

            def taps(a, b):
                for m in range(a, b):
                    group, k = divmod(m, 31)
                    for j, i in enumerate(CONV_DVE[group]):
                        src, acc, wk = up_in(i, k, k + S), BIG[:, 16 + i, :], v("taps", i * 31 + k)
                        if k == 0:
                            ins = TS(acc, src, wk, None, ALU.mult)
                        else:
                            dve.wait_ge(sem("conv_tap"), 3 * (m - 1) + j + 1)
                            ins = STT(acc, src, wk, acc, ALU.mult, ALU.add)
                        ins.then_inc(sem("conv_tap"), 1)

            dve.wait_ge(sem("conv_pads"), 4)
            for i in range(8):
                conv_in(i)
                if i >= 5:
                    dve.wait_ge(*read(FIRST["conv_in"] + i - 2))
                    dve.wait_ge(*read(FIRST["conv_in"] + i - 1))
                    taps(3 * (i - 5), 3 * (i - 4))
            start, n = half_of("qk"), half_of("z_b") - half_of("qk")
            for i in range(n):
                if i == 4:
                    dve.wait_ge(sem("small_done"), 2)
                    own(TTn(gt2, cols2(PS[:, SC[0], 0:128])[:, :, 0:16],
                            r("b_gate").unsqueeze(1).broadcast_to([P, TT, 16]), ALU.add))
                    settled()
                    for d in range(2):
                        f = gt2[:, :, 4 + 8 * d:8 + 8 * d]
                        STT(lfx[:, :, 4 * d:4 * d + 4], f, -1.0, f, ALU.mult, ALU.max).then_inc(sem("lstm_logs"), 1)
                if i == 8:
                    dve.wait_ge(sem("lstm_exp"), 2)
                    for d in range(2):
                        f = gt2[:, :, 4 + 8 * d:8 + 8 * d]
                        STT(lf2[:, :, 4 * d:4 * d + 4], f, 0.0, lfx[:, :, 4 * d:4 * d + 4], ALU.min, ALU.subtract)\
                            .then_inc(sem("lstm_logs"), 1)
                if i == 12:
                    for q in range(2):
                        dve.wait_ge(*read(FIRST["conv_in"] + 6 + q))
                halves(start + i + 1)
                taps(9 + 53 * i // n, 9 + 53 * (i + 1) // n)
            dve.wait_ge(sem("conv_tap"), 186)

            for kind, n in EVEN_STEPS:
                if kind == "scores":
                    dve.wait_ge(sem("lstm_decay"), n + 1)
                    for i, (a, b) in enumerate(LSTM_COLS):
                        d, t = i // 2, i % 2
                        tab = c("causal", P if t == 0 else 0, S) if d == 0 else c("anti", 0, S if t == 0 else P)
                        nc.vector.tensor_tensor_reduce(
                            EB[:, n % 2, i, a:b], PS[:, SC[0], d * S + a:d * S + b], tab, -1.0, 0.0, ALU.add,
                            ALU.min, nM[:, 4 * n + i:4 * n + i + 1]).then_inc(sem("lstm_decay_read"), 1)
                    dve.wait_ge(sem("lstm_decay_read"), 4 * n + 4)
                    dve.wait_ge(sem("lstm_rows_copied"), 2)
                    q = slice(4 * n, 4 * n + 4)
                    TTn(floor[:, q], nF.rearrange("p (i h) -> p i h", h=4)[:, :, n], nM[:, q], ALU.add)\
                        .then_inc(sem("lstm_arg"), 1)
                    dve.wait_ge(sem("lstm_scores"), n + 1)
                    for i, (a, b) in enumerate(LSTM_COLS):
                        dve.wait_ge(sem("lstm_dw"), 4 * n + i + 1)
                        t = i % 2
                        nc.vector.tensor_tensor_reduce(
                            EB[:, n % 2, i, a:b], PS[:, SC[1], t * S + a:t * S + b], EB[:, n % 2, i, a:b],
                            P ** -0.5, 0.0, ALU.mult, ALU.add, den[:, 4 * n + i:4 * n + i + 1])\
                            .then_inc(sem("lstm_scores_read"), 1)
                    dve.wait_ge(sem("lstm_scores_read"), 4 * n + 4)
                    own(STT(den2[:, q], den[:, q], -1.0, den[:, q], ALU.mult, ALU.max))
                    settled()
                    dve.wait_ge(sem("lstm_floor"), n + 1)
                    own(TTn(den2[:, q], den2[:, q], floor[:, q], ALU.max))
                    settled()
                    own(nc.vector.reciprocal(den2[:, q], den2[:, q]))
                    settled()
                    w_, eb = WM[:, n % 2, :], EB[:, n % 2]
                    k = 4 * n
                    own(TS(w_[:, 0:S], eb[:, 2, 0:S], den2[:, k + 2:k + 3], None, ALU.mult))
                    own(TS(w_[:, S:2 * S], eb[:, 1, 0:S], den2[:, k + 1:k + 2], None, ALU.mult))
                    settled()
                    STT(w_[:, 0:P], eb[:, 0, 0:P], den2[:, k:k + 1], w_[:, 0:P], ALU.mult, ALU.add)
                    STT(w_[:, S + P:2 * S], eb[:, 3, P:S], den2[:, k + 3:k + 4], w_[:, S + P:2 * S], ALU.mult,
                        ALU.add).then_inc(sem("lstm_w"), 1)
                elif kind == "z_b":
                    u = FIRST["z_b"] + n
                    keep_up(u)
                    dve.wait_ge(sem("zb_tanh"), n + 1)
                    freed(STT(T1[:, 1, :], T1[:, 1, :], 1.0, bank_of(u), ALU.add, ALU.mult), u)
                    dve.wait_ge(*read(u))
                    oz = BIG[:, 8 + 2 * n:10 + 2 * n, :]
                    dve.wait_ge(*read(FIRST["o"] + n))
                    STT(oz, oz, 1.0, cols2(T1[:, 1, :]), ALU.add, ALU.mult).then_inc(sem("oz_ready"), 1)
                elif kind == "var":
                    dve.wait_ge(sem("lstm_rs"), 2 * n + 2)
                    dve.wait_ge(sem("oz_ready"), n + 1)
                    for e in range(2):
                        own(STT(Y[:, 8 + 2 * n + e, :], PS[:, AV[0], e * S:(e + 1) * S], v("hn_g", 2 * n + e),
                                BIG[:, 8 + 2 * n + e, :], ALU.mult, ALU.mult))
                    settled()
                    y = Y[:, 8 + 2 * n:10 + 2 * n, :]
                    STT(y, y, 0.25, RSH.unsqueeze(1).broadcast_to([P, 2, S]), ALU.mult, ALU.mult)\
                        .then_inc(sem("yb_done"), 1)
                elif kind == "gn":
                    c0 = 2 * gn_pair(n)
                    if c0 == 0:
                        for e in range(CONV_POOL):
                            dve.wait_ge(sem(f"pool_acc[{e}]"), 31)
                    for e in range(2):
                        ins = TS(GNU[:, n % 2, e * S:(e + 1) * S], BIG[:, 16 + c0 + e, :], 0.5,
                                 v("tap_b", c0 + e), ALU.mult, ALU.add)
                    ins.then_inc(sem("gn_u"), 1)
                    dve.wait_ge(sem("gn_u"), n + 1)
                    dve.wait_ge(sem("gn_mean"), n + 1)
                    TTn(XC, GNU[:, n % 2, :], PS[:, PT[1], :], ALU.subtract).then_inc(sem("gn_xc"), 1)
                elif kind == "gn_var":
                    dve.wait_ge(sem("gn_rs"), 2 * n + 2)
                    own(TTn(XC, XC, RSG, ALU.mult))
                    settled()
                    c0 = 2 * gn_pair(n)
                    for e in range(2):
                        q = XC[:, e * S:(e + 1) * S]
                        ins = TS(q, q, v("gn_g", c0 + e), v("gn_b", c0 + e), ALU.mult, ALU.add)
                    ins.then_inc(sem("gn_xg"), 1)
                    dve.wait_ge(sem("gn_tanh"), n + 1)
                    own(STT(T2[:, 1, :], T2[:, 1, :], 1.0, XC, ALU.add, ALU.mult))
                    settled()
                    STT(Y[:, c0:c0 + 2, :], cols2(T2[:, 1, :]), 0.5, BIG[:, c0:c0 + 2, :], ALU.mult,
                        ALU.mult).then_inc(sem("gn_done"), 1)

            def post_norm(m, base, dst, name):
                dve.wait_ge(sem("gains_in"), 32 if m == 4 else 48)
                for t in range(TT):
                    q = row_rstd(m, t)
                    own(STT(cols2(xh[:, t, :]), PS[:, DEEP + 2 * t:DEEP + 2 * t + 2, :], q, cols2(gB[:, :]),
                            ALU.mult, ALU.mult))
                    settled()
                    TTn(dst[:, t, :], xh[:, t, :], base[:, t, :], ALU.add).then_inc(sem(name), 1)

            for k in range(16):
                deep_low("even_out", Y, EVEN_OUT, k)
                halves(half_of("even_out") + k + 1)
            halves(half_of("lora") + SPLITS)
            post_norm(4, xb, xa, "x4_ready")
            dve.wait_ge(sem("x4_ready"), TT)
            rows_scale(5, xa)

            turned_evac(3, "g4")
            for i in range(5):
                keep_up(FIRST["lora"] + i)
            dve.wait_ge(sem("lora_rs"), 2)
            for k in range(5):
                STT(LQ[:, k, :], LQ[:, k, :], v("g_q", k) if k < 3 else v("g_kv", k - 3),
                    RSL[:, 0:S] if k < 3 else RSL[:, S:2 * S], ALU.mult, ALU.mult).then_inc(sem("lora_scaled"), 1)
            for i in range(6):
                u = FIRST["z_c"] + i
                keep_up(u)
                dve.wait_ge(sem("zcd_tanh"), i + 1)
                o = ZC[:, 2 * i:2 * i + 2, :] if i < 4 else ZD[:, 2 * i - 8:2 * i - 6, :]
                freed(STT(o, cols2(T1[:, i % 2, :]), 1.0, cols2(bank_of(u)), ALU.add, ALU.mult), u)
            for k in range(5):
                low(k, LQ[:, k, :], "lora_hi", k, "lora_ready")
            for m in range(2):
                dve.wait_ge(sem("fft2"), m + 1)
                nc.vector.tensor_copy(Y[:, 8 + 2 * m:10 + 2 * m, :], cols2(PS[:, PT[m], :]))\
                    .then_inc(sem("fft2_copied"), 1)

            def rotate(n, src):
                tiles = 2 if n < 2 else 1
                dve.wait_ge(sem("rope_tables"), 2)
                if n < 2:
                    dve.wait_ge(sem(f"uq_read[{n}]"), 3)
                dve.wait_ge(sem("rope_swapped"), n + 1)
                a, b = T2[:, 0, 0:tiles * S], T2[:, 1, 0:tiles * S]
                if n:
                    dve.wait_ge(sem("rope_ready"), n)
                own(TTn(cols2(a, tiles), src, ropes[0].unsqueeze(1).broadcast_to([P, tiles, S]), ALU.mult))
                TTn(cols2(b, tiles), cols2(PS[:, SC[1], 0:tiles * S], tiles),
                    ropes[1].unsqueeze(1).broadcast_to([P, tiles, S]), ALU.mult)\
                    .then_inc(sem("rope_swapped_read"), 1)
                settled()
                dve.wait_ge(sem("rope_swapped_read"), n + 1)
                TTn(src, cols2(a, tiles), cols2(b, tiles), ALU.add).then_inc(sem("rope_ready"), 1)

            for n in range(1, 14, 2):
                multiplied(UQ_HALF[n])
                nc.vector.tensor_copy(uq_dest(n), cols2(PS[:, PT[1], :]) if n < 10 else PS[:, PT[1], :])\
                    .then_inc(sem("uq_read[1]"), 1)
                if n == 5:
                    rotate(0, QR[:, 0:2, :])
                if n == 9:
                    for k in range(4):
                        low((5 + k) % 8, Y[:, 8 + k, :], "fft2_hi", k, "fft2_split")
                    rotate(1, QR[:, 2:4, :])
                    rotate(2, KR[:, :, :])
            multiplied(half_of("w_fd") + 1)
            for m in range(2):
                dve.wait_ge(*read(FIRST["z_d"] + m))
                STT(Y[:, 8 + 2 * m:10 + 2 * m, :], cols2(PS[:, AV[m], :]), 0.5, ZD[:, 2 * m:2 * m + 2, :],
                    ALU.mult, ALU.mult).then_inc(sem("yd_done"), 1)
            halves(half_of("odd_out") + SPLITS)

            for i in range(8 + 3):
                if i < 8:
                    dve.wait_ge(sem("mla_scores"), i + 1)
                    q = mmax[:, 2 * i:2 * i + 2]
                    own(nc.vector.tensor_reduce(q, cols2(PS[:, SC[i % 2], :]), AX.X, ALU.max))
                    settled()
                    TS(q, q, -MLA_SCALE, None, ALU.mult).then_inc(sem("mla_max"), 1)
                if 1 <= i < 9:
                    h = i - 1
                    dve.wait_ge(sem("mla_probs"), 2 * h + 2)
                    q = msum[:, 2 * h:2 * h + 2]
                    nc.vector.reciprocal(q, q).then_inc(sem("mla_rec"), 1)
                if i >= 3:
                    h = i - 3
                    dve.wait_ge(sem("mla_out"), h + 1)
                    if h % 2 == 0:
                        dve.wait_ge(*read(FIRST["z_c"] + h // 2))
                    STT(Y[:, h, :], PS[:, AV[h % 2], 0:S], 0.5, ZC[:, h, :], ALU.mult, ALU.mult)\
                        .then_inc(sem("yc_done"), 1)
                if i < 8:
                    deep_low("odd_out", Y, ODD_OUT, i)
            for k in range(8, 12):
                deep_low("odd_out", Y, ODD_OUT, k)
                halves(half_of("odd_out") + k + 1)
            post_norm(6, xa, xb, "out_ready")

        @block.gpsimd
        def _(pool):
            nc.gpsimd.memset(CM, 0.0).then_inc(sem("cm_zero"), 1)
            for j in range(NJ):
                pool.wait_ge(sem("fac_ready"), FAC[j])
                for t in range(TT):
                    q = PB[:, j % 8, 0:P] if t == 0 else PB[:, j % 8, P:3 * P]
                    ins = nc.gpsimd.tensor_scalar(q, q, fac[:, 2 * j + t:2 * j + t + 1], None, ALU.mult)
                ins.then_inc(sem("probs_scaled"), 1)
            for buf, name, value in ((UP_DVE, "merged_split", KD), (UP_POOL, "x3_ready", TT)):
                pool.wait_ge(sem(name), value)
                nc.gpsimd.memset(buf[:, :, 0:15], 0.0).then_inc(sem("conv_pads"), 1)
                nc.gpsimd.memset(buf[:, :, 15 + S:CONV_W], 0.0).then_inc(sem("conv_pads"), 1)
            pool.wait_ge(sem("conv_pads"), 4)
            for i in range(CONV_POOL):
                pool.wait_ge(*read(FIRST["conv_in"] + i))
            for k in range(31):
                for i in range(CONV_POOL):
                    src, acc, tmp = up_in(i, k, k + S), BIG[:, 16 + i, :], POOL_TMP[:, i, :]
                    wk = v("taps", i * 31 + k)
                    if k == 0:
                        nc.gpsimd.tensor_scalar(acc, src, wk, None, ALU.mult).then_inc(sem(f"pool_acc[{i}]"), 1)
                    else:
                        pool.wait_ge(sem(f"pool_acc[{i}]"), k)
                        nc.gpsimd.tensor_scalar(tmp, src, wk, None, ALU.mult).then_inc(sem(f"pool_tmp[{i}]"), 1)
                if k:
                    for i in range(CONV_POOL):
                        acc, tmp = BIG[:, 16 + i, :], POOL_TMP[:, i, :]
                        pool.wait_ge(sem(f"pool_tmp[{i}]"), k)
                        ins = nc.gpsimd.tensor_tensor(acc, acc, tmp, ALU.add).then_inc(sem(f"pool_acc[{i}]"), 1)
            for h in range(8):
                pool.wait_ge(sem("mla_rec"), h + 1)
                for t in range(TT):
                    q = MP[:, h % 4, t * S:(t + 1) * S]
                    ins = nc.gpsimd.tensor_scalar(q, q, msum[:, 2 * h + t:2 * h + t + 1], None, ALU.mult)
                ins.then_inc(sem("mla_scaled"), 1)


def slope(i):
    return np.exp2(-8.0 * i / 12)


def constant_tables():
    p = np.arange(P)[:, None]
    s = np.arange(S)[None, :]
    masked = np.float64(MASKED)
    out = np.zeros((P, NC_), np.float32)
    late = np.zeros((P, NL_), np.float32)

    def put(name, a):
        o, n = C_AT[name]
        out[:, o:o + n] = np.asarray(a, np.float64).reshape(P, n)

    put("ident", np.eye(P))
    put("mean", np.concatenate([np.full((P, P), 1.0 / n) for n in (128, 256, 384)], 1))
    put("neg_upper", np.concatenate([-1.0 * (p + t * P <= s) for t in range(TT)], 1))
    put("neg_lower", np.concatenate([-1.0 * (p + t * P >= s) for t in range(TT)], 1))
    dist = p + P - s
    causal = np.where(dist >= 0, 0.0, masked)
    put("causal", causal)
    put("anti", np.where(s >= p, 0.0, masked))
    dil = []
    for g, (w, rate) in enumerate(((128, 1), (512, 4), (2048, 16))):
        for h in range(2):
            ok = (dist >= 0) & (dist <= w) & (dist % rate == 0)
            dil.append(np.where(ok, -8.0 * slope(2 * (2 * g + h) + 1) * dist, masked))
    put("dil_bias", np.concatenate(dil, 1))
    put("nsa_bias", np.concatenate([np.where(dist >= 0, -8.0 * slope(2 * h + 2) * dist, masked)
                                    for h in range(6)], 1))
    bias, mask = np.zeros((P, 2, TT, 3, 32)), np.zeros((P, 2, TT, 3, 32))
    end = np.arange(15) * 16 + 31
    for g in range(2):
        for t in range(TT):
            for h in range(3):
                far = p + t * P - end[None, :]
                bias[:, g, t, h, :15] = np.where(far >= 0, -slope(2 * (3 * g + h) + 2) * far, masked)
                mask[:, g, t, h, :15] = far >= 0
    put("cmp_bias", bias)
    put("cmp_mask", mask)
    rows = np.zeros((P, 4, P))
    for h in range(4):
        rows[h, h], rows[64 + h, h] = 1.0, 1.0
    put("rows", rows)
    inv = (10000.0 ** (-np.arange(0, 64, 2, dtype=np.float32) / np.float32(64))).astype(np.float32)
    put("inv_freq", np.tile(inv, 4)[:, None])

    def put_late(name, a):
        o, n = L_AT[name]
        late[:, o:o + n] = np.asarray(a, np.float64).reshape(P, n)

    ch = 2 * np.pi * ((np.arange(P)[:, None] * np.arange(P)[None, :]) % P) / P
    put_late("dft_ch", np.concatenate([np.cos(ch), np.sin(ch)], 1) / np.sqrt(P))
    tk = 2 * np.pi * ((np.arange(S)[:, None] * np.arange(S)[None, :]) % S) / S
    put_late("dft_cos", np.concatenate([np.cos(tk)[t * P:(t + 1) * P] for t in range(TT)], 1) / np.sqrt(S))
    put_late("dft_nsin", np.concatenate([-np.sin(tk)[t * P:(t + 1) * P] for t in range(TT)], 1) / np.sqrt(S))
    swap = np.zeros((P, P))
    for m in range(P):
        if m % 64 < 32:
            swap[m + 32, m] = -1.0
        else:
            swap[m - 32, m] = 1.0
    put_late("rope_swap", swap)
    return out, late


def wide(w, k):
    n = w.shape[1] // 256
    return w.reshape(k, P, n, 256).transpose(2, 1, 0, 3).reshape(n, P, k * 256)


def deep_units(w):
    n = w.shape[0] // 256
    return w.reshape(n, 2, P, D).transpose(0, 2, 1, 3).reshape(n, P, 2 * D)


def halves_of(w, k, tiles):
    n = w.shape[1] // (tiles * P)
    a = w.reshape(k, P, n, tiles, P).transpose(2, 1, 3, 0, 4).reshape(n, P, tiles * k * P)
    out = np.zeros((n, P, HALF), np.float32)
    out[:, :, :a.shape[2]] = a
    return out.reshape(n // 2, 2, P, HALF).transpose(0, 2, 1, 3).reshape(n // 2, P, UNIT)


def columns(v, n):
    return v.reshape(n, P).T


def kernel(**inputs):
    import concourse.bacc as bacc
    from concourse.bass_utils import run_bass_kernel_spmd

    a = {k: np.asarray(q) for k, q in inputs.items()}
    w_in, b_in = a["w_in"][0], a["b_in"][0]
    at = np.cumsum([0, 256, 256, 256, 4, 384, 384, 384, 384, 128, 128, 128, 128, 128, 128, 18, 3072])
    (qa, ka, va, fa, qb, kb, vb, qc, kc, vcm, ks, vs, kw, vw, gc, gates) = (
        np.arange(i, j) for i, j in zip(at[:-1], at[1:]))
    qc = np.concatenate([qc[h * DH:(h + 1) * DH] for i in range(3) for h in (i, i + 3)])
    cols = [qa, ka]
    for g in range(3):
        cols += [qb[g * P:(g + 1) * P], kb[g * P:(g + 1) * P]]
    cols += [qc, ks, kw, kc]
    feat = np.concatenate(cols)
    vcols = np.concatenate([va, vb, vs, vw])
    order = np.concatenate([feat, vcols, vcm])
    w_pc = np.concatenate([a["w_pc"][0][h * DH:(h + 1) * DH] for i in range(3) for h in (i, i + 3)])
    up = a["w_up"][0].reshape(D, 2, NF, P).transpose(0, 2, 1, 3).reshape(D, 2 * DFF)
    ew = a["even_w_in_2"][0]
    e_at = np.cumsum([0, 1024, 1024, 1024, 512, 512, 1024, 1024, 1024, 16])
    a_val, a_gate, z_a, eq, ek, ev, eo, z_b, eg = (ew[:, i:j] for i, j in zip(e_at[:-1], e_at[1:]))

    def pair(x_, y_, n):
        return np.stack([x_.reshape(D, n, P), y_.reshape(D, n, P)], 2).reshape(D, 2 * n * P)

    ow = a["odd_w_in_2"][0]
    o_at = np.cumsum([0, 384, 256, 64, 512, 1024, 512])
    cq, ckv, kr, f_in, z_c, z_d = (ow[:, i:j] for i, j in zip(o_at[:-1], o_at[1:]))
    uq = a["odd_w_uq_2"][0].reshape(384, 8, 192)
    uq = np.concatenate([uq[:, :, :128].reshape(384, 1024), uq[:, :, 128:].reshape(384, 512)], 1)
    ukv = a["odd_w_ukv_2"][0].reshape(256, 8, 256)
    odd_out = a["odd_w_out_2"][0]
    units = {
        "proj": wide(w_in[:, order], KD), "gates": wide(w_in[:, gates], KD),
        "cmp": np.concatenate([a[n][0].reshape(2, 8, P, 256).transpose(0, 2, 1, 3).reshape(2, P, UNIT)
                               for n in ("cmp_k_w1", "cmp_v_w1")]),
        "w_p": halves_of(np.concatenate([a["w_pa"][0], a["w_pb"][0], w_pc]), KD, 1),
        "w_o": wide(a["w_o"][0], KD), "up": wide(up, KD), "down": deep_units(a["w_down"][0]),
        "conv_in": wide(pair(a_val, a_gate, 8), KD), "z_a": wide(z_a, KD), "qk": wide(pair(eq, ek, 4), KD),
        "v": wide(ev, KD), "o": wide(eo, KD), "z_b": wide(z_b, KD),
        "even_out": deep_units(a["even_w_out_2"][0]),
        "lora": wide(np.concatenate([cq, ckv, kr, kr], 1), KD), "f_in": wide(f_in, KD),
        "w_uq": halves_of(uq, 3, 2), "w_uk": halves_of(ukv[:, :, :128].reshape(256, 1024), 2, 4),
        "w_uv": ukv[:, :, 128:].reshape(2, P, 2, 512).transpose(1, 2, 0, 3).reshape(1, P, UNIT),
        "z_c": wide(z_c, KD), "z_d": wide(z_d, KD),
        "w_fd": a["odd_w_fd_2"][0].reshape(1, 4, P, 512).transpose(0, 2, 1, 3).reshape(1, P, UNIT),
        "odd_out": deep_units(np.concatenate([odd_out[8 * P:], odd_out[:8 * P]])),
    }
    w = np.concatenate([units[name] for name, n in STREAM])
    small = np.concatenate([w_in[:, fa], w_in[:, gc], eg], 1)
    w_small = small.reshape(KD, P, 38).transpose(1, 0, 2)
    cmp_w2 = np.stack([a[n][0].reshape(2, P, DH).transpose(1, 0, 2) for n in ("cmp_k_w2", "cmp_v_w2")], 1)

    vecs = np.zeros((P, NV_), np.float32)

    def put(name, x_):
        o, n = V_AT[name]
        vecs[:, o:o + x_.shape[1]] = x_

    put("g1", columns(a["norm1_g"][0], 8))
    put("b_feat", columns(np.concatenate([b_in[feat], b_in[vcm]]), 17))
    put("b_gates", columns(b_in[gates], 24))
    put("pe", a["cmp_pe"][0].reshape(16, P).T)
    put("g2", columns(a["norm2_g"][0], 8))
    put("conv_w", columns(a["conv_w"][0].reshape(-1), 66))
    put("conv_b", columns(a["conv_b"][0], 22))
    put("g3", columns(a["even_g_pre_2"][0], 8))
    put("taps", a["even_conv_w_2"][0].reshape(31, 8, P).transpose(2, 1, 0).reshape(P, 248))
    put("tap_b", columns(a["even_conv_b_2"][0], 8))
    put("gn_g", columns(a["even_gn_g_2"][0], 8))
    put("gn_b", columns(a["even_gn_b_2"][0], 8))
    put("hn_g", columns(a["even_hn_g_2"][0], 8))
    put("g4", columns(a["odd_g_pre_2"][0], 8))
    put("g_q", columns(a["odd_g_q_2"][0], 3))
    put("g_kv", columns(a["odd_g_kv_2"][0], 2))
    rows = np.concatenate([b_in[vcols], b_in[fa], b_in[gc], a["even_b_gate_2"][0]])[None, :]
    gains = np.stack([a["final_g"], a["even_g_post_2"][0], a["odd_g_post_2"][0]])
    consts, late = constant_tables()
    arrays = {"w": w, "w_small": w_small, "consts": consts, "late": late, "vecs": vecs, "rows": rows,
              "gains": gains, "x": a["x"][0].reshape(TT, P, D).transpose(1, 0, 2),
              "positions": a["positions_2"].astype(np.int32), "cmp_w2": cmp_w2}
    arrays = {k: np.ascontiguousarray(q) for k, q in arrays.items()}
    nc = bacc.Bacc("TRN2", target_bir_lowering=False, num_devices=1)
    args = {k: nc.dram_tensor(k, q.shape, mybir.dt.from_np(q.dtype), kind="ExternalInput").ap()
            for k, q in arrays.items()}
    out = nc.dram_tensor("out", (S, D), F32, kind="ExternalOutput").ap()
    program(nc, out=out, **args)
    r = run_bass_kernel_spmd(nc, [arrays], core_ids=[0])
    return r.results[0]["out"].reshape(1, S, D)
```

```python
from contextlib import ExitStack

import numpy as np

import concourse.bass as bass
from concourse import mybir

P = 128
S = 256
TT = S // P
D = 1024
KD = D // P
DFF = 2816
NF = DFF // P
DH = 64
EPS, LN_EPS = 1e-6, 1e-5
MASKED = -1e30
RING = 3
SPLITS = 3
HALF = 1024
UNIT = 2048
MLA_SCALE = 192 ** -0.5
TURN = (6.28125, 0.0019350051879882812, 3.0199159795074593e-07)
MAGIC = 1.5 * 2.0 ** 23
PI_IN = 3.1415925
LSTM_COLS = ((0, P), (0, S), (0, S), (P, S))

F32 = mybir.dt.float32
F32R = mybir.dt.float32r
I32 = mybir.dt.int32
ALU = mybir.AluOpType
ACT = mybir.ActivationFunctionType
AX = mybir.AxisListType

CONST = dict(ident=128, mean=3 * 128, neg_upper=2 * 256, neg_lower=2 * 256, causal=256, anti=256,
             dil_bias=6 * 256, nsa_bias=6 * 256, cmp_bias=12 * 32, cmp_mask=12 * 32, rows=4 * 128,
             inv_freq=1)
LATE = dict(dft_ch=256, dft_cos=2 * 256, dft_nsin=2 * 256, rope_swap=128)
VECS = dict(g1=8, b_feat=18, b_gates=24, pe=16, g2=8, conv_w=66, conv_b=22, g3=8, taps=8 * 31,
            tap_b=8, gn_g=8, gn_b=8, hn_g=8, g4=8, g_q=3, g_kv=2)
ROWS = dict(b_v=896, b_small=22, b_gate=16)


def offsets(table):
    at, out = 0, {}
    for name, n in table.items():
        out[name] = (at, n)
        at += n
    return out, at


C_AT, NC_ = offsets(CONST)
V_AT, NV_ = offsets(VECS)
R_AT, NR_ = offsets(ROWS)
L_AT, NL_ = offsets(LATE)
assert NL_ <= CONST["dil_bias"]
for _name, (_o, _n) in L_AT.items():
    C_AT[_name] = (C_AT["dil_bias"][0] + _o, _n)

STREAM = [("proj", 12), ("cmp", 4), ("gates", 12), ("w_p", 4), ("w_o", 4), ("up", 22), ("down", 11),
          ("conv_in", 8), ("qk", 4), ("z_a", 4), ("v_o_z", 12), ("even_out", 8),
          ("lora", 3), ("f_in", 2), ("z_c", 4), ("z_d", 2), ("w_uq", 3), ("w_uk", 1), ("w_uv", 1),
          ("w_fd", 1), ("odd_out", 6)]
FIRST, NU = {}, 0
for _name, _n in STREAM:
    FIRST[_name] = NU
    NU += _n

CMP0, CMP1 = FIRST["cmp"], FIRST["cmp"] + 4


def half_at(u):
    return 2 * (u if u < CMP0 else u - 4)


def half_of(name):
    return half_at(FIRST[name])


def unit_of(q):
    return q // 2 if q // 2 < CMP0 else q // 2 + 4


HALVES = half_at(NU)


def v_unit(h):
    return FIRST["v_o_z"] + 3 * h


def o_unit(h):
    return v_unit(h) + 1


def z_unit(h):
    return v_unit(h) + 2


JOBS = [("fox", h // 2, h % 2, 2 + h // 2, h * DH, h) for h in range(4)]
JOBS += [("dil", 4 + 2 * g, h, 5 + 2 * g, 256 + (2 * g + h) * DH, 2 * g + h)
         for h in range(2) for g in range(3)]
for _i in range(3):
    for _h in (_i, _i + 3):
        _g = _h // 3
        JOBS.append(("sel", 10 + _i, _g, 13, 640 + _g * DH, _h))
        JOBS.append(("win", 10 + _i, _g, 14, 768 + _g * DH, _h))
NJ = len(JOBS)
PT_LAG, PV_LAG = 4, 5
Y_TILE = [h // 2 if k == "fox" else 2 + h // 2 if k == "dil" else 5 + h % 3
          for k, _, _, _, _, h in JOBS]
Y_PLACE = {0: (0, 0, 0), 1: (0, 1, 0), 2: (1, 0, 0), 3: (1, 1, 0), 4: (0, 0, 1), 5: (1, 0, 2),
           6: (0, 0, 3), 7: (1, 0, 4)}
COPIES = [(0, (0, 1), 3), (1, (2, 3), 9), (0, (4,), 9), (1, (5,), 13), (0, (6,), 17), (1, (7,), 21)]
Y_SPLIT_AT = {NJ: (0, 1, 2, 3), NJ + 1: (4,), NJ + PV_LAG - 1: (5,)}
GATE_HALVES = [0] + [min(16, -(-16 * (j + 1) // NJ)) for j in range(NJ + PV_LAG)]
FAC = [j + 1 if j < 4 else 5 + (j - 4) // 3 if j < 10 else j - 3 for j in range(NJ)]

EVEN_STEPS = []
for _h in range(4):
    EVEN_STEPS += [([("weigh", _h), ("gn_y", _h - 1)] if _h else [("decay", 0)]) + [("gn_u", _h)],
                   [("yb", _h - 1)] if _h else [("weigh", 0)],
                   [], [("turn", _h), ("gn", _h)], [("pv", _h), ("gn_var", _h)],
                   [("var", _h)] + ([("decay", _h + 1)] if _h < 3 else []) + [("gn_x", _h)]]
EVEN_STEPS[-3] += [("split", 0)]
EVEN_STEPS[-2] += [("deep", 0), ("split", 1)]
EVEN_STEPS[-1][1:1] = [("deep", 1)]
EVEN_STEPS += [[("yb", 3), ("gn_y", 3)]]
EVEN_HALVES = 22
EVEN_EARLY = 3

UQ_HALF = [half_of("w_uq") + n if n < 6 else half_of("w_uk") + (n - 6) // 2 for n in range(14)]
UQ_DONE = [("uq_part", (n - 4) // 2) if n >= 6 and n % 2 == 0 else ("half_used", UQ_HALF[n] + 1)
           for n in range(14)]

DOWN = [k for k in range(NF)]
DOWN_EARLY = 4
EVEN_OUT = [4, 5, 6, 7, 2, 3, 8, 9, 10, 11, 12, 13, 0, 1, 14, 15]
ODD_OUT = [8, 9, 10, 11, 0, 1, 2, 3, 4, 5, 6, 7]
DEEP0 = {"down": 0, "even_out": NF, "odd_out": NF + 16}
GN_PAIRS = (2, 3, 1, 0)
CONV_DVE = ((4, 5), (6, 7))
CONV_POOL = 4
CONV_W = S + 30
TAPS = 31
PRODUCTS = [(i, k) for k in range(TAPS) for i in (2, 3)] + [(1, k) for k in range(TAPS)]
ADDED = [sum(1 for _, k in PRODUCTS[:m] if k) for m in range(len(PRODUCTS) + 1)]
PROD_RING = 3
PAIR_ADDED = {1: 2 * (TAPS - 1), 0: 4 * (TAPS - 1)}


def program(nc, w, w_small, consts, late, vecs, rows, gains, x, positions, cmp_w2, out):
    ctx = ExitStack()
    with ctx:
        def sb(name, shape, dt=F32):
            return ctx.enter_context(nc.sbuf_tensor(name, shape, dt))

        sems = {}

        def sem(name):
            if name not in sems:
                sems[name] = ctx.enter_context(nc.semaphore(name.replace("[", "_").replace("]", "")))
            return sems[name]

        ring = sb("ring", [P, RING, UNIT])
        cn = sb("cn", [P, NC_])
        vc = sb("vc", [P, NV_])
        rw = sb("rw", [P, NR_ - ROWS["b_v"]])
        wh, wl = sb("wh", [P, SPLITS, HALF], F32R), sb("wl", [P, SPLITS, HALF], F32R)
        hh, hl = sb("hh", [P, KD, S], F32R), sb("hl", [P, KD, S], F32R)
        wsh, wsl = sb("wsh", [P, KD, 38], F32R), sb("wsl", [P, KD, 38], F32R)
        w2s = sb("w2s", [P, 2, 2, DH])
        xa = sb("xa", [P, TT, D])
        xb = sb("xb", [P, TT, D])
        BIG = sb("BIG", [P, 24, S])
        QK = sb("QK", [P, 16, S])
        V = sb("V", [P, TT, 1024])
        Y = sb("Y", [P, 16, S])
        PB = sb("PB", [P, 8, 384])
        SM = sb("SM", [P, 3, 512])
        PTS = sb("PTS", [P, 2, 512])
        T1 = sb("T1", [P, 2, 512])
        T2 = sb("T2", [P, 2, 512])
        stat = sb("stat", [P, 48])
        tiny = sb("tiny", [P, 640])
        eps_t = sb("eps_t", [P, 2])
        PS = ctx.enter_context(nc.psum_tensor("PS", [P, 8, 512], F32))

        def c(name, a=0, b=None):
            o, n = C_AT[name]
            return cn[:, o + a:o + (n if b is None else b)]

        b_v = BIG[:, 20:24, :].rearrange("p a b -> p (a b)")[:, 0:ROWS["b_v"]]

        def v(name, i=0, n=1):
            o, _ = V_AT[name]
            return vc[:, o + i:o + i + n]

        def r(name, a=0, b=None):
            o, n = R_AT[name]
            b = n if b is None else b
            return b_v[:, a:b] if name == "b_v" else rw[:, o - ROWS["b_v"] + a:o - ROWS["b_v"] + b]

        ident = c("ident")
        block = ctx.enter_context(nc.Block())
        G, SC, PT, AV, DEEP = (0, 1), (2, 3), (4, 5), (6, 7), 4

        ssq, rms = stat[:, 0:16], stat[:, 16:32]
        lsum, nmax, fac = tiny[:, 0:44], tiny[:, 44:88], tiny[:, 88:132]
        gnsa = tiny[:, 132:168]
        lfa = tiny[:, 168:192]
        small = tiny[:, 192:236].rearrange("p (t c) -> p t c", t=TT)
        gt2 = tiny[:, 236:268].rearrange("p (t c) -> p t c", t=TT)
        lf2 = tiny[:, 268:284].rearrange("p (t c) -> p t c", t=TT)
        lfx = tiny[:, 284:300].rearrange("p (t c) -> p t c", t=TT)
        half_b = tiny[:, 300:324]
        nF, nM, floor, den = (tiny[:, 324 + 16 * i:340 + 16 * i] for i in range(4))
        dil = tiny[:, 388:420]
        cst = tiny[:, 420:480]
        mmax, msum = tiny[:, 480:496], tiny[:, 496:512]
        den2 = tiny[:, 512:528]
        flat2 = PB[:, 0:3, :].rearrange("p a b -> p (a b)")[:, 0:960].rearrange(
            "p (i j c) -> p i j c", i=2, j=16)
        PBF = PB[:, :, :].rearrange("p a b -> p (a b)")
        BR = PBF[:, 0:6 * S].rearrange("p (i c) -> p i c", i=2)
        YF = Y[:, :, :].rearrange("p a b -> p (a b)")
        xh = PBF[:, 0:TT * D].rearrange("p (t d) -> p t d", t=TT)
        gB = V[:, 0, :]
        wsm = T2[:, :, :].rearrange("p a b -> p (a b)")[:, 0:KD * 38]
        XF = xa[:, :, :].rearrange("p a b -> p (a b)")
        UP_DVE = YF[:, 0:4 * CONV_W].rearrange("p (i c) -> p i c", i=4)
        UP_POOL = XF[:, 0:CONV_POOL * CONV_W].rearrange("p (i c) -> p i c", i=CONV_POOL)
        PROD = XF[:, CONV_POOL * CONV_W:CONV_POOL * CONV_W + PROD_RING * S].rearrange(
            "p (i c) -> p i c", i=PROD_RING)
        CM = SM[:, 2, 0:384]
        cmpPT = T2[:, 0, :].rearrange("p (g q) -> p g q", g=2)
        CH = T2[:, 1, 0:128].rearrange("p (i k c) -> p i k c", i=2, k=2)
        cvv = T2[:, 1, 128:256]
        ckT = T2[:, 1, 256:272]
        foxr = T1[:, 0, 0:256]
        EB = PBF[:, 0:2048].rearrange("p (h i s) -> p h i s", h=2, i=4)
        WM = PBF[:, 2048:3072].rearrange("p (h s) -> p h s", h=2)
        diag = T1[:, 0, 0:2 * P].rearrange("p (t c) -> p t c", t=TT)
        GNU = SM[:, 0:2, :]
        erow = SM[:, 2, :]
        QKF = QK[:, :, :].rearrange("p a b -> p (a b)")
        RSH, RSG, XC = QKF[:, 2048:2304], QKF[:, 2560:3072], QKF[:, 3072:3584]
        QN, KN, ZC = BIG[:, 0:8, :], BIG[:, 8:16, :], BIG[:, 16:24, :]
        ZD, QR, LQ = QK[:, 0:4, :], QK[:, 4:8, :], QK[:, 8:14, :]
        KR = QK[:, 13:14, :]
        LS = PBF[:, 0:5 * S].rearrange("p (k q) -> p k q", k=5)
        RSL = T2[:, 0, :]
        MP = PBF[:, 0:2048].rearrange("p (h s) -> p h s", h=4)
        FT = Y[:, 12:16, :]
        F1 = Y[:, 0:8, :].rearrange("p (g a) q -> p g (a q)", g=4)
        _o = C_AT["nsa_bias"][0]
        ropes = [cn[:, _o + i * S:_o + (i + 1) * S] for i in range(6)]

        def up_in(i, a, b):
            return UP_POOL[:, i, a:b] if i < CONV_POOL else UP_DVE[:, i - CONV_POOL, a:b]

        def branch(i):
            return BR[:, i % 2, :]

        def flat(i, j):
            return flat2[:, i, j, :]

        def cmph(i, k, g):
            return CH[:, i, k, g * 15:(g + 1) * 15]

        def cmpP(t, g):
            return CM[:, (g * 2 + t) * 96:(g * 2 + t + 1) * 96]

        WIDE = [u for s, n in STREAM if s not in ("cmp", "w_p", "down", "even_out", "w_uq", "w_uk", "w_uv",
                                                  "w_fd", "odd_out")
                for u in range(FIRST[s], FIRST[s] + n)]
        G_AT = {u: i for i, u in enumerate(WIDE)}

        def read(u):
            n = G_AT[u]
            return sem(f"bank_free[{n % 2}]"), n // 2 + 1

        @block.sync
        def _(sp):
            for src, dst, name in ((x[:, 0], xa[:, 0, :], "x_in[0]"), (x[:, 1], xa[:, 1, :], "x_in[1]"),
                                   (consts[:, 0:P], ident, "ident_in"), (vecs, vc[:, :], "vecs_in")):
                nc.sync.dma_start(dst, src).then_inc(sem(name), 16)
            for s in range(RING):
                nc.sync.dma_start(ring[:, s, :], w[s]).then_inc(sem(f"unit_in[{s}]"), 16)
            nc.sync.dma_start(wsm, w_small).then_inc(sem("w_small_in"), 16)
            nc.sync.dma_start(w2s[:, :, :, :], cmp_w2).then_inc(sem("cmp_w2_in"), 16)
            n = ROWS["b_v"]
            nc.sync.dma_start(rw[:, :], rows[:, n:].broadcast_to([P, NR_ - n])).then_inc(sem("rows_in"), 16)
            nc.sync.dma_start(b_v, rows[:, 0:n].broadcast_to([P, n])).then_inc(sem("rows_in"), 16)

            def refill(u):
                v_ = u - RING
                if CMP0 <= v_ < CMP1:
                    sp.wait_ge(sem("cmp_units"), v_ - CMP0 + 1)
                else:
                    sp.wait_ge(sem("split_done"), half_at(v_) + 2)
                nc.sync.dma_start(ring[:, u % RING, :], w[u]).then_inc(sem(f"unit_in[{u % RING}]"), 16)

            for n in range(RING):
                refill(RING + n)
                a, b = P + (NC_ - P) * n // RING, P + (NC_ - P) * (n + 1) // RING
                nc.sync.dma_start(cn[:, a:b], consts[:, a:b]).then_inc(sem("consts_in"), 16)

            def refills(a, b, skipped):
                with sp.Fori(a // RING, b // RING) as i:
                    for s in range(RING):
                        sp.wait_ge(sem("split_done"), i * (2 * RING) + 2 * (s + 1 - RING - skipped))
                        nc.sync.dma_start(ring[:, s, :], w[bass.ds(i * RING + s, 1)].rearrange(
                            "o p n -> (o p) n")).then_inc(sem(f"unit_in[{s}]"), 16)

            first = CMP0 + RING
            turns = -(-(CMP1 + RING) // RING) * RING
            last = NU // RING * RING
            refills(2 * RING, first // RING * RING, 0)
            for u in range(first // RING * RING, turns):
                refill(u)
            refills(turns, last, CMP1 - CMP0)
            for u in range(last, NU):
                refill(u)
            for t in range(TT):
                sp.wait_ge(sem("out_ready"), t + 1)
                nc.sync.dma_start(out[t * P:(t + 1) * P, :], xb[:, t, :]).then_inc(sem("out_stored"), 16)
            sp.wait_ge(sem("out_stored"), 16 * TT)

        @block.tensor
        def _(pe):
            def unit_in(u):
                pe.wait_ge(sem(f"unit_in[{u % RING}]"), 16 * (u // RING + 1))
                return ring[:, u % RING, :]

            def mm(o, lhsT, rhs, start, stop):
                return nc.tensor.matmul(o, lhsT, rhs, start=start, stop=stop, skip_group_check=True)

            def g_bank(u):
                n = G_AT[u]
                if n >= 2:
                    pe.wait_ge(sem(f"bank_free[{n % 2}]"), n // 2)
                return PS[:, G[n % 2], :]

            def half_in(q):
                pe.wait_ge(sem("split_done"), q + 1)
                return wh[:, q % SPLITS, :], wl[:, q % SPLITS, :]

            def half_out(m):
                m.then_inc(sem("half_used"), 1)

            def three(o, lh, ll, rh, rl, start):
                mm(o, lh, rh, start, False)
                mm(o, lh, rl, False, False)
                return mm(o, ll, rh, False, True)

            def wide_b(u, parts=(0, 1)):
                o = g_bank(u) if 0 in parts else PS[:, G[G_AT[u] % 2], :]
                for half in parts:
                    a, b = half_in(half_at(u) + half)
                    for j in range(2):
                        for k in range(4):
                            c_ = slice(k * 256 + j * P, k * 256 + (j + 1) * P)
                            kk = 4 * half + k
                            act_in(kk)
                            m = three(o[:, j * S:(j + 1) * S], a[:, c_], b[:, c_], hh[:, kk, :], hl[:, kk, :],
                                      kk == 0 and j == 0)
                    half_out(m)

            def wide_a(u, split=None, parts=(0, 1)):
                o = g_bank(u) if 0 in parts else PS[:, G[G_AT[u] % 2], :]
                n = split or 256
                for half in parts:
                    a, b = half_in(half_at(u) + half)
                    for k in range(4):
                        kk, c_ = 4 * half + k, slice(k * 256, k * 256 + n)
                        act_in(kk)
                        for t in range(TT):
                            q = slice(t * P, (t + 1) * P)
                            m = three(o[:, t * n:(t + 1) * n], hh[:, kk, q], hl[:, kk, q], a[:, c_], b[:, c_],
                                      kk == 0 and t == 0)
                        if split:
                            c_ = slice(k * 256 + P, (k + 1) * 256)
                            m = three(o[:, S:2 * S], a[:, c_], b[:, c_], hh[:, kk, :], hl[:, kk, :], False)
                    half_out(m)

            acts = {"sem": None, "base": 0, "next": KD}

            def act_in(kk):
                if kk >= acts["next"]:
                    pe.wait_ge(sem(acts["sem"]), acts["base"] + kk + 1)
                    acts["next"] = kk + 1

            def activations(name, base):
                acts.update(sem=name, base=base, next=0)

            def norm_transposes(n):
                src = (xa, xb, xb, xa)[n]
                for t in range(TT):
                    pe.wait_ge(sem("diag_ready"), TT * n + t + 1)
                    for k in range(KD):
                        m = mm(PS[:, 2 + k // 2, (k % 2) * S + t * P:(k % 2) * S + (t + 1) * P],
                               src[:, t, k * P:(k + 1) * P], diag[:, t, :], True, True)
                m.then_inc(sem("rows_turned"), 1)

            def normed(n):
                activations("h_split", KD * n)

            def deep(first, a, b, bank):
                i0 = DEEP0[first]
                for k in range(a, b):
                    wh_, wl_ = half_in(half_of(first) + k)
                    pe.wait_ge(sem("deep_split"), i0 + k + 1)
                    for t in range(TT):
                        q = slice(t * P, (t + 1) * P)
                        for h in range(2):
                            c_ = slice(h * 512, (h + 1) * 512)
                            m = three(PS[:, bank + 2 * t + h, :], hh[:, k % 8, q], hl[:, k % 8, q], wh_[:, c_],
                                      wl_[:, c_], k == 0)
                    half_out(m)

            def smalls(a, n):
                act_in(KD - 1)
                pe.wait_ge(sem("w_small_split"), 1)
                for t in range(TT):
                    for k in range(KD):
                        q = slice(t * P, (t + 1) * P)
                        m = three(PS[:, SC[0], t * 64:t * 64 + n], hh[:, k, q], hl[:, k, q],
                                  wsh[:, k, a:a + n], wsl[:, k, a:a + n], k == 0)
                m.then_inc(sem("small_done"), 1)

            pe.wait_ge(sem("ident_in"), 16)
            norm_transposes(0)
            normed(0)
            for i in range(2):
                wide_b(i)
            smalls(0, 22)
            for i in range(2, 8):
                wide_b(i)
            wide_a(8, split=P)
            for i in range(9, 12):
                wide_a(i)

            pe.wait_ge(sem("consts_in"), 16 * RING)
            pe.wait_ge(sem("fox_logs"), 3)
            for half in range(2):
                for t in range(TT):
                    m = mm(PS[half * 64:half * 64 + 4, SC[0], 0:S], lfa[:, 16 + 4 * t:20 + 4 * t],
                           c("neg_upper", t * S, (t + 1) * S), t == 0, t == TT - 1)
            m.then_inc(sem("fox_rows"), 1)

            def cmp_hidden(i):
                pe.wait_ge(sem("flat_ready"), i + 1)
                for half in range(2):
                    u = FIRST["cmp"] + 2 * i + half
                    wt = unit_in(u)
                    for m_ in range(2):
                        for k in range(8):
                            j = 8 * half + k
                            m = mm(PS[:, PT[i], 32 * m_:32 * m_ + 30],
                                   wt[:, k * 256 + m_ * P:k * 256 + (m_ + 1) * P], flat(i, j),
                                   j == 0 and m_ == 0, j == 15)
                    m.then_inc(sem("cmp_units"), 1)

            def cmp_out(i):
                pe.wait_ge(sem("cmp_gelu"), i + 1)
                pe.wait_ge(sem("cmp_w2_in"), 16)
                for g in range(2):
                    for rep in range(3 if i else 1):
                        for k in range(2):
                            h = cmph(i, k, g)
                            if i == 0:
                                m = mm(PS[g * 64:g * 64 + 64, AV[0], 128:143], w2s[:, 0, k, :], h, k == 0, k == 1)
                            else:
                                m = mm(PS[32 * rep:32 * rep + 15, AV[1], 128 + g * 64:192 + g * 64], h,
                                       w2s[:, 1, k, :], k == 0, k == 1)
                m.then_inc(sem("cmp_done"), 1)

            def cmp_scores():
                pe.wait_ge(sem("cmp_kv"), 1)
                pe.wait_ge(*read(5))
                pe.wait_ge(*read(6))
                pe.wait_ge(sem("fox_rows_copied"), 2)
                for t in range(TT):
                    for h in range(6):
                        g = h // 3
                        m = mm(PS[:, SC[g], t * 96 + (h % 3) * 32:t * 96 + (h % 3) * 32 + 15],
                               QK[g * 64:g * 64 + 64, 10 + h % 3, t * P:(t + 1) * P],
                               ckT[g * 64:g * 64 + 64, 0:15], True, True)
                m.then_inc(sem("cmp_scores"), 1)

            def cmp_probs():
                pe.wait_ge(sem("cmp_probs"), 1)
                for t in range(TT):
                    for g in range(2):
                        m = nc.tensor.transpose(PS[0:96, PT[g], t * P:(t + 1) * P], cmpP(t, g), ident)
                m.then_inc(sem("cmp_probs_turned"), 1)

            def scores(j):
                kind, q, half, k, _, h = JOBS[j]
                last = 7 if kind in ("sel", "win") else 4
                pe.wait_ge(*read(last - 1))
                pe.wait_ge(*read(last))
                if j >= 2:
                    pe.wait_ge(sem("scores_read"), j - 1)
                else:
                    pe.wait_ge(sem("cmp_scores_read"), 1)
                if kind == "fox":
                    pe.wait_ge(sem("fox_rows_copied"), 2)
                b = SC[j % 2]
                lo = half * 64
                for t in range(TT):
                    o = PS[:, b, 0:P] if t == 0 else PS[:, b, P:P + S]
                    n = P * (t + 1)
                    m = mm(o, QK[lo:lo + 64, q, t * P:(t + 1) * P], QK[lo:lo + 64, k, 0:n],
                           True, kind != "fox")
                    if kind == "fox":
                        a, _ = C_AT["rows"]
                        m = mm(o, cn[lo:lo + 4, a + h * P:a + (h + 1) * P], foxr[lo:lo + 4, 0:n], False, True)
                m.then_inc(sem("scores"), 1)

            def turn(j):
                pe.wait_ge(sem("probs_scaled"), j + 1)
                if j >= 2:
                    pe.wait_ge(sem("probs_copied"), j - 1)
                else:
                    pe.wait_ge(sem("cmp_probs_copied"), 2)
                p, b = PB[:, j % 8, :], PT[j % 2]
                nc.tensor.transpose(PS[:, b, 0:P], p[:, 0:P], ident)
                nc.tensor.transpose(PS[:, b, P:2 * P], p[:, P:2 * P], ident)
                nc.tensor.transpose(PS[:, b, 2 * P:3 * P], p[:, 2 * P:3 * P], ident)\
                    .then_inc(sem("probs_turned"), 1)

            def pv(j):
                kind, _, half, _, col, h = JOBS[j]
                yt = Y_TILE[j]
                b, hb, copied = Y_PLACE[yt]
                pe.wait_ge(sem("y_copied"), copied) if copied else pe.wait_ge(sem("cmp_kv"), 2)
                bank = AV[b]
                lo = (h // 3 if kind in ("sel", "win") else h % 2) * 64
                o = PS[lo:lo + 64, bank, hb * S:(hb + 1) * S]
                first = kind != "win"
                if kind == "sel":
                    i = h % 3
                    pe.wait_ge(sem("cmp_probs_copied"), 2)
                    mm(o, cvv[32 * i:32 * i + 15, (h // 3) * 64:(h // 3 + 1) * 64],
                       cmpPT[32 * i:32 * i + 15, h // 3, :], True, False)
                    first = False
                for u in {"fox": (9,), "dil": (10, 11), "sel": (11,), "win": (8,)}[kind]:
                    pe.wait_ge(*read(u))
                pe.wait_ge(sem("probs_copied"), j + 1)
                mm(o, V[:, 0, col:col + DH], PTS[:, j % 2, 0:S], first, False)
                m = mm(PS[lo:lo + 64, bank, hb * S + P:(hb + 1) * S], V[:, 1, col:col + DH], PTS[:, j % 2, S:S + P], False,
                       kind != "sel")
                m.then_inc(sem("pv_done"), 1)

            def step(j):
                if j < NJ:
                    scores(j)
                if 0 <= j - PT_LAG < NJ:
                    turn(j - PT_LAG)
                if 0 <= j - PV_LAG < NJ:
                    pv(j - PV_LAG)

            cmp_hidden(0)
            cmp_hidden(1)
            wide_b(FIRST["gates"])
            cmp_out(0)
            wide_b(FIRST["gates"] + 1)
            cmp_out(1)
            wide_b(FIRST["gates"] + 2)
            cmp_scores()
            wide_b(FIRST["gates"] + 3)
            cmp_probs()
            for j in range(NJ + PV_LAG):
                for q in range(GATE_HALVES[j], GATE_HALVES[j + 1]):
                    wide_b(FIRST["gates"] + 4 + q // 2, (q % 2,))
                step(j)

            for i in range(8):
                a, b = half_in(half_of("w_p") + i)
                if i >= 2:
                    pe.wait_ge(sem("branches"), i - 1)
                o = (PS[:, 2 + 2 * (i % 2), 0:S], PS[:, 2 + 2 * (i % 2), S:2 * S], PS[:, 3 + 2 * (i % 2), 0:S])
                for s_, (k0, k1) in enumerate(((0, 2), (2, 5), (5, 8))):
                    for k in range(k0, k1):
                        if i == 0:
                            pe.wait_ge(sem("y_split"), 1 + [k in c_[1] for c_ in COPIES].index(True))
                        c_ = slice(k * P, (k + 1) * P)
                        m = three(o[s_], a[:, c_], b[:, c_], hh[:, k, :], hl[:, k, :], k == k0)
                half_out(m)
            activations("merged_split", 0)
            for i in range(4):
                wide_a(FIRST["w_o"] + i)

            norm_transposes(1)
            normed(1)
            for i in range(NF):
                wide_b(FIRST["up"] + i)
            deep("down", 0, NF, DEEP)

            norm_transposes(2)
            normed(2)
            for i in range(8):
                wide_b(FIRST["conv_in"] + i)
            smalls(22, 16)
            for i in range(4):
                wide_b(FIRST["qk"] + i)
            for i in range(4):
                wide_b(FIRST["z_a"] + i)
            wide_a(v_unit(0))

            pe.wait_ge(sem("lstm_logs"), 4)
            for d, (tri, f0, i0) in enumerate((("neg_upper", 0, 0), ("neg_lower", 4, 8))):
                for t in range(TT):
                    mm(PS[0:4, SC[1], d * S:(d + 1) * S], lf2[:, t, f0:f0 + 4], c(tri, t * S, (t + 1) * S),
                       t == 0, False)
                for t in range(TT):
                    m = mm(PS[0:4, SC[1], d * S + t * P:d * S + (t + 1) * P], gt2[:, t, i0:i0 + 4], ident,
                           False, t == TT - 1)
            for d, (tri, f0) in enumerate((("neg_upper", 0), ("neg_lower", 4))):
                for t in range(TT):
                    for j in range(TT):
                        m = mm(PS[:, SC[0], 128 + 8 * d + 4 * t:132 + 8 * d + 4 * t],
                               c(tri, j * S + t * P, j * S + (t + 1) * P), lf2[:, j, f0:f0 + 4],
                               j == 0, j == TT - 1)
            m.then_inc(sem("lstm_rows"), 1)

            def lstm_scores(h):
                pe.wait_ge(sem("lstm_rows_copied"), 2)
                pe.wait_ge(*read(FIRST["qk"] + h))
                if h >= 1:
                    pe.wait_ge(sem("lstm_decay_read"), 4 * h)
                a, _ = C_AT["rows"]
                mm(PS[:, SC[0], :], cn[0:4, a + h * P:a + (h + 1) * P], erow[0:4, :], True, True)\
                    .then_inc(sem("lstm_decay"), 1)
                if h >= 1:
                    pe.wait_ge(sem("lstm_scores_read"), 4 * h)
                for t in range(TT):
                    m = mm(PS[:, SC[1], t * S:(t + 1) * S], QK[:, 2 * h, t * P:(t + 1) * P],
                           QK[:, 2 * h + 1, :], True, True)
                m.then_inc(sem("lstm_scores"), 1)

            def lstm_turn(h):
                pe.wait_ge(sem("lstm_w"), h + 1)
                if h >= 1:
                    pe.wait_ge(sem("lstm_wT"), h)
                for t in range(TT):
                    for s in range(TT):
                        m = nc.tensor.transpose(PS[:, PT[0], s * S + t * P:s * S + (t + 1) * P],
                                                WM[:, h % 2, t * S + s * P:t * S + (s + 1) * P], ident)
                m.then_inc(sem("lstm_turned"), 1)

            def lstm_pv(h):
                pe.wait_ge(sem("lstm_wT"), h + 1)
                pe.wait_ge(*read(v_unit(h)))
                if h >= 1:
                    pe.wait_ge(sem("yb_done"), h)
                for e in range(2):
                    for s in range(TT):
                        m = mm(PS[:, AV[0], e * S:(e + 1) * S], V[:, s, h * 256 + e * P:h * 256 + (e + 1) * P],
                               PTS[:, h % 2, s * S:(s + 1) * S], s == 0, s == TT - 1)
                m.then_inc(sem("lstm_h"), 1)

            def lstm_var(h):
                pe.wait_ge(sem("lstm_sq"), h + 1)
                for e in range(2):
                    m = mm(PS[:, AV[1], 0:S], c("mean", P, 2 * P), T1[:, 0, e * S:(e + 1) * S], e == 0, e == 1)
                m.then_inc(sem("lstm_var"), 1)

            def gn(i):
                pe.wait_ge(sem("gn_u"), i + 1)
                if i >= 1:
                    pe.wait_ge(sem("gn_done"), i)
                mm(PS[:, PT[1], :], c("mean", 0, P), GNU[:, i % 2, :], True, True).then_inc(sem("gn_mean"), 1)

            def gn_var(i):
                pe.wait_ge(sem("gn_sq"), i + 1)
                mm(PS[:, PT[1], :], c("mean", 0, P), T2[:, 0, :], True, True).then_inc(sem("gn_var"), 1)

            parts = {"decay": lstm_scores, "turn": lstm_turn, "pv": lstm_pv, "var": lstm_var, "gn": gn,
                     "gn_var": gn_var}
            for i, step_ in enumerate(EVEN_STEPS):
                if i < EVEN_HALVES:
                    u = o_unit(0) + i // 2
                    (wide_a if (u - FIRST["v_o_z"]) % 3 == 0 else wide_b)(u, parts=(i % 2,))
                for kind, n in step_:
                    if kind == "deep":
                        if n == 0:
                            for u in (o_unit(3), z_unit(3)):
                                pe.wait_ge(*read(u))
                            pe.wait_ge(sem("lstm_decay_read"), 16)
                            pe.wait_ge(sem("lstm_scores_read"), 16)
                        deep("even_out", n * EVEN_EARLY, (n + 1) * EVEN_EARLY, 0)
                    elif kind in parts:
                        parts[kind](n)
            deep("even_out", EVEN_EARLY * 2, 16, 0)

            norm_transposes(3)
            normed(3)
            for i in range(3):
                wide_b(FIRST["lora"] + i)
            for i in range(2):
                wide_b(FIRST["f_in"] + i)
            pe.wait_ge(sem("lora_sq"), 1)
            for k in range(3):
                mm(PS[:, SC[0], 0:S], c("mean", 256, 384), LS[:, k, :], k == 0, k == 2)
            for k in range(2):
                m = mm(PS[:, SC[0], S:2 * S], c("mean", P, 2 * P), LS[:, 3 + k, :], k == 0, k == 1)
            m.then_inc(sem("lora_var"), 1)
            for i in range(4):
                wide_b(FIRST["z_c"] + i)
            for i in range(2):
                wide_b(FIRST["z_d"] + i)

            pe.wait_ge(sem("late_in"), 16)
            pe.wait_ge(sem("lora_rs"), 1)
            pe.wait_ge(*read(FIRST["f_in"]))
            pe.wait_ge(*read(FIRST["f_in"] + 1))
            for g in range(4):
                for t in range(TT):
                    n = 2 * g + t
                    if n % 2 == 0 and n >= 4:
                        pe.wait_ge(sem("fft1_copied"), n // 2 - 1)
                    m = mm(PS[:, SC[g % 2], t * S:(t + 1) * S], FT[:, g, t * P:(t + 1) * P], c("dft_ch"), True, True)
                m.then_inc(sem("fft1"), 1)
            for g in range(4):
                pe.wait_ge(sem("fft1_copied"), g + 1)
                o = PS[:, PT[g // 2], (g % 2) * S:(g % 2 + 1) * S]
                for t in range(TT):
                    mm(o, F1[:, g, t * S:t * S + P], c("dft_cos", t * S, (t + 1) * S), t == 0, False)
                for t in range(TT):
                    m = mm(o, F1[:, g, t * S + P:(t + 1) * S], c("dft_nsin", t * S, (t + 1) * S), False, t == 1)
                if g % 2:
                    m.then_inc(sem("fft2"), 1)
            def rope_swap(n, src):
                pe.wait_ge(*((sem(f"uq_read[{n}]"), 3) if n < 2 else read(FIRST["lora"] + 2)))
                if n >= 1:
                    pe.wait_ge(sem("rope_swapped_read"), n)
                w_ = 512 if n < 2 else 256
                mm(PS[:, SC[1], 0:w_], c("rope_swap"), src, True, True).then_inc(sem("rope_swapped"), 1)

            def uq_bank(n):
                if n < 2:
                    pe.wait_ge(sem("fft2_copied"), n + 1)
                else:
                    pe.wait_ge(sem(f"uq_read[{n % 2}]"), n // 2)

            pe.wait_ge(sem("lora_ready"), 5)
            for n in range(6):
                uq_bank(n)
                a, b = half_in(half_of("w_uq") + n)
                for j in range(2):
                    for k in range(3):
                        c_ = slice((3 * j + k) * P, (3 * j + k + 1) * P)
                        m = three(PS[:, PT[n % 2], j * S:(j + 1) * S], a[:, c_], b[:, c_], hh[:, k, :],
                                  hl[:, k, :], k == 0)
                half_out(m)
            rope_swap(0, QR[:, 0:2, :])
            for n in range(6, 10):
                uq_bank(n)
                if n % 2 == 0:
                    a, b = half_in(half_of("w_uk") + (n - 6) // 2)
                for j in range(2):
                    for k in range(2):
                        c_ = slice(((n % 2) * 4 + 2 * j + k) * P, ((n % 2) * 4 + 2 * j + k + 1) * P)
                        m = three(PS[:, PT[n % 2], j * S:(j + 1) * S], a[:, c_], b[:, c_], hh[:, 3 + k, :],
                                  hl[:, 3 + k, :], k == 0)
                m.then_inc(sem(UQ_DONE[n][0]), 1)
            rope_swap(1, QR[:, 2:4, :])
            for n in range(10, 14):
                uq_bank(n)
                t, h = n % 2, (n - 10) // 2
                if t == 0:
                    a, b = half_in(half_of("w_uv") + h)
                for k in range(2):
                    q, c_ = slice(t * P, (t + 1) * P), slice(k * 512, (k + 1) * 512)
                    m = three(PS[:, PT[n % 2], :], hh[:, 3 + k, q], hl[:, 3 + k, q], a[:, c_], b[:, c_], k == 0)
                m.then_inc(sem(UQ_DONE[n][0]), 1)
                if n == 11:
                    rope_swap(2, KR[:, 0, :])

            for half in range(2):
                a, b = half_in(half_of("w_fd") + half)
                pe.wait_ge(sem("fft2_split"), 2 * half + 2)
                for j in range(4):
                    for k in range(2):
                        kk, c_ = 2 * half + k, slice(k * 512 + j * P, k * 512 + (j + 1) * P)
                        m = three(PS[:, AV[j // 2], (j % 2) * S:(j % 2 + 1) * S], a[:, c_], b[:, c_],
                                  hh[:, (5 + kk) % 8, :],
                                  hl[:, (5 + kk) % 8, :], kk == 0 and j % 2 == 0)
                half_out(m)

            def mla_scores(h):
                if h == 0:
                    pe.wait_ge(sem("uq_read[0]"), 7)
                    pe.wait_ge(sem("uq_read[1]"), 7)
                    pe.wait_ge(sem("rope_ready"), 3)
                if h >= 2:
                    pe.wait_ge(sem("mla_probs"), 2 * (h - 1))
                lo = 64 * (h % 2)
                for t in range(TT):
                    mm(PS[:, SC[h % 2], t * S:(t + 1) * S], QN[:, h, t * P:(t + 1) * P], KN[:, h, :], True, False)
                    m = mm(PS[:, SC[h % 2], t * S:(t + 1) * S], QR[lo:lo + 64, h // 2, t * P:(t + 1) * P],
                           KR[lo:lo + 64, 0, :], False, True)
                m.then_inc(sem("mla_scores"), 1)

            def mla_turn(h):
                pe.wait_ge(sem("mla_scaled"), h + 1)
                if h >= 2:
                    pe.wait_ge(sem("mla_copied"), h - 1)
                for t in range(TT):
                    for s in range(TT):
                        m = nc.tensor.transpose(PS[:, PT[h % 2], s * S + t * P:s * S + (t + 1) * P],
                                                MP[:, h % 4, t * S + s * P:t * S + (s + 1) * P], ident)
                m.then_inc(sem("mla_turned"), 1)

            def mla_pv(h):
                pe.wait_ge(sem("mla_copied"), h + 1)
                if h < 2:
                    pe.wait_ge(sem("yd_done"), h + 1)
                else:
                    pe.wait_ge(sem("yc_done"), h - 1)
                for s in range(TT):
                    m = mm(PS[:, AV[h % 2], 0:S], V[:, s, h * P:(h + 1) * P], PTS[:, h % 2, s * S:(s + 1) * S],
                           s == 0, s == TT - 1)
                m.then_inc(sem("mla_out"), 1)

            for i in range(8 + 3):
                if i < 8:
                    mla_scores(i)
                if 2 <= i < 10:
                    mla_turn(i - 2)
                if i >= 3:
                    mla_pv(i - 3)

            pe.wait_ge(sem("yc_done"), 8)
            deep("odd_out", 0, 12, DEEP)

        def ahead(split_half):
            at = {"next": 0}

            def halves(n):
                for q in range(at["next"], min(n, HALVES)):
                    split_half(q)
                at["next"] = max(at["next"], min(n, HALVES))
            return halves

        def bank_of(u):
            return PS[:, G[G_AT[u] % 2], :]

        def freed(ins, u):
            return ins.then_inc(sem(f"bank_free[{G_AT[u] % 2}]"), 1)

        def cols2(ap, n=2):
            return ap.rearrange("p (t c) -> p t c", t=n)

        def uq_dest(n):
            if n < 4:
                return QN[:, 2 * n:2 * n + 2, :]
            if n < 6:
                return QR[:, 2 * n - 8:2 * n - 6, :]
            if n < 10:
                return KN[:, 2 * n - 12:2 * n - 10, :]
            return V[:, n % 2, (n - 10) // 2 * 512:((n - 10) // 2 + 1) * 512]

        def add_pe(eng, i):
            return eng.tensor_tensor(flat2[:, i], flat2[:, i], v("pe", 0, 16).unsqueeze(2).broadcast_to(
                [P, 16, 30]), ALU.add)

        @block.scalar
        def _(act):
            A = nc.scalar.activation

            def split_half(q):
                u = unit_of(q)
                act.wait_ge(sem(f"unit_in[{u % RING}]"), 16 * (u // RING + 1))
                if q >= SPLITS:
                    act.wait_ge(sem("half_used"), q + 1 - SPLITS)
                e = q % 2 * HALF
                A(wh[:, q % SPLITS, :], ring[:, u % RING, e:e + HALF], ACT.Copy).then_inc(sem("hi_ready"), 1)

            halves = ahead(split_half)

            def multiplied(q):
                halves(q + SPLITS)
                act.wait_ge(sem("half_used"), q + 1)
                halves(q + SPLITS + 1)

            def unit(u):
                multiplied(half_at(u) + 1)

            def high(k, src, name, **scale):
                A(hh[:, k, :], src, ACT.Copy, **scale).then_inc(sem(name), 1)

            def deep_high(first, buf, tiles, k):
                if k >= 8:
                    act.wait_ge(sem("half_used"), half_of(first) + k - 7)
                high(k % 8, buf[:, tiles[k], :], "deep_hi")

            def root_table(m):
                A(stat[:, 32 + m:33 + m], eps_t[:, 0:1], ACT.Sqrt)

            def row_root(m, t):
                A(rms[:, TT * m + t:TT * m + t + 1], ssq[:, TT * m + t:TT * m + t + 1], ACT.Sqrt,
                  bias=eps_t[:, 0:1]).then_inc(sem(f"row_rms[{t}]"), 1)

            def row_stat(m, t, src):
                A(cols2(xh[:, t, :]), src, ACT.Square, scale=D ** -0.5,
                  accum_out=ssq[:, TT * m + t:TT * m + t + 1]).then_inc(sem(f"row_ssq[{t}]"), 1)
                act.wait_ge(sem(f"row_ssq[{t}]"), m + 1)
                row_root(m, t)

            def row_stats(m, src, name=None):
                if name:
                    act.wait_ge(sem(name), 1)
                row_stat(m, 0, cols2(src[:, 0, :]))
                act.wait_ge(sem("row_ssq[1]"), m + 1)
                row_root(m, 1)

            def turned_evac(n, gain):
                act.wait_ge(sem("rows_turned"), n + 1)
                for k in range(KD):
                    high(k, PS[:, 2 + k // 2, (k % 2) * S:(k % 2 + 1) * S], "h_hi", scale=v(gain, k))

            def flat_copies(i, u, col, bias):
                b = G[G_AT[u] % 2]
                for g in range(2):
                    src = PS[g * 64:g * 64 + 64, b, col:col + S].rearrange("p (c j r) -> p j c r", c=16, j=8)
                    for par in range(2):
                        for a in range(2):
                            ins = A(flat2[par * 64:par * 64 + 64, i, a * 8:a * 8 + 8, g * 15:g * 15 + 15],
                                    src[:, :, a:a + 15, par], ACT.Identity,
                                    bias=v("b_feat", bias)[g * 64:g * 64 + 64, :])
                return ins

            act.wait_ge(sem("eps_set"), 2)
            root_table(0)
            act.wait_ge(sem("x_in[0]"), 16)
            row_stats(0, xa)
            halves(SPLITS)
            act.wait_ge(sem("vecs_in"), 16)
            turned_evac(0, "g1")
            act.wait_ge(sem("w_small_in"), 16)
            A(wsh[:, :, :], cols2(wsm, KD), ACT.Copy).then_inc(sem("w_small_hi"), 1)
            unit(0)
            for j in range(2):
                ins = A(QK[:, j, :], bank_of(0)[:, j * S:(j + 1) * S], ACT.Identity, bias=v("b_feat", j))
            freed(ins, 0)
            unit(1)
            act.wait_ge(sem("fox_logs"), 1)
            e1 = lfa[:, 0:8]
            A(e1, e1, ACT.Exp, scale=-1.0).then_inc(sem("fox_exp"), 1)
            act.wait_ge(sem("fox_exp"), 1)
            A(e1, e1, ACT.Ln, bias=1.0).then_inc(sem("fox_exp"), 1)
            A(cols2(gnsa), small[:, :, 4:22], ACT.Tanh, scale=0.5).then_inc(sem("nsa_tanh"), 1)

            for i in range(1, 7):
                unit(i)
                for j in range(2):
                    ins = A(QK[:, 2 * i + j, :], bank_of(i)[:, j * S:(j + 1) * S], ACT.Identity,
                            bias=v("b_feat", 2 * i + j))
                freed(ins, i)
            unit(7)
            A(QK[:, 14, :], bank_of(7)[:, 0:S], ACT.Identity, bias=v("b_feat", 14))
            freed(flat_copies(0, 7, S, 15), 7)
            unit(8)
            flat_copies(1, 8, S, 16).then_inc(sem("vc_flat"), 1)
            for i in range(9, 12):
                unit(i)
            act.wait_ge(sem("fox_rows"), 1)
            for half in range(2):
                lo = 64 * half
                A(foxr[lo:lo + 4, :], PS[lo:lo + 4, SC[0], 0:S], ACT.Copy).then_inc(sem("fox_rows_copied"), 1)

            def gate(i):
                unit(FIRST["gates"] + i)
                gate_read(i)

            def gate_read(i):
                u = FIRST["gates"] + i
                for j in range(2):
                    ins = A(BIG[:, 2 * i + j, :], bank_of(u)[:, j * S:(j + 1) * S], ACT.Tanh, scale=0.5,
                            bias=half_b[:, 2 * i + j:2 * i + j + 1])
                freed(ins, u)

            def cmp_gelu(i):
                act.wait_ge(sem("cmp_units"), 2 * i + 2)
                A(CH[:, i, :, 0:30], cols2(PS[:, PT[i], 0:64])[:, :, 0:30], ACT.Gelu_apprx_tanh)\
                    .then_inc(sem("cmp_gelu"), 1)

            def cmp_kv(i):
                act.wait_ge(sem("cmp_done"), i + 1)
                if i == 0:
                    ins = A(ckT[:, 0:15], PS[:, AV[0], 128:143], ACT.Copy)
                else:
                    for rep in range(3):
                        ins = A(cvv[32 * rep:32 * rep + 15, :], PS[32 * rep:32 * rep + 15, AV[1], 128:256],
                                ACT.Copy)
                ins.then_inc(sem("cmp_kv"), 1)

            act.wait_ge(sem("half_bias"), 1)
            halves(half_of("gates") + SPLITS)
            cmp_gelu(0)
            cmp_gelu(1)
            cmp_kv(0)
            gate(0)
            cmp_kv(1)
            gate(1)
            gate(2)
            act.wait_ge(sem("cmp_centred"), 1)
            cm12 = cols2(CM, 12)[:, :, 0:15]
            A(cm12, cm12, ACT.Exp).then_inc(sem("cmp_exp"), 1)
            gate(3)
            act.wait_ge(sem("cmp_probs_turned"), 1)
            for g in range(2):
                A(cmpPT[0:96, g, :], PS[0:96, PT[g], 0:S], ACT.Copy).then_inc(sem("cmp_probs_copied"), 1)

            def exp_job(j):
                act.wait_ge(sem("scores_read"), j + 1)
                if j >= 8:
                    act.wait_ge(sem("probs_turned"), j - 7)
                for t in range(TT):
                    a, b = (0, P) if t == 0 else (P, 3 * P)
                    A(PB[:, j % 8, a:b], SM[:, j % 3, a:b], ACT.Exp, scale=-1.0,
                      bias=nmax[:, 2 * j + t:2 * j + t + 1],
                      accum_out=lsum[:, 2 * j + t:2 * j + t + 1]).then_inc(sem("att_exp"), 1)

            def dil_exp(n):
                act.wait_ge(sem("dil_diff"), n + 1)
                A(dil[:, 0:6], dil[:, 0:6], ACT.Exp).then_inc(sem("dil_exp"), 1)

            def probs_copy(j):
                act.wait_ge(sem("probs_turned"), j + 1)
                if j >= 2:
                    act.wait_ge(sem("pv_done"), j - 1)
                A(PTS[:, j % 2, 0:384], PS[:, PT[j % 2], 0:384], ACT.Copy).then_inc(sem("probs_copied"), 1)

            for j in range(NJ + PV_LAG):
                if 0 <= j - PT_LAG < NJ:
                    probs_copy(j - PT_LAG)
                if j < NJ:
                    exp_job(j)
                    if j in (6, 9):
                        dil_exp((j - 6) // 3)
                for q in range(GATE_HALVES[j], GATE_HALVES[j + 1]):
                    multiplied(half_of("gates") + 8 + q)
                    if q % 2:
                        gate_read(4 + q // 2)
                for n in Y_SPLIT_AT.get(j, ()):
                    act.wait_ge(sem("y_copied"), n + 1)
                    a, b = COPIES[n][1][0], COPIES[n][1][-1] + 1
                    A(hh[:, a:b, :], Y[:, a:b, :], ACT.Copy).then_inc(sem("y_hi"), 1)
            act.wait_ge(sem("scores_read"), NJ)
            nc.scalar.dma_start(cn[:, C_AT["dil_bias"][0]:C_AT["dil_bias"][0] + NL_], late).then_inc(sem("late_in"), 16)
            nc.scalar.dma_start(ropes[5].bitcast(I32), positions.broadcast_to([P, S]))\
                .then_inc(sem("positions_in"), 16)

            nc.scalar.dma_start(gB[:, :], gains[0:1, :].broadcast_to([P, D])).then_inc(sem("gains_in"), 16)
            multiplied(half_of("w_p") + 7)
            for k in range(KD):
                act.wait_ge(sem("merged"), k + 1)
                high(k, Y[:, 8 + k, :], "merged_hi")
            for i in range(4):
                if i == 3:
                    root_table(1)
                    halves(half_of("w_o") + 7 + SPLITS)
                else:
                    unit(FIRST["w_o"] + i)
            for i in range(2):
                act.wait_ge(*read(FIRST["w_o"] + 2 + i))
            row_stats(1, xb)
            halves(half_of("up") + SPLITS)
            turned_evac(1, "g2")
            CV = T2
            for i in range(NF):
                u = FIRST["up"] + i
                unit(u)
                if i == NF - 1:
                    act.wait_ge(*read(FIRST["up"] + DOWN_EARLY - 2))
                    act.wait_ge(*read(FIRST["up"] + DOWN_EARLY - 1))
                    for k in range(DOWN_EARLY):
                        deep_high("down", BIG, DOWN, k)
                A(CV[:, i % 2, 0:S], bank_of(u)[:, 0:S], ACT.Identity, scale=v("conv_w", 2 * NF + i),
                  bias=v("conv_b", i)).then_inc(sem("ffn_tap"), 1)
                act.wait_ge(sem("ffn_conv"), i + 1)
                A(CV[:, i % 2, S:2 * S], CV[:, i % 2, 0:S], ACT.Gelu_apprx_tanh).then_inc(sem("ffn_gelu"), 1)
            for k in range(DOWN_EARLY, NF):
                if k == DOWN_EARLY:
                    for i in range(2):
                        act.wait_ge(*read(FIRST["up"] + NF - 2 + i))
                deep_high("down", BIG, DOWN, k)
                halves(half_of("down") + k + 1)
                if k == 16:
                    act.wait_ge(sem("angles"), 1)
                    A(ropes[0], ropes[0], ACT.Sin).then_inc(sem("rope_tables"), 1)
                    A(ropes[1], ropes[1], ACT.Sin).then_inc(sem("rope_tables"), 1)
            root_table(2)
            halves(half_of("down") + NF - 1 + SPLITS)
            act.wait_ge(sem("half_used"), half_of("down") + NF - 1 + 1)
            row_stats(2, xa, "x2_ready")
            row_stats(3, xb, "x3_ready")
            halves(half_of("conv_in") + SPLITS)

            turned_evac(2, "g3")

            def products(a, b):
                for m in range(a, b):
                    i, k = PRODUCTS[m]
                    act.wait_ge(*read(FIRST["conv_in"] + i))
                    e = ADDED[m]
                    if k and e >= PROD_RING:
                        act.wait_ge(sem("prod_added"), e - PROD_RING + 1)
                    A(PROD[:, e % PROD_RING, :] if k else BIG[:, 16 + i, :], up_in(i, k, k + S), ACT.Copy,
                      scale=v("taps", i * TAPS + k)).then_inc(sem("prod_ready"), 1)

            def gate_logs():
                act.wait_ge(sem("lstm_logs"), 2)
                A(lfx, lfx, ACT.Exp, scale=-1.0).then_inc(sem("lstm_exp"), 1)
                act.wait_ge(sem("lstm_exp"), 1)
                A(lfx, lfx, ACT.Ln, bias=1.0).then_inc(sem("lstm_exp"), 1)

            act.wait_ge(sem("conv_pads"), 4)
            units = v_unit(0) + 1 - FIRST["conv_in"]
            total = 2 * (units - 4)
            for n in range(units):
                u = FIRST["conv_in"] + n
                for half in range(2):
                    multiplied(half_at(u) + half)
                    if half:
                        b = bank_of(u)
                        if n < 8:
                            A(T1[:, n % 2, 0:S], b[:, S:2 * S], ACT.Tanh, scale=0.5).then_inc(sem("a_gate"), 1)
                        elif n < 12:
                            i = n - 8
                            freed(A(QK[:, 2 * i:2 * i + 2, :], cols2(b), ACT.Copy), u)
                        elif n < 16:
                            i = n - 12
                            freed(A(BIG[:, 2 * i:2 * i + 2, :], cols2(b), ACT.Silu), u)
                        else:
                            freed(A(V[:, :, 0:256], cols2(b), ACT.Copy), u)
                    if n >= 4:
                        q = 2 * (n - 4) + half
                        products(len(PRODUCTS) * q // total, len(PRODUCTS) * (q + 1) // total)
                if n == 9:
                    gate_logs()
            act.wait_ge(sem("lstm_rows"), 1)
            A(erow[0:4, :], PS[0:4, SC[1], :], ACT.Copy).then_inc(sem("lstm_rows_copied"), 1)
            A(nF, PS[:, SC[0], 128:144], ACT.Copy).then_inc(sem("lstm_rows_copied"), 1)

            def even_evac(u):
                h, kind = divmod(u - FIRST["v_o_z"], 3)
                if kind == 0:
                    freed(A(V[:, :, h * 256:(h + 1) * 256], cols2(bank_of(u)), ACT.Copy), u)
                elif kind == 1:
                    freed(A(BIG[:, 8 + 2 * h:10 + 2 * h, :], cols2(bank_of(u)), ACT.Tanh, scale=0.5), u)
                else:
                    if h:
                        act.wait_ge(sem("oz_ready"), h)
                    A(T1[:, 1, :], bank_of(u), ACT.Tanh, scale=0.5).then_inc(sem("zb_tanh"), 1)

            for i, step_ in enumerate(EVEN_STEPS):
                if i < EVEN_HALVES:
                    multiplied(half_at(o_unit(0)) + i)
                    if i % 2:
                        even_evac(o_unit(0) + i // 2)
                for kind, n in step_:
                    if kind == "decay":
                        for q, (a, b) in enumerate(LSTM_COLS):
                            act.wait_ge(sem("lstm_decay_read"), 4 * n + q + 1)
                            A(EB[:, n % 2, q, a:b], EB[:, n % 2, q, a:b], ACT.Exp, scale=-1.0,
                              bias=nM[:, 4 * n + q:4 * n + q + 1]).then_inc(sem("lstm_dw"), 1)
                        act.wait_ge(sem("lstm_arg"), n + 1)
                        A(floor[:, 4 * n:4 * n + 4], floor[:, 4 * n:4 * n + 4], ACT.Exp)\
                            .then_inc(sem("lstm_floor"), 1)
                    elif kind == "turn":
                        act.wait_ge(sem("lstm_turned"), n + 1)
                        A(PTS[:, n % 2, :], PS[:, PT[0], :], ACT.Copy).then_inc(sem("lstm_wT"), 1)
                    elif kind == "pv":
                        act.wait_ge(sem("lstm_h"), n + 1)
                        A(T1[:, 0, :], PS[:, AV[0], :], ACT.Square).then_inc(sem("lstm_sq"), 1)
                    elif kind == "var":
                        act.wait_ge(sem("lstm_var"), n + 1)
                        A(RSH, PS[:, AV[1], 0:S], ACT.Ln, bias=eps_t[:, 0:1]).then_inc(sem("lstm_rs"), 1)
                        act.wait_ge(sem("gn_var"), n + 1)
                        A(RSG, PS[:, PT[1], :], ACT.Ln, bias=eps_t[:, 1:2]).then_inc(sem("gn_rs"), 1)
                        act.wait_ge(sem("lstm_rs"), 2 * n + 1)
                        A(RSH, RSH, ACT.Exp, scale=-0.5).then_inc(sem("lstm_rs"), 1)
                        act.wait_ge(sem("gn_rs"), 2 * n + 1)
                        A(RSG, RSG, ACT.Exp, scale=-0.5).then_inc(sem("gn_rs"), 1)
                    elif kind == "gn":
                        act.wait_ge(sem("gn_xc"), n + 1)
                        A(T2[:, 0, :], XC, ACT.Square).then_inc(sem("gn_sq"), 1)
                    elif kind == "gn_x":
                        act.wait_ge(sem("gn_xg"), n + 1)
                        A(T2[:, 1, :], XC, ACT.Tanh, scale=0.5).then_inc(sem("gn_tanh"), 1)
                    elif kind == "deep":
                        halves(half_of("even_out") + (n + 1) * EVEN_EARLY + SPLITS)
                    elif kind == "split":
                        act.wait_ge(sem("gn_done"), 3)
                        act.wait_ge(sem("yb_done"), 3)
                        for k in range(4 * n, 4 * n + 4):
                            deep_high("even_out", Y, EVEN_OUT, k)
            nc.scalar.dma_start(gB[:, :], gains[1:2, :].broadcast_to([P, D])).then_inc(sem("gains_in"), 16)
            for k in range(8, 16):
                if k == 12:
                    act.wait_ge(sem("gn_done"), 4)
                    act.wait_ge(sem("yb_done"), 4)
                deep_high("even_out", Y, EVEN_OUT, k)
                halves(half_of("even_out") + k + 1)
            root_table(4)
            halves(half_of("even_out") + 15 + SPLITS)
            act.wait_ge(sem("half_used"), half_of("even_out") + 15 + 1)
            for t in range(TT):
                row_stat(4, t, PS[:, 2 * t:2 * t + 2, :])
            row_stats(5, xa, "x4_ready")
            halves(half_of("lora") + SPLITS)

            turned_evac(3, "g4")
            for i in range(3):
                u = FIRST["lora"] + i
                unit(u)
                freed(A(LQ[:, 2 * i:2 * i + 2, :], cols2(bank_of(u)), ACT.Copy), u)
            act.wait_ge(*read(FIRST["lora"] + 1))
            act.wait_ge(*read(FIRST["lora"] + 2))
            A(LS, LQ[:, 0:5, :], ACT.Square).then_inc(sem("lora_sq"), 1)
            for i in range(2):
                u = FIRST["f_in"] + i
                unit(u)
                freed(A(FT[:, 2 * i:2 * i + 2, :], cols2(bank_of(u)), ACT.Copy), u)
            act.wait_ge(sem("lora_var"), 1)
            A(RSL, PS[:, SC[0], :], ACT.Ln, bias=eps_t[:, 0:1]).then_inc(sem("lora_rs"), 1)
            act.wait_ge(sem("lora_rs"), 1)
            A(RSL, RSL, ACT.Exp, scale=-0.5).then_inc(sem("lora_rs"), 1)
            for i in range(6):
                u = FIRST["z_c"] + i
                unit(u)
                A(T1[:, i % 2, :], bank_of(u), ACT.Tanh, scale=0.5).then_inc(sem("zcd_tanh"), 1)
            for g in range(4):
                act.wait_ge(sem("fft1"), g + 1)
                A(F1[:, g, :], PS[:, SC[g % 2], :], ACT.Copy).then_inc(sem("fft1_copied"), 1)
            for k in range(5):
                act.wait_ge(sem("lora_scaled"), k + 1)
                high(k, LQ[:, k, :], "lora_hi")
            for n in range(0, 14, 2):
                halves(UQ_HALF[n] + SPLITS)
                name, value = UQ_DONE[n]
                act.wait_ge(sem(name), value)
                A(uq_dest(n), cols2(PS[:, PT[0], :]) if n < 10 else PS[:, PT[0], :], ACT.Copy)\
                    .then_inc(sem("uq_read[0]"), 1)
                if n == 6:
                    act.wait_ge(sem("fft2_copied"), 2)
                    for k in range(4):
                        high((5 + k) % 8, Y[:, 8 + k, :], "fft2_hi")
            halves(half_of("odd_out") + SPLITS)

            for i in range(8 + 3):
                if i < 8:
                    act.wait_ge(sem("mla_max"), i + 1)
                    if i >= 4:
                        act.wait_ge(sem("mla_turned"), i - 3)
                    for t in range(TT):
                        A(MP[:, i % 4, t * S:(t + 1) * S], PS[:, SC[i % 2], t * S:(t + 1) * S], ACT.Exp,
                          scale=MLA_SCALE, bias=mmax[:, 2 * i + t:2 * i + t + 1],
                          accum_out=msum[:, 2 * i + t:2 * i + t + 1]).then_inc(sem("mla_probs"), 1)
                if 2 <= i < 10:
                    h = i - 2
                    act.wait_ge(sem("mla_turned"), h + 1)
                    if h >= 2:
                        act.wait_ge(sem("mla_out"), h - 1)
                    A(PTS[:, h % 2, :], PS[:, PT[h % 2], :], ACT.Copy).then_inc(sem("mla_copied"), 1)
                if i < 4:
                    act.wait_ge(sem("yd_done"), 2)
                    deep_high("odd_out", Y, ODD_OUT, i)
                elif i < 8:
                    act.wait_ge(sem("yc_done"), i - 3)
                    deep_high("odd_out", Y, ODD_OUT, i)
            act.wait_ge(sem("mla_out"), 8)
            nc.scalar.dma_start(gB[:, :], gains[2:3, :].broadcast_to([P, D])).then_inc(sem("gains_in"), 16)
            for k in range(8, 12):
                act.wait_ge(sem("yc_done"), k - 3)
                deep_high("odd_out", Y, ODD_OUT, k)
                halves(half_of("odd_out") + k + 1)
            root_table(6)
            multiplied(half_of("odd_out") + 11)
            for t in range(TT):
                row_stat(6, t, PS[:, DEEP + 2 * t:DEEP + 2 * t + 2, :])

        @block.vector
        def _(dve):
            TTn, TS, STT = nc.vector.tensor_tensor, nc.vector.tensor_scalar, nc.vector.scalar_tensor_tensor
            steps = {"n": 0}

            def own(ins):
                steps["n"] += 1
                return ins.then_inc(sem("dve_step"), 1)

            def settled():
                dve.wait_ge(sem("dve_step"), steps["n"])

            def split_half(q):
                dve.wait_ge(sem("hi_ready"), q + 1)
                e = q % 2 * HALF
                TTn(wl[:, q % SPLITS, :], ring[:, unit_of(q) % RING, e:e + HALF],
                    wh[:, q % SPLITS, :].bitcast(F32), ALU.subtract).then_inc(sem("split_done"), 1)

            halves = ahead(split_half)

            def multiplied(q):
                halves(q + SPLITS)
                dve.wait_ge(sem("half_used"), q + 1)
                halves(q + SPLITS + 1)

            def unit(u):
                multiplied(half_at(u) + 1)

            def keep_up(u):
                halves(half_at(u) + SPLITS + 2)

            def low(k, src, hi, i, name):
                dve.wait_ge(sem(hi), i + 1)
                TTn(hl[:, k, :], src, hh[:, k, :].bitcast(F32), ALU.subtract).then_inc(sem(name), 1)

            def deep_low(first, buf, tiles, k):
                low(k % 8, buf[:, tiles[k], :], "deep_hi", DEEP0[first] + k, "deep_split")

            def row_rstd(m, t):
                dve.wait_ge(sem(f"row_rms[{t}]"), m + 1)
                q = rms[:, TT * m + t:TT * m + t + 1]
                own(nc.vector.reciprocal(q, q))
                settled()
                return q

            def row_squares(m, src):
                nc.vector.tensor_tensor_reduce(
                    xh[:, 1, :], src[:, 1, :], src[:, 1, :], 1 / D, 0.0, ALU.mult, ALU.add,
                    ssq[:, TT * m + 1:TT * m + 2]).then_inc(sem("row_ssq[1]"), 1)

            def scales(m):
                for t in range(TT):
                    TS(diag[:, t, :], ident, row_rstd(m, t), None, ALU.mult).then_inc(sem("diag_ready"), 1)

            def turned_evac(n, gain):
                for k in range(KD):
                    dve.wait_ge(sem("h_hi"), KD * n + k // 2 * 2 + 2)
                    STT(hl[:, k, :], PS[:, 2 + k // 2, (k % 2) * S:(k % 2 + 1) * S], v(gain, k),
                        hh[:, k, :].bitcast(F32), ALU.mult, ALU.subtract).then_inc(sem("h_split"), 1)

            nc.vector.memset(eps_t[:, 0:1], EPS).then_inc(sem("eps_set"), 1)
            nc.vector.memset(eps_t[:, 1:2], LN_EPS).then_inc(sem("eps_set"), 1)
            dve.wait_ge(sem("x_in[1]"), 16)
            row_squares(0, xa)
            dve.wait_ge(sem("ident_in"), 16)
            scales(0)
            halves(SPLITS)
            dve.wait_ge(sem("vecs_in"), 16)
            turned_evac(0, "g1")
            dve.wait_ge(sem("w_small_hi"), 1)
            TTn(wsl[:, :, :], cols2(wsm, KD), wsh[:, :, :].bitcast(F32), ALU.subtract)\
                .then_inc(sem("w_small_split"), 1)
            TS(half_b, v("b_gates", 0, 24), 0.5, None, ALU.mult).then_inc(sem("half_bias"), 1)
            keep_up(0)
            keep_up(1)
            dve.wait_ge(sem("small_done"), 1)
            dve.wait_ge(sem("rows_in"), 32)
            own(TTn(small, cols2(PS[:, SC[0], 0:128])[:, :, 0:22],
                    r("b_small").unsqueeze(1).broadcast_to([P, TT, 22]), ALU.add))
            settled()
            f = small[:, :, 0:4]
            STT(cols2(lfa[:, 0:8]), f, -1.0, f, ALU.mult, ALU.max).then_inc(sem("fox_logs"), 1)
            dve.wait_ge(sem("fox_exp"), 2)
            STT(cols2(lfa[:, 8:16]), f, 0.0, cols2(lfa[:, 0:8]), ALU.min, ALU.subtract).then_inc(sem("fox_logs"), 1)
            dve.wait_ge(sem("fox_logs"), 2)
            TS(lfa[:, 16:24], lfa[:, 8:16], 8.0, None, ALU.mult).then_inc(sem("fox_logs"), 1)
            dve.wait_ge(sem("nsa_tanh"), 1)
            TS(gnsa, gnsa, 1.0, 0.5, ALU.add, ALU.mult).then_inc(sem("nsa_gates"), 1)

            for i in range(8, 12):
                unit(i)
                if i == 8:
                    dve.wait_ge(sem("vc_flat"), 1)
                a, n = (768, 128) if i == 8 else (256 * (i - 9), 256)
                b = cols2(bank_of(i)[:, 0:2 * n])
                freed(TTn(V[:, :, a:a + n], b, r("b_v", a, a + n).unsqueeze(1).broadcast_to([P, TT, n]),
                          ALU.add), i)
                if i == 8:
                    dve.wait_ge(*read(7))
                    for q in range(2):
                        add_pe(nc.vector, q).then_inc(sem("flat_ready"), 1)

            for i in range(3):
                keep_up(FIRST["gates"] + i)
            dve.wait_ge(sem("cmp_scores"), 1)
            dve.wait_ge(sem("consts_in"), 16 * RING)
            dve.wait_ge(sem("cm_zero"), 1)
            for g in range(2):
                view = [cols2(q, 6)[:, :, 0:15] for q in
                        (CM[:, g * 192:g * 192 + 192], PS[:, SC[g], 0:192], c("cmp_bias", g * 192, g * 192 + 192))]
                STT(view[0], view[1], DH ** -0.5, view[2], ALU.mult, ALU.add).then_inc(sem("cmp_scores_read"), 1)
            dve.wait_ge(sem("cmp_scores_read"), 2)
            cm12 = cols2(CM, 12)[:, :, 0:15]
            own(nc.vector.tensor_reduce(cst[:, 0:12], cm12, AX.X, ALU.max))
            settled()
            TTn(cm12, cm12, cst[:, 0:12].unsqueeze(2).broadcast_to([P, 12, 15]), ALU.subtract)\
                .then_inc(sem("cmp_centred"), 1)
            dve.wait_ge(sem("cmp_exp"), 1)
            own(TTn(cm12, cm12, cols2(c("cmp_mask"), 12)[:, :, 0:15], ALU.mult))
            settled()
            own(nc.vector.tensor_reduce(cst[:, 12:24], cm12, AX.X, ALU.add))
            settled()
            own(TS(cst[:, 12:24], cst[:, 12:24], 1e-30, None, ALU.max))
            settled()
            own(nc.vector.reciprocal(cst[:, 24:36], cst[:, 12:24]))
            settled()
            gates3 = cols2(gnsa).rearrange("p t (h b) -> p t h b", b=3)
            dve.wait_ge(sem("nsa_gates"), 1)
            for g in range(2):
                own(TTn(cols2(cst[:, 36 + 6 * g:42 + 6 * g]), cols2(cst[:, 24 + 6 * g:30 + 6 * g]),
                        gates3[:, :, 3 * g:3 * g + 3, 0], ALU.mult))
            settled()
            TTn(cm12, cm12, cst[:, 36:48].unsqueeze(2).broadcast_to([P, 12, 15]), ALU.mult)\
                .then_inc(sem("cmp_probs"), 1)

            def scores_in(j):
                kind, h = JOBS[j][0], JOBS[j][5]
                dve.wait_ge(sem("scores"), j + 1)
                if j >= 3:
                    dve.wait_ge(sem("att_exp"), 2 * (j - 2))
                tab = "causal" if kind == "fox" else "dil_bias" if kind == "dil" else "nsa_bias"
                o = 0 if kind == "fox" else h * S
                for t in range(TT):
                    a, b, q = (0, P, o + P) if t == 0 else (P, 3 * P, o)
                    ins = nc.vector.tensor_tensor_reduce(
                        SM[:, j % 3, a:b], PS[:, SC[j % 2], a:b], c(tab, q, q + b - a), -DH ** -0.5, 3e38,
                        ALU.add, ALU.min, nmax[:, 2 * j + t:2 * j + t + 1])
                ins.then_inc(sem("scores_read"), 1)

            def factor(j):
                kind, h = JOBS[j][0], JOBS[j][5]
                if kind != "dil":
                    dve.wait_ge(sem("att_exp"), 2 * j + 2)
                    fj = fac[:, 2 * j:2 * j + 2]
                    if kind == "fox":
                        nc.vector.reciprocal(fj, lsum[:, 2 * j:2 * j + 2]).then_inc(sem("fac_ready"), 1)
                        return
                    own(nc.vector.reciprocal(fj, lsum[:, 2 * j:2 * j + 2]))
                    settled()
                    TTn(fj, fj, gates3[:, :, h, 1 if kind == "sel" else 2], ALU.mult)\
                        .then_inc(sem("fac_ready"), 1)
                elif j in (6, 9):
                    a = 2 * (j - 2)
                    nm = cols2(nmax[:, a:a + 6], 3)
                    dve.wait_ge(sem("scores_read"), j + 1)
                    own(TTn(dil[:, 6:8], nm[:, 0, :], nm[:, 1, :], ALU.min))
                    settled()
                    own(TTn(dil[:, 6:8], dil[:, 6:8], nm[:, 2, :], ALU.min))
                    settled()
                    n = (j - 6) // 3
                    TTn(cols2(dil[:, 0:6], 3), dil[:, 6:8].unsqueeze(1).broadcast_to([P, 3, 2]), nm,
                        ALU.subtract).then_inc(sem("dil_diff"), 1)
                    dve.wait_ge(sem("dil_exp"), n + 1)
                    dve.wait_ge(sem("att_exp"), 2 * j + 2)
                    own(TTn(dil[:, 8:14], dil[:, 0:6], lsum[:, a:a + 6], ALU.mult))
                    settled()
                    own(TTn(dil[:, 14:16], dil[:, 8:10], dil[:, 10:12], ALU.add))
                    settled()
                    own(TTn(dil[:, 14:16], dil[:, 14:16], dil[:, 12:14], ALU.add))
                    settled()
                    own(nc.vector.reciprocal(dil[:, 16:18], dil[:, 14:16]))
                    settled()
                    TTn(cols2(fac[:, a:a + 6], 3), cols2(dil[:, 0:6], 3),
                        dil[:, 16:18].unsqueeze(1).broadcast_to([P, 3, 2]), ALU.mult)\
                        .then_inc(sem("fac_ready"), 1)

            keep_up(FIRST["gates"] + 3)
            for j in range(NJ + PV_LAG):
                if j < NJ:
                    scores_in(j)
                if 1 <= j <= NJ and JOBS[j - 1][0] != "dil":
                    factor(j - 1)
                if j in (6, 9):
                    factor(j)
                halves(half_of("gates") + 8 + GATE_HALVES[j + 1] + SPLITS)
                for bank, tiles, last in COPIES:
                    if last == j - PV_LAG:
                        dve.wait_ge(sem("pv_done"), last + 1)
                        n = len(tiles)
                        nc.vector.tensor_copy(Y[:, tiles[0]:tiles[0] + n, :],
                                              cols2(PS[:, AV[bank], 0:n * S], n)).then_inc(sem("y_copied"), 1)
                for n in Y_SPLIT_AT.get(j, ()):
                    a, b = COPIES[n][1][0], COPIES[n][1][-1] + 1
                    dve.wait_ge(sem("y_hi"), n + 1)
                    TTn(hl[:, a:b, :], Y[:, a:b, :], hh[:, a:b, :].bitcast(F32), ALU.subtract)\
                        .then_inc(sem("y_split"), 1)

            for i in range(8):
                multiplied(half_of("w_p") + i)
                if i == KD - 1:
                    for k in range(4):
                        low(k, Y[:, 8 + k, :], "merged_hi", k, "merged_split")
                b = 2 + 2 * (i % 2)
                if i < 2:
                    for q in (10, 11):
                        dve.wait_ge(*read(FIRST["gates"] + q))
                a = branch(i)
                if i >= 2:
                    dve.wait_ge(sem("merged"), i - 1)
                STT(cols2(a[:, 0:2 * S]), BIG[:, i:16:8, :], 1.0, cols2(PS[:, b, :]), ALU.add, ALU.mult)
                STT(a[:, 2 * S:3 * S], BIG[:, 16 + i, :], 1.0, PS[:, b + 1, 0:S], ALU.add, ALU.mult)\
                    .then_inc(sem("branches"), 1)
            for k in range(4, KD):
                low(k, Y[:, 8 + k, :], "merged_hi", k, "merged_split")
            for i in range(4):
                u = FIRST["w_o"] + i
                if i < 3:
                    unit(u)
                else:
                    halves(half_at(u) + 1 + SPLITS)
                    dve.wait_ge(sem("half_used"), half_at(u) + 2)
                q = slice(i * 256, (i + 1) * 256)
                freed(STT(xb[:, :, q], cols2(bank_of(u)), 0.5, xa[:, :, q], ALU.mult, ALU.add), u)
            for i in range(2):
                dve.wait_ge(*read(FIRST["w_o"] + 2 + i))
            row_squares(1, xb)
            scales(1)
            halves(half_of("up") + SPLITS)
            turned_evac(1, "g2")
            for i in range(NF):
                u = FIRST["up"] + i
                keep_up(u)
                if i == NF - 1:
                    for k in range(DOWN_EARLY):
                        deep_low("down", BIG, DOWN, k)
                dve.wait_ge(sem("ffn_tap"), i + 1)
                a, cv = bank_of(u)[:, 0:S], T2[:, i % 2, 0:S]
                own(STT(cv[:, 1:S], a[:, 0:S - 1], v("conv_w", NF + i), cv[:, 1:S], ALU.mult, ALU.add))
                settled()
                STT(cv[:, 2:S], a[:, 0:S - 2], v("conv_w", i), cv[:, 2:S], ALU.mult, ALU.add)\
                    .then_inc(sem("ffn_conv"), 1)
                dve.wait_ge(sem("ffn_gelu"), i + 1)
                freed(TTn(BIG[:, i, :], T2[:, i % 2, S:2 * S], bank_of(u)[:, S:2 * S], ALU.mult), u)

            for k in range(DOWN_EARLY, 16):
                deep_low("down", BIG, DOWN, k)
                halves(half_of("down") + k + 1)
            dve.wait_ge(sem("positions_in"), 16)
            own(nc.vector.tensor_copy(ropes[4], ropes[5].bitcast(I32)))
            settled()
            own(TS(ropes[2], ropes[4], c("inv_freq"), None, ALU.mult))
            settled()
            own(TS(ropes[3], ropes[2], 1 / (2 * np.pi), 0.25, ALU.mult, ALU.add))
            own(TS(ropes[4], ropes[2], 1 / (2 * np.pi), MAGIC, ALU.mult, ALU.add))
            settled()
            own(TS(ropes[3], ropes[3], MAGIC, MAGIC, ALU.add, ALU.subtract))
            own(TS(ropes[4], ropes[4], MAGIC, None, ALU.subtract))
            settled()
            for part in range(3):
                for q in range(2):
                    src = ropes[2] if part == 0 else ropes[q]
                    own(STT(ropes[q], ropes[3 + q], -TURN[part], src, ALU.mult, ALU.add))
                settled()
            own(TS(ropes[0], ropes[0], float(np.pi / 2), PI_IN, ALU.add, ALU.min))
            own(TS(ropes[1], ropes[1], -PI_IN, PI_IN, ALU.max, ALU.min))
            settled()
            TS(ropes[0], ropes[0], -PI_IN, None, ALU.max).then_inc(sem("angles"), 1)

            for k in range(16, NF):
                deep_low("down", BIG, DOWN, k)
                halves(half_of("down") + k + 1)
            halves(half_of("down") + NF - 1 + SPLITS)
            dve.wait_ge(sem("half_used"), half_of("down") + NF)
            for t in range(TT):
                TTn(cols2(xa[:, t, :]), PS[:, DEEP + 2 * t:DEEP + 2 * t + 2, :], cols2(xb[:, t, :]), ALU.add)\
                    .then_inc(sem("x2_ready"), 1)
            dve.wait_ge(sem("gains_in"), 16)
            dve.wait_ge(sem("x2_ready"), TT)
            row_squares(2, xa)
            for t in range(TT):
                q = row_rstd(2, t)
                STT(xb[:, t, :], xa[:, t, :], q, gB[:, :], ALU.mult, ALU.mult).then_inc(sem("x3_ready"), 1)
            dve.wait_ge(sem("x3_ready"), TT)
            row_squares(3, xb)
            scales(3)
            halves(half_of("conv_in") + SPLITS)

            turned_evac(2, "g3")

            def conv_in(i):
                u = FIRST["conv_in"] + i
                keep_up(u)
                dve.wait_ge(sem("a_gate"), i + 1)
                freed(STT(up_in(i, 15, 15 + S), T1[:, i % 2, 0:S], 1.0, bank_of(u)[:, 0:S], ALU.add, ALU.mult), u)

            def taps(a, b):
                for m in range(a, b):
                    i, k = CONV_DVE[m // (2 * TAPS)][m % 2], m % (2 * TAPS) // 2
                    src, acc, wk = up_in(i, k, k + S), BIG[:, 16 + i, :], v("taps", i * TAPS + k)
                    if k == 0:
                        dve.wait_ge(*read(FIRST["conv_in"] + i))
                        ins = TS(acc, src, wk, None, ALU.mult)
                    else:
                        dve.wait_ge(sem("conv_tap"), m - 1)
                        ins = STT(acc, src, wk, acc, ALU.mult, ALU.add)
                    ins.then_inc(sem("conv_tap"), 1)

            dve.wait_ge(sem("conv_pads"), 4)
            for i in range(8):
                conv_in(i)
                if i >= 6:
                    taps(7 * (i - 6), 7 * (i - 5))
            at = 14
            for i in range(18):
                halves(half_of("qk") + i + 1 + SPLITS)
                if i == 0:
                    dve.wait_ge(sem("small_done"), 2)
                    own(TTn(gt2, cols2(PS[:, SC[0], 0:128])[:, :, 0:16],
                            r("b_gate").unsqueeze(1).broadcast_to([P, TT, 16]), ALU.add))
                    settled()
                    for d in range(2):
                        f = gt2[:, :, 4 + 8 * d:8 + 8 * d]
                        STT(lfx[:, :, 4 * d:4 * d + 4], f, -1.0, f, ALU.mult, ALU.max).then_inc(sem("lstm_logs"), 1)
                if i == 5:
                    dve.wait_ge(sem("lstm_exp"), 2)
                    for d in range(2):
                        f = gt2[:, :, 4 + 8 * d:8 + 8 * d]
                        STT(lf2[:, :, 4 * d:4 * d + 4], f, 0.0, lfx[:, :, 4 * d:4 * d + 4], ALU.min, ALU.subtract)\
                            .then_inc(sem("lstm_logs"), 1)
                n = 14 + (99 - 14) * (i + 1) // 18
                taps(at, n)
                at = n
            for s_, step_ in enumerate(EVEN_STEPS):
                if s_ < EVEN_HALVES:
                    halves(half_at(o_unit(0)) + s_ + 1 + SPLITS)
                for kind, n in step_:
                    if kind == "decay":
                        dve.wait_ge(sem("lstm_decay"), n + 1)
                        for i, (a, b) in enumerate(LSTM_COLS):
                            d, t = i // 2, i % 2
                            tab = c("causal", P if t == 0 else 0, S) if d == 0 else c("anti", 0, S if t == 0 else P)
                            nc.vector.tensor_tensor_reduce(
                                EB[:, n % 2, i, a:b], PS[:, SC[0], d * S + a:d * S + b], tab, -1.0, 0.0, ALU.add,
                                ALU.min, nM[:, 4 * n + i:4 * n + i + 1]).then_inc(sem("lstm_decay_read"), 1)
                        dve.wait_ge(sem("lstm_decay_read"), 4 * n + 4)
                        dve.wait_ge(sem("lstm_rows_copied"), 2)
                        q = slice(4 * n, 4 * n + 4)
                        TTn(floor[:, q], nF.rearrange("p (i h) -> p i h", h=4)[:, :, n], nM[:, q], ALU.add)\
                            .then_inc(sem("lstm_arg"), 1)
                    elif kind == "weigh":
                        q = slice(4 * n, 4 * n + 4)
                        dve.wait_ge(sem("lstm_scores"), n + 1)
                        for i, (a, b) in enumerate(LSTM_COLS):
                            dve.wait_ge(sem("lstm_dw"), 4 * n + i + 1)
                            t = i % 2
                            nc.vector.tensor_tensor_reduce(
                                EB[:, n % 2, i, a:b], PS[:, SC[1], t * S + a:t * S + b], EB[:, n % 2, i, a:b],
                                P ** -0.5, 0.0, ALU.mult, ALU.add, den[:, 4 * n + i:4 * n + i + 1])\
                                .then_inc(sem("lstm_scores_read"), 1)
                        dve.wait_ge(sem("lstm_scores_read"), 4 * n + 4)
                        own(STT(den2[:, q], den[:, q], -1.0, den[:, q], ALU.mult, ALU.max))
                        settled()
                        dve.wait_ge(sem("lstm_floor"), n + 1)
                        own(TTn(den2[:, q], den2[:, q], floor[:, q], ALU.max))
                        settled()
                        own(nc.vector.reciprocal(den2[:, q], den2[:, q]))
                        settled()
                        w_, eb = WM[:, n % 2, :], EB[:, n % 2]
                        k = 4 * n
                        own(TS(w_[:, 0:S], eb[:, 2, 0:S], den2[:, k + 2:k + 3], None, ALU.mult))
                        own(TS(w_[:, S:2 * S], eb[:, 1, 0:S], den2[:, k + 1:k + 2], None, ALU.mult))
                        settled()
                        STT(w_[:, 0:P], eb[:, 0, 0:P], den2[:, k:k + 1], w_[:, 0:P], ALU.mult, ALU.add)
                        STT(w_[:, S + P:2 * S], eb[:, 3, P:S], den2[:, k + 3:k + 4], w_[:, S + P:2 * S], ALU.mult,
                            ALU.add).then_inc(sem("lstm_w"), 1)
                    elif kind == "yb":
                        dve.wait_ge(sem("lstm_rs"), 2 * n + 2)
                        dve.wait_ge(sem("oz_ready"), n + 1)
                        for e in range(2):
                            own(STT(Y[:, 8 + 2 * n + e, :], PS[:, AV[0], e * S:(e + 1) * S], v("hn_g", 2 * n + e),
                                    BIG[:, 8 + 2 * n + e, :], ALU.mult, ALU.mult))
                        settled()
                        y = Y[:, 8 + 2 * n:10 + 2 * n, :]
                        STT(y, y, 0.25, RSH.unsqueeze(1).broadcast_to([P, 2, S]), ALU.mult, ALU.mult)\
                            .then_inc(sem("yb_done"), 1)
                    elif kind == "gn_u":
                        c0 = 2 * GN_PAIRS[n]
                        if GN_PAIRS[n] in PAIR_ADDED:
                            dve.wait_ge(sem("prod_added"), PAIR_ADDED[GN_PAIRS[n]])
                        else:
                            dve.wait_ge(sem("conv_tap"), 2 * TAPS * (n + 1))
                        for e in range(2):
                            ins = TS(GNU[:, n % 2, e * S:(e + 1) * S], BIG[:, 16 + c0 + e, :], 0.5,
                                     v("tap_b", c0 + e), ALU.mult, ALU.add)
                        ins.then_inc(sem("gn_u"), 1)
                    elif kind == "gn":
                        dve.wait_ge(sem("gn_u"), n + 1)
                        dve.wait_ge(sem("gn_mean"), n + 1)
                        TTn(XC, GNU[:, n % 2, :], PS[:, PT[1], :], ALU.subtract).then_inc(sem("gn_xc"), 1)
                    elif kind == "gn_x":
                        dve.wait_ge(sem("gn_rs"), 2 * n + 2)
                        own(TTn(XC, XC, RSG, ALU.mult))
                        settled()
                        c0 = 2 * GN_PAIRS[n]
                        for e in range(2):
                            q = XC[:, e * S:(e + 1) * S]
                            ins = TS(q, q, v("gn_g", c0 + e), v("gn_b", c0 + e), ALU.mult, ALU.add)
                        ins.then_inc(sem("gn_xg"), 1)
                    elif kind == "gn_y":
                        c0 = 2 * GN_PAIRS[n]
                        dve.wait_ge(sem("gn_tanh"), n + 1)
                        own(STT(T2[:, 1, :], T2[:, 1, :], 1.0, XC, ALU.add, ALU.mult))
                        settled()
                        STT(Y[:, c0:c0 + 2, :], cols2(T2[:, 1, :]), 0.5, BIG[:, c0:c0 + 2, :], ALU.mult,
                            ALU.mult).then_inc(sem("gn_done"), 1)
                    elif kind == "deep":
                        halves(half_of("even_out") + (n + 1) * EVEN_EARLY + SPLITS)
                    elif kind == "split":
                        for k in range(4 * n, 4 * n + 4):
                            deep_low("even_out", Y, EVEN_OUT, k)
                if s_ < EVEN_HALVES and s_ % 6 == 3:
                    n = s_ // 6
                    u = z_unit(n)
                    dve.wait_ge(sem("zb_tanh"), n + 1)
                    freed(STT(T1[:, 1, :], T1[:, 1, :], 1.0, bank_of(u), ALU.add, ALU.mult), u)
                    dve.wait_ge(*read(u))
                    oz = BIG[:, 8 + 2 * n:10 + 2 * n, :]
                    dve.wait_ge(*read(o_unit(n)))
                    STT(oz, oz, 1.0, cols2(T1[:, 1, :]), ALU.add, ALU.mult).then_inc(sem("oz_ready"), 1)
                if at < 4 * TAPS:
                    n = min(at + 5, 4 * TAPS)
                    taps(at, n)
                    at = n

            def post_norm(m, bank, base, dst, name):
                dve.wait_ge(sem("gains_in"), 32 if m == 4 else 48)
                for t in range(TT):
                    q = row_rstd(m, t)
                    own(STT(cols2(xh[:, t, :]), PS[:, bank + 2 * t:bank + 2 * t + 2, :], q, cols2(gB[:, :]),
                            ALU.mult, ALU.mult))
                    settled()
                    TTn(dst[:, t, :], xh[:, t, :], base[:, t, :], ALU.add).then_inc(sem(name), 1)

            for k in range(8, 16):
                deep_low("even_out", Y, EVEN_OUT, k)
                halves(half_of("even_out") + k + 1)
            post_norm(4, 0, xb, xa, "x4_ready")
            dve.wait_ge(sem("x4_ready"), TT)
            row_squares(5, xa)
            scales(5)
            halves(half_of("lora") + SPLITS)

            turned_evac(3, "g4")
            for i in range(5):
                keep_up(FIRST["lora"] + i)
            dve.wait_ge(sem("lora_rs"), 2)
            for k in range(5):
                STT(LQ[:, k, :], LQ[:, k, :], v("g_q", k) if k < 3 else v("g_kv", k - 3),
                    RSL[:, 0:S] if k < 3 else RSL[:, S:2 * S], ALU.mult, ALU.mult).then_inc(sem("lora_scaled"), 1)
            for i in range(6):
                u = FIRST["z_c"] + i
                keep_up(u)
                dve.wait_ge(sem("zcd_tanh"), i + 1)
                o = ZC[:, 2 * i:2 * i + 2, :] if i < 4 else ZD[:, 2 * i - 8:2 * i - 6, :]
                freed(STT(o, cols2(T1[:, i % 2, :]), 1.0, cols2(bank_of(u)), ALU.add, ALU.mult), u)
            for k in range(5):
                low(k, LQ[:, k, :], "lora_hi", k, "lora_ready")
            for m in range(2):
                dve.wait_ge(sem("fft2"), m + 1)
                nc.vector.tensor_copy(Y[:, 8 + 2 * m:10 + 2 * m, :], cols2(PS[:, PT[m], :]))\
                    .then_inc(sem("fft2_copied"), 1)

            def rotate(n, src):
                tiles = 2 if n < 2 else 1
                dve.wait_ge(sem("rope_tables"), 2)
                if n < 2:
                    dve.wait_ge(sem(f"uq_read[{n}]"), 3)
                dve.wait_ge(sem("rope_swapped"), n + 1)
                a, b = T2[:, 0, 0:tiles * S], T2[:, 1, 0:tiles * S]
                if n:
                    dve.wait_ge(sem("rope_ready"), n)
                own(TTn(cols2(a, tiles), src, ropes[0].unsqueeze(1).broadcast_to([P, tiles, S]), ALU.mult))
                TTn(cols2(b, tiles), cols2(PS[:, SC[1], 0:tiles * S], tiles),
                    ropes[1].unsqueeze(1).broadcast_to([P, tiles, S]), ALU.mult)\
                    .then_inc(sem("rope_swapped_read"), 1)
                settled()
                dve.wait_ge(sem("rope_swapped_read"), n + 1)
                TTn(src, cols2(a, tiles), cols2(b, tiles), ALU.add).then_inc(sem("rope_ready"), 1)

            for n in range(1, 14, 2):
                multiplied(UQ_HALF[n])
                nc.vector.tensor_copy(uq_dest(n), cols2(PS[:, PT[1], :]) if n < 10 else PS[:, PT[1], :])\
                    .then_inc(sem("uq_read[1]"), 1)
                if n == 5:
                    rotate(0, QR[:, 0:2, :])
                if n == 7:
                    for k in range(4):
                        low((5 + k) % 8, Y[:, 8 + k, :], "fft2_hi", k, "fft2_split")
                if n == 9:
                    rotate(1, QR[:, 2:4, :])
                if n == 11:
                    rotate(2, KR[:, :, :])
            multiplied(half_of("w_fd") + 1)
            for m in range(2):
                dve.wait_ge(*read(FIRST["z_d"] + m))
                STT(Y[:, 8 + 2 * m:10 + 2 * m, :], cols2(PS[:, AV[m], :]), 0.5, ZD[:, 2 * m:2 * m + 2, :],
                    ALU.mult, ALU.mult).then_inc(sem("yd_done"), 1)
            halves(half_of("odd_out") + SPLITS)

            for i in range(8 + 3):
                if i < 8:
                    dve.wait_ge(sem("mla_scores"), i + 1)
                    q = mmax[:, 2 * i:2 * i + 2]
                    own(nc.vector.tensor_reduce(q, cols2(PS[:, SC[i % 2], :]), AX.X, ALU.max))
                    settled()
                    TS(q, q, -MLA_SCALE, None, ALU.mult).then_inc(sem("mla_max"), 1)
                if 1 <= i < 9:
                    h = i - 1
                    dve.wait_ge(sem("mla_probs"), 2 * h + 2)
                    q = msum[:, 2 * h:2 * h + 2]
                    nc.vector.reciprocal(q, q).then_inc(sem("mla_rec"), 1)
                if i >= 3:
                    h = i - 3
                    dve.wait_ge(sem("mla_out"), h + 1)
                    if h % 2 == 0:
                        dve.wait_ge(*read(FIRST["z_c"] + h // 2))
                    STT(Y[:, h, :], PS[:, AV[h % 2], 0:S], 0.5, ZC[:, h, :], ALU.mult, ALU.mult)\
                        .then_inc(sem("yc_done"), 1)
                if i < 8:
                    deep_low("odd_out", Y, ODD_OUT, i)
            for k in range(8, 12):
                deep_low("odd_out", Y, ODD_OUT, k)
                halves(half_of("odd_out") + k + 1)
            post_norm(6, DEEP, xa, xb, "out_ready")

        @block.gpsimd
        def _(pool):
            nc.gpsimd.memset(CM, 0.0).then_inc(sem("cm_zero"), 1)
            for j in range(NJ):
                pool.wait_ge(sem("fac_ready"), FAC[j])
                for t in range(TT):
                    q = PB[:, j % 8, 0:P] if t == 0 else PB[:, j % 8, P:3 * P]
                    ins = nc.gpsimd.tensor_scalar(q, q, fac[:, 2 * j + t:2 * j + t + 1], None, ALU.mult)
                ins.then_inc(sem("probs_scaled"), 1)
            for i in range(KD):
                a = branch(i)
                pool.wait_ge(sem("branches"), i + 1)
                nc.gpsimd.tensor_tensor(a[:, 0:S], a[:, 0:S], a[:, S:2 * S], ALU.add)\
                    .then_inc(sem("branch_sum"), 1)
                pool.wait_ge(sem("branch_sum"), i + 1)
                nc.gpsimd.tensor_tensor(Y[:, 8 + i, :], a[:, 0:S], a[:, 2 * S:3 * S], ALU.add)\
                    .then_inc(sem("merged"), 1)
            for buf, name, value in ((UP_DVE, "merged_split", KD), (UP_POOL, "x3_ready", TT)):
                pool.wait_ge(sem(name), value)
                nc.gpsimd.memset(buf[:, :, 0:15], 0.0).then_inc(sem("conv_pads"), 1)
                nc.gpsimd.memset(buf[:, :, 15 + S:CONV_W], 0.0).then_inc(sem("conv_pads"), 1)
            pool.wait_ge(sem("conv_pads"), 4)
            for m, (i, k) in enumerate(PRODUCTS):
                if k:
                    acc, e = BIG[:, 16 + i, :], ADDED[m]
                    pool.wait_ge(sem("prod_ready"), m + 1)
                    if k > 1:
                        pool.wait_ge(sem("prod_added"), e - 1 if i > 1 else e)
                    nc.gpsimd.tensor_tensor(acc, acc, PROD[:, e % PROD_RING, :], ALU.add)\
                        .then_inc(sem("prod_added"), 1)
            e = ADDED[-1]
            pool.wait_ge(*read(FIRST["conv_in"]))
            pool.wait_ge(sem("prod_added"), e)
            for k in range(TAPS + 1):
                acc = BIG[:, 16, :]
                if k < TAPS:
                    if k > PROD_RING:
                        pool.wait_ge(sem("prod_added"), e + k - PROD_RING)
                    nc.gpsimd.tensor_scalar(PROD[:, k % PROD_RING, :] if k else acc, up_in(0, k, k + S),
                                            v("taps", k), None, ALU.mult).then_inc(sem("pool_prod"), 1)
                if k >= 2:
                    pool.wait_ge(sem("pool_prod"), k)
                    if k > 2:
                        pool.wait_ge(sem("prod_added"), e + k - 2)
                    nc.gpsimd.tensor_tensor(acc, acc, PROD[:, (k - 1) % PROD_RING, :], ALU.add)\
                        .then_inc(sem("prod_added"), 1)
            for h in range(8):
                pool.wait_ge(sem("mla_rec"), h + 1)
                for t in range(TT):
                    q = MP[:, h % 4, t * S:(t + 1) * S]
                    ins = nc.gpsimd.tensor_scalar(q, q, msum[:, 2 * h + t:2 * h + t + 1], None, ALU.mult)
                ins.then_inc(sem("mla_scaled"), 1)


def slope(i):
    return np.exp2(-8.0 * i / 12)


def constant_tables():
    p = np.arange(P)[:, None]
    s = np.arange(S)[None, :]
    masked = np.float64(MASKED)
    out = np.zeros((P, NC_), np.float32)
    late = np.zeros((P, NL_), np.float32)

    def put(name, a):
        o, n = C_AT[name]
        out[:, o:o + n] = np.asarray(a, np.float64).reshape(P, n)

    put("ident", np.eye(P))
    put("mean", np.concatenate([np.full((P, P), 1.0 / n) for n in (128, 256, 384)], 1))
    put("neg_upper", np.concatenate([-1.0 * (p + t * P <= s) for t in range(TT)], 1))
    put("neg_lower", np.concatenate([-1.0 * (p + t * P >= s) for t in range(TT)], 1))
    dist = p + P - s
    causal = np.where(dist >= 0, 0.0, masked)
    put("causal", causal)
    put("anti", np.where(s >= p, 0.0, masked))
    dil = []
    for g, (w, rate) in enumerate(((128, 1), (512, 4), (2048, 16))):
        for h in range(2):
            ok = (dist >= 0) & (dist <= w) & (dist % rate == 0)
            dil.append(np.where(ok, -8.0 * slope(2 * (2 * g + h) + 1) * dist, masked))
    put("dil_bias", np.concatenate(dil, 1))
    put("nsa_bias", np.concatenate([np.where(dist >= 0, -8.0 * slope(2 * h + 2) * dist, masked)
                                    for h in range(6)], 1))
    bias, mask = np.zeros((P, 2, TT, 3, 32)), np.zeros((P, 2, TT, 3, 32))
    end = np.arange(15) * 16 + 31
    for g in range(2):
        for t in range(TT):
            for h in range(3):
                far = p + t * P - end[None, :]
                bias[:, g, t, h, :15] = np.where(far >= 0, -slope(2 * (3 * g + h) + 2) * far, masked)
                mask[:, g, t, h, :15] = far >= 0
    put("cmp_bias", bias)
    put("cmp_mask", mask)
    rows = np.zeros((P, 4, P))
    for h in range(4):
        rows[h, h], rows[64 + h, h] = 1.0, 1.0
    put("rows", rows)
    inv = (10000.0 ** (-np.arange(0, 64, 2, dtype=np.float32) / np.float32(64))).astype(np.float32)
    put("inv_freq", np.tile(inv, 4)[:, None])

    def put_late(name, a):
        o, n = L_AT[name]
        late[:, o:o + n] = np.asarray(a, np.float64).reshape(P, n)

    ch = 2 * np.pi * ((np.arange(P)[:, None] * np.arange(P)[None, :]) % P) / P
    put_late("dft_ch", np.concatenate([np.cos(ch), np.sin(ch)], 1) / np.sqrt(P))
    tk = 2 * np.pi * ((np.arange(S)[:, None] * np.arange(S)[None, :]) % S) / S
    put_late("dft_cos", np.concatenate([np.cos(tk)[t * P:(t + 1) * P] for t in range(TT)], 1) / np.sqrt(S))
    put_late("dft_nsin", np.concatenate([-np.sin(tk)[t * P:(t + 1) * P] for t in range(TT)], 1) / np.sqrt(S))
    swap = np.zeros((P, P))
    for m in range(P):
        if m % 64 < 32:
            swap[m + 32, m] = -1.0
        else:
            swap[m - 32, m] = 1.0
    put_late("rope_swap", swap)
    return out, late


def wide(w, k):
    n = w.shape[1] // 256
    return w.reshape(k, P, n, 256).transpose(2, 1, 0, 3).reshape(n, P, k * 256)


def deep_units(w):
    n = w.shape[0] // 256
    return w.reshape(n, 2, P, D).transpose(0, 2, 1, 3).reshape(n, P, 2 * D)


def halves_of(w, k, tiles):
    n = w.shape[1] // (tiles * P)
    a = w.reshape(k, P, n, tiles, P).transpose(2, 1, 3, 0, 4).reshape(n, P, tiles * k * P)
    out = np.zeros((n, P, HALF), np.float32)
    out[:, :, :a.shape[2]] = a
    return out.reshape(n // 2, 2, P, HALF).transpose(0, 2, 1, 3).reshape(n // 2, P, UNIT)


def columns(v, n):
    return v.reshape(n, P).T


def kernel(**inputs):
    import concourse.bacc as bacc
    from concourse.bass_utils import run_bass_kernel_spmd

    a = {k: np.asarray(q) for k, q in inputs.items()}
    w_in, b_in = a["w_in"][0], a["b_in"][0]
    at = np.cumsum([0, 256, 256, 256, 4, 384, 384, 384, 384, 128, 128, 128, 128, 128, 128, 18, 3072])
    (qa, ka, va, fa, qb, kb, vb, qc, kc, vcm, ks, vs, kw, vw, gc, gates) = (
        np.arange(i, j) for i, j in zip(at[:-1], at[1:]))
    qc = np.concatenate([qc[h * DH:(h + 1) * DH] for i in range(3) for h in (i, i + 3)])
    cols = [qa, ka]
    for g in range(3):
        cols += [qb[g * P:(g + 1) * P], kb[g * P:(g + 1) * P]]
    cols += [qc, ks, kw, kc]
    feat = np.concatenate(cols)
    vcols = np.concatenate([va, vb, vs, vw])
    order = np.concatenate([feat, vcols[768:], vcm, vcols[:768]])
    w_pc = np.concatenate([a["w_pc"][0][h * DH:(h + 1) * DH] for i in range(3) for h in (i, i + 3)])
    up = a["w_up"][0].reshape(D, 2, NF, P).transpose(0, 2, 1, 3).reshape(D, 2 * DFF)
    ew = a["even_w_in_2"][0]
    e_at = np.cumsum([0, 1024, 1024, 1024, 512, 512, 1024, 1024, 1024, 16])
    a_val, a_gate, z_a, eq, ek, ev, eo, z_b, eg = (ew[:, i:j] for i, j in zip(e_at[:-1], e_at[1:]))

    def pair(x_, y_, n):
        return np.stack([x_.reshape(D, n, P), y_.reshape(D, n, P)], 2).reshape(D, 2 * n * P)

    ow = a["odd_w_in_2"][0]
    o_at = np.cumsum([0, 384, 256, 64, 512, 1024, 512])
    cq, ckv, kr, f_in, z_c, z_d = (ow[:, i:j] for i, j in zip(o_at[:-1], o_at[1:]))
    uq = a["odd_w_uq_2"][0].reshape(384, 8, 192)
    uq = np.concatenate([uq[:, :, :128].reshape(384, 1024), uq[:, :, 128:].reshape(384, 512)], 1)
    ukv = a["odd_w_ukv_2"][0].reshape(256, 8, 256)
    odd_out = a["odd_w_out_2"][0]
    units = {
        "proj": wide(w_in[:, order], KD), "gates": wide(w_in[:, gates], KD),
        "cmp": np.concatenate([a[n][0].reshape(2, 8, P, 256).transpose(0, 2, 1, 3).reshape(2, P, UNIT)
                               for n in ("cmp_k_w1", "cmp_v_w1")]),
        "w_p": halves_of(np.concatenate([a["w_pa"][0], a["w_pb"][0], w_pc]), KD, 1),
        "w_o": wide(a["w_o"][0], KD), "up": wide(up, KD), "down": deep_units(a["w_down"][0]),
        "conv_in": wide(pair(a_val, a_gate, 8), KD), "z_a": wide(z_a, KD), "qk": wide(pair(eq, ek, 4), KD),
        "v_o_z": np.stack([wide(q, KD) for q in (ev, eo, z_b)], 1).reshape(12, P, UNIT),
        "even_out": deep_units(a["even_w_out_2"][0].reshape(16, P, D)[EVEN_OUT].reshape(2 * D, D)),
        "lora": wide(np.concatenate([cq, ckv, kr, kr], 1), KD), "f_in": wide(f_in, KD),
        "w_uq": halves_of(uq, 3, 2), "w_uk": halves_of(ukv[:, :, :128].reshape(256, 1024), 2, 4),
        "w_uv": ukv[:, :, 128:].reshape(2, P, 2, 512).transpose(1, 2, 0, 3).reshape(1, P, UNIT),
        "z_c": wide(z_c, KD), "z_d": wide(z_d, KD),
        "w_fd": a["odd_w_fd_2"][0].reshape(1, 4, P, 512).transpose(0, 2, 1, 3).reshape(1, P, UNIT),
        "odd_out": deep_units(np.concatenate([odd_out[8 * P:], odd_out[:8 * P]])),
    }
    w = np.concatenate([units[name] for name, n in STREAM])
    small = np.concatenate([w_in[:, fa], w_in[:, gc], eg], 1)
    w_small = small.reshape(KD, P, 38).transpose(1, 0, 2)
    cmp_w2 = np.stack([a[n][0].reshape(2, P, DH).transpose(1, 0, 2) for n in ("cmp_k_w2", "cmp_v_w2")], 1)

    vecs = np.zeros((P, NV_), np.float32)

    def put(name, x_):
        o, n = V_AT[name]
        vecs[:, o:o + x_.shape[1]] = x_

    put("g1", columns(a["norm1_g"][0], 8))
    put("b_feat", columns(np.concatenate([b_in[feat], b_in[vcm]]), 17))
    put("b_gates", columns(b_in[gates], 24))
    put("pe", a["cmp_pe"][0].reshape(16, P).T)
    put("g2", columns(a["norm2_g"][0], 8))
    put("conv_w", columns(a["conv_w"][0].reshape(-1), 66))
    put("conv_b", columns(a["conv_b"][0], 22))
    put("g3", columns(a["even_g_pre_2"][0], 8))
    put("taps", a["even_conv_w_2"][0].reshape(31, 8, P).transpose(2, 1, 0).reshape(P, 248))
    put("tap_b", columns(a["even_conv_b_2"][0], 8))
    put("gn_g", columns(a["even_gn_g_2"][0], 8))
    put("gn_b", columns(a["even_gn_b_2"][0], 8))
    put("hn_g", columns(a["even_hn_g_2"][0], 8))
    put("g4", columns(a["odd_g_pre_2"][0], 8))
    put("g_q", columns(a["odd_g_q_2"][0], 3))
    put("g_kv", columns(a["odd_g_kv_2"][0], 2))
    rows = np.concatenate([b_in[vcols], b_in[fa], b_in[gc], a["even_b_gate_2"][0]])[None, :]
    gains = np.stack([a["final_g"], a["even_g_post_2"][0], a["odd_g_post_2"][0]])
    consts, late = constant_tables()
    arrays = {"w": w, "w_small": w_small, "consts": consts, "late": late, "vecs": vecs, "rows": rows,
              "gains": gains, "x": a["x"][0].reshape(TT, P, D).transpose(1, 0, 2),
              "positions": a["positions_2"].astype(np.int32), "cmp_w2": cmp_w2}
    arrays = {k: np.ascontiguousarray(q) for k, q in arrays.items()}
    nc = bacc.Bacc("TRN2", target_bir_lowering=False, num_devices=1)
    args = {k: nc.dram_tensor(k, q.shape, mybir.dt.from_np(q.dtype), kind="ExternalInput").ap()
            for k, q in arrays.items()}
    out = nc.dram_tensor("out", (S, D), F32, kind="ExternalOutput").ap()
    program(nc, out=out, **args)
    r = run_bass_kernel_spmd(nc, [arrays], core_ids=[0])
    return r.results[0]["out"].reshape(1, S, D)
```
